# Optimizing a Trainium2 kernel written in Bass

```python
import math
import jax, jax.numpy as jnp
from jax import lax
import numpy as np

D_MODEL = 1024
BATCH = 1
SEQ = 256
DEPTH = 1

CONV_DIM = 512
CONV_WIDTH = 3
ATTN_HEADS = 8
ATTN_HEAD_DIM = 64
ATTN_DIM = ATTN_HEADS * ATTN_HEAD_DIM
MOBA_BLOCK = 256
MOBA_TOPK = 3
Q_CHUNK = 128
REL_BUCKETS = 32
REL_MAX_DISTANCE = 128
GLA_HEADS = 4
GLA_KEY_DIM = 64
GLA_VALUE_DIM = 128
GLA_QK_DIM = GLA_HEADS * GLA_KEY_DIM
GLA_V_DIM = GLA_HEADS * GLA_VALUE_DIM
GLA_GATE_RANK = 16
GLA_GATE_TEMP = 16.0
GLA_CHUNK = 64
N_BRANCHES = 3
BRANCH_DIM = 512
IN_SPLITS = (CONV_DIM, CONV_DIM, CONV_DIM, ATTN_DIM, ATTN_DIM, ATTN_DIM,
             GLA_QK_DIM, GLA_QK_DIM, GLA_V_DIM, GLA_V_DIM, GLA_GATE_RANK)
D_IN = 3 * CONV_DIM + 3 * ATTN_DIM + 2 * GLA_QK_DIM + 2 * GLA_V_DIM + GLA_GATE_RANK
N_GROUPS = 4
EXPERTS_PER_GROUP = 8
N_EXPERTS = N_GROUPS * EXPERTS_PER_GROUP
TOP_K = 2
EXPERT_FF = 512
EXPERT_BLOCK = 256
RMS_EPS = 1e-6

kernel_name = 'hybrid_conv_moba_gla_hmoe'

def rms_norm(x, g):
    xf = x.astype(jnp.float32)
    y = xf * lax.rsqrt(jnp.mean(xf * xf, axis=-1, keepdims=True) + RMS_EPS)
    return (y * g.astype(jnp.float32)).astype(x.dtype)

def short_conv(b_gate, c_gate, x_in, conv_w, conv_b):
    u = c_gate * x_in
    sn = u.shape[1]
    up = jnp.pad(u, ((0, 0), (CONV_WIDTH - 1, 0), (0, 0)))
    y = conv_b
    for j in range(CONV_WIDTH):
        y = y + conv_w[j] * up[:, j:j + sn]
    return b_gate * y

def t5_bucket(rel):
    n = jnp.maximum(rel, 0)
    max_exact = REL_BUCKETS // 2
    scaled = jnp.log(jnp.maximum(n, max_exact).astype(jnp.float32) / max_exact) / math.log(REL_MAX_DISTANCE / max_exact)
    large = jnp.minimum(max_exact + (scaled * (REL_BUCKETS - max_exact)).astype(jnp.int32), REL_BUCKETS - 1)
    return jnp.where(n < max_exact, n, large)

def moba_attention(q, k, v, rel_bias_table):
    bn, sn, nh, dh = q.shape
    f32 = jnp.float32
    n_blocks = max(-(-sn // MOBA_BLOCK), MOBA_TOPK)
    pad = n_blocks * MOBA_BLOCK - sn
    n_chunks = sn // Q_CHUNK
    scale = dh ** -0.5
    qh = q.transpose(0, 2, 1, 3)

    def to_blocks(t):
        t = jnp.pad(t.transpose(0, 2, 1, 3), ((0, 0), (0, 0), (0, pad), (0, 0)))
        return t.reshape(bn, nh, n_blocks, MOBA_BLOCK, dh)

    kblk, vblk = to_blocks(k), to_blocks(v)
    kmean = kblk.mean(axis=3)
    q_block = jnp.arange(sn) // MOBA_BLOCK
    past = jnp.arange(n_blocks)[None, :] < q_block[:, None]
    gate = jnp.einsum('bhsd,bhnd->bhsn', qh, kmean).astype(f32)
    gate = jnp.where(past, gate, -jnp.inf)
    _, sel = lax.top_k(gate, MOBA_TOPK)

    q_items = qh.reshape(bn, nh, n_chunks, Q_CHUNK, dh).transpose(0, 2, 1, 3, 4).reshape(bn * n_chunks, nh, Q_CHUNK, dh)
    sel_items = sel.reshape(bn, nh, n_chunks, Q_CHUNK, MOBA_TOPK).transpose(0, 2, 1, 3, 4).reshape(bn * n_chunks, nh, Q_CHUNK, MOBA_TOPK)
    table = rel_bias_table.astype(f32).T
    head3 = jnp.arange(nh)[:, None, None]
    head4 = jnp.arange(nh)[:, None, None, None]
    n_sel = MOBA_TOPK * MOBA_BLOCK

    def attend(args):
        qc, selc, item = args
        b = item // n_chunks
        c = item % n_chunks
        kb, vb = kblk[b], vblk[b]
        q_pos = c * Q_CHUNK + jnp.arange(Q_CHUNK)
        own = (c * Q_CHUNK) // MOBA_BLOCK
        k_sel = kb[head3, selc]
        v_sel = vb[head3, selc]
        kpos_sel = selc[..., None] * MOBA_BLOCK + jnp.arange(MOBA_BLOCK)
        s_sel = (jnp.einsum('hqd,hqktd->hqkt', qc, k_sel).astype(f32) * scale
                 + table[head4, t5_bucket(q_pos[None, :, None, None] - kpos_sel)])
        valid = jnp.arange(MOBA_TOPK) < own
        s_sel = jnp.where(valid[None, None, :, None], s_sel, -jnp.inf)
        k_own = lax.dynamic_index_in_dim(kb, own, axis=1, keepdims=False)
        v_own = lax.dynamic_index_in_dim(vb, own, axis=1, keepdims=False)
        rel_own = q_pos[:, None] - (own * MOBA_BLOCK + jnp.arange(MOBA_BLOCK))[None, :]
        s_own = jnp.einsum('hqd,htd->hqt', qc, k_own).astype(f32) * scale + table[:, t5_bucket(rel_own)]
        s_own = jnp.where(rel_own >= 0, s_own, -jnp.inf)
        logits = jnp.concatenate([s_sel.reshape(nh, Q_CHUNK, n_sel), s_own], axis=-1)
        p = jax.nn.softmax(logits, axis=-1).astype(qc.dtype)
        p_sel = p[..., :n_sel].reshape(nh, Q_CHUNK, MOBA_TOPK, MOBA_BLOCK)
        p_own = p[..., n_sel:]
        return (jnp.einsum('hqkt,hqktd->hqd', p_sel, v_sel)
                + jnp.einsum('hqt,htd->hqd', p_own, v_own))

    out = lax.map(attend, (q_items, sel_items, jnp.arange(bn * n_chunks)))
    return out.reshape(bn, n_chunks, nh, Q_CHUNK, dh).transpose(0, 1, 3, 2, 4).reshape(bn, sn, nh * dh)

def gla(q, k, v, r, z, w_alpha, b_alpha, out_norm):
    bn, sn, _ = q.shape
    f32 = jnp.float32
    nc = sn // GLA_CHUNK
    qf = q.astype(f32).reshape(bn, sn, GLA_HEADS, GLA_KEY_DIM) * GLA_KEY_DIM ** -0.5
    kf = k.astype(f32).reshape(bn, sn, GLA_HEADS, GLA_KEY_DIM)
    vf = v.astype(f32).reshape(bn, sn, GLA_HEADS, GLA_VALUE_DIM)
    log_a = jax.nn.log_sigmoid((z @ w_alpha + b_alpha).astype(f32)) / GLA_GATE_TEMP
    log_a = log_a.reshape(bn, sn, GLA_HEADS, GLA_KEY_DIM)

    def chunked(t):
        return t.reshape(bn, nc, GLA_CHUNK, GLA_HEADS, -1).transpose(0, 3, 1, 2, 4)

    qc, kc, vc, ac = chunked(qf), chunked(kf), chunked(vf), chunked(log_a)
    bcum = jnp.cumsum(ac, axis=3)
    btot = bcum[:, :, :, -1:, :]
    qe = qc * jnp.exp(bcum)
    ke = kc * jnp.exp(-bcum)
    kd = kc * jnp.exp(btot - bcum)
    causal = jnp.tril(jnp.ones((GLA_CHUNK, GLA_CHUNK), dtype=bool))
    att = jnp.where(causal, jnp.einsum('bhnid,bhnjd->bhnij', qe, ke), 0.0)
    o = jnp.einsum('bhnij,bhnjv->bhniv', att, vc)
    kv = jnp.einsum('bhnjd,bhnjv->bhndv', kd, vc)
    decay = jnp.exp(btot[:, :, :, 0, :])

    def step(state, inp):
        kv_n, dec_n = inp
        return dec_n[..., None] * state + kv_n, state

    s0 = jnp.zeros((bn, GLA_HEADS, GLA_KEY_DIM, GLA_VALUE_DIM), f32)
    _, s_prev = lax.scan(step, s0, (kv.transpose(2, 0, 1, 3, 4), decay.transpose(2, 0, 1, 3)))
    s_prev = s_prev.transpose(1, 2, 0, 3, 4)
    o = o + jnp.einsum('bhnid,bhndv->bhniv', qe, s_prev)
    o = o.transpose(0, 2, 3, 1, 4).reshape(bn, sn, GLA_HEADS, GLA_VALUE_DIM)
    o = rms_norm(o, out_norm).reshape(bn, sn, GLA_V_DIM)
    return (o * jax.nn.silu(r.astype(f32))).astype(r.dtype)

def hier_moe(h, w_rg, b_rg, w_re, b_re, w_g, w_u, w_d):
    bn, sn, d = h.shape
    f32 = jnp.float32
    t = bn * sn
    xt = h.reshape(t, d)
    p_group = jax.nn.softmax((xt @ w_rg + b_rg).astype(f32), axis=-1)
    group = jnp.argmax(p_group, axis=-1)
    p_group_top = jnp.take_along_axis(p_group, group[:, None], axis=-1)
    le = (xt @ w_re + b_re).astype(f32).reshape(t, N_GROUPS, EXPERTS_PER_GROUP)
    le_sel = jnp.take_along_axis(le, group[:, None, None], axis=1)[:, 0]
    top_p, top_i = lax.top_k(jax.nn.softmax(le_sel, axis=-1), TOP_K)
    weights = p_group_top * top_p / jnp.sum(top_p, axis=-1, keepdims=True)
    expert_id = group[:, None] * EXPERTS_PER_GROUP + top_i

    n_assign = t * TOP_K
    e_flat = expert_id.reshape(-1).astype(jnp.int32)
    w_flat = weights.reshape(-1).astype(h.dtype)
    tok_flat = jnp.repeat(jnp.arange(t, dtype=jnp.int32), TOP_K)
    counts = jnp.zeros((N_EXPERTS,), jnp.int32).at[e_flat].add(1)
    padded = ((counts + EXPERT_BLOCK - 1) // EXPERT_BLOCK) * EXPERT_BLOCK
    pad_end = jnp.cumsum(padded)
    pad_start = pad_end - padded
    start = jnp.cumsum(counts) - counts
    order = jnp.argsort(e_flat)
    e_sorted = e_flat[order]
    dest = pad_start[e_sorted] + (jnp.arange(n_assign, dtype=jnp.int32) - start[e_sorted])
    n_blocks = -(-n_assign // EXPERT_BLOCK) + N_EXPERTS
    n_rows = n_blocks * EXPERT_BLOCK
    row_tok = jnp.full((n_rows,), t, jnp.int32).at[dest].set(tok_flat[order])
    row_w = jnp.zeros((n_rows,), h.dtype).at[dest].set(w_flat[order])
    block_expert = jnp.minimum(
        jnp.searchsorted(pad_end, jnp.arange(n_blocks, dtype=jnp.int32) * EXPERT_BLOCK, side='right'),
        N_EXPERTS - 1)
    x_pad = jnp.concatenate([xt, jnp.zeros((1, d), xt.dtype)], axis=0)
    xs = x_pad[row_tok].reshape(n_blocks, EXPERT_BLOCK, d)

    def expert_block(args):
        xb, e = args
        return (jax.nn.silu(xb @ w_g[e]) * (xb @ w_u[e])) @ w_d[e]

    ys = lax.map(expert_block, (xs, block_expert)).reshape(n_rows, d)
    y = jax.ops.segment_sum(ys * row_w[:, None], row_tok, num_segments=t + 1)[:t]
    return y.reshape(bn, sn, d).astype(h.dtype)

def setup_inputs(seed: int = 0) -> dict:
    key = jax.random.key(seed)
    ks = jax.random.split(key, 22)
    f32 = jnp.float32

    def normal(k, shape, scale):
        return jax.random.normal(k, shape, f32) * scale

    def gain(k, shape):
        return 1.0 + 0.01 * jax.random.normal(k, shape, f32)

    return {
        'x': normal(ks[0], (BATCH, SEQ, D_MODEL), 1.0),
        'rel_bias_table': normal(ks[1], (REL_BUCKETS, ATTN_HEADS), 0.1),
        'norm_mix': gain(ks[2], (DEPTH, D_MODEL)),
        'w_in': normal(ks[3], (DEPTH, D_MODEL, D_IN), D_MODEL ** -0.5),
        'conv_w': normal(ks[4], (DEPTH, CONV_WIDTH, CONV_DIM), CONV_WIDTH ** -0.5),
        'conv_b': normal(ks[5], (DEPTH, CONV_DIM), 0.02),
        'q_norm': gain(ks[6], (DEPTH, ATTN_HEAD_DIM)),
        'k_norm': gain(ks[7], (DEPTH, ATTN_HEAD_DIM)),
        'w_gla_alpha': normal(ks[8], (DEPTH, GLA_GATE_RANK, GLA_QK_DIM), GLA_GATE_RANK ** -0.5),
        'b_gla_alpha': normal(ks[9], (DEPTH, GLA_QK_DIM), 0.1),
        'gla_out_norm': gain(ks[10], (DEPTH, GLA_VALUE_DIM)),
        'w_merge_gate': normal(ks[11], (DEPTH, N_BRANCHES, D_MODEL, D_MODEL), D_MODEL ** -0.5),
        'w_branch': normal(ks[12], (DEPTH, N_BRANCHES, BRANCH_DIM, D_MODEL), BRANCH_DIM ** -0.5),
        'w_out': normal(ks[13], (DEPTH, D_MODEL, D_MODEL), D_MODEL ** -0.5),
        'norm_ffn': gain(ks[14], (DEPTH, D_MODEL)),
        'w_router_group': normal(ks[15], (DEPTH, D_MODEL, N_GROUPS), D_MODEL ** -0.5),
        'b_router_group': normal(ks[16], (DEPTH, N_GROUPS), 0.01),
        'w_router_expert': normal(ks[17], (DEPTH, D_MODEL, N_EXPERTS), D_MODEL ** -0.5),
        'b_router_expert': normal(ks[18], (DEPTH, N_EXPERTS), 0.01),
        'w_expert_gate': normal(ks[19], (DEPTH, N_EXPERTS, D_MODEL, EXPERT_FF), D_MODEL ** -0.5),
        'w_expert_up': normal(ks[20], (DEPTH, N_EXPERTS, D_MODEL, EXPERT_FF), D_MODEL ** -0.5),
        'w_expert_down': normal(ks[21], (DEPTH, N_EXPERTS, EXPERT_FF, D_MODEL), EXPERT_FF ** -0.5),
    }

def reference(x, rel_bias_table, norm_mix, w_in, conv_w, conv_b, q_norm, k_norm,
              w_gla_alpha, b_gla_alpha, gla_out_norm, w_merge_gate, w_branch, w_out,
              norm_ffn, w_router_group, b_router_group, w_router_expert, b_router_expert,
              w_expert_gate, w_expert_up, w_expert_down):
    bn, sn, _ = x.shape
    split_points = np.cumsum(IN_SPLITS)[:-1].tolist()
    for l in range(DEPTH):
        h = rms_norm(x, norm_mix[l])
        (cb, cc, cx, aq, ak, av, gq, gk, gv, gr, gz) = jnp.split(h @ w_in[l], split_points, axis=-1)
        y_conv = short_conv(cb, cc, cx, conv_w[l], conv_b[l])
        q = rms_norm(aq.reshape(bn, sn, ATTN_HEADS, ATTN_HEAD_DIM), q_norm[l])
        k = rms_norm(ak.reshape(bn, sn, ATTN_HEADS, ATTN_HEAD_DIM), k_norm[l])
        v = av.reshape(bn, sn, ATTN_HEADS, ATTN_HEAD_DIM)
        y_attn = moba_attention(q, k, v, rel_bias_table)
        y_gla = gla(gq, gk, gv, gr, gz, w_gla_alpha[l], b_gla_alpha[l], gla_out_norm[l])
        merged = jnp.zeros_like(x)
        for n, y_b in enumerate((y_conv, y_attn, y_gla)):
            merged = merged + jax.nn.sigmoid(h @ w_merge_gate[l, n]) * (y_b @ w_branch[l, n])
        x = x + merged @ w_out[l]
        h2 = rms_norm(x, norm_ffn[l])
        x = x + hier_moe(h2, w_router_group[l], b_router_group[l], w_router_expert[l], b_router_expert[l],
                         w_expert_gate[l], w_expert_up[l], w_expert_down[l])
    return x


_drawn_inputs = setup_inputs


def setup_inputs(seed=0):
    import zlib

    import numpy as np

    out = dict(_drawn_inputs(seed))
    spreads = {}
    factors = {'rel_bias_table': 25.568,
     'norm_mix': 3.319,
     'conv_b': 16.793,
     'q_norm': 41.914,
     'k_norm': 50.016,
     'b_gla_alpha': 3.359,
     'gla_out_norm': 21.751,
     'norm_ffn': 12.418,
     'b_router_group': 30.468,
     'b_router_expert': 29.128}
    for name, (base, spread) in spreads.items():
        noise = np.random.default_rng([zlib.crc32(name.encode()), seed]).standard_normal(out[name].shape)
        drawn = base * np.exp(spread * noise) if base else spread * noise
        out[name] = __import__('jax').numpy.asarray(drawn.astype(out[name].dtype))
    for name, factor in factors.items():
        out[name] = (out[name] * factor).astype(out[name].dtype)
    return out
```

```python
import math
from contextlib import ExitStack

import numpy as np

import concourse.bass as bass
from concourse import mybir

F32 = mybir.dt.float32
F32R = mybir.dt.float32r
BF16 = mybir.dt.bfloat16
I32 = mybir.dt.int32
U32 = mybir.dt.uint32
ALU = mybir.AluOpType
ACT = mybir.ActivationFunctionType
AX_X = mybir.AxisListType.X

P = 128
T = 256
TT = T // P
D = 1024
KD = D // P
C = 512
KC = C // P
EPS = 1e-6
NH = 8
DH = 64
GH = 4
GK = 64
GV = 128
CH = 64
TEMP = 16.0
NG = 4
EPG = 8
NE = NG * EPG
TOPK = 2
SLOTS = T * TOPK
WIN = 64
MAXWIN = T // WIN
SPAD = SLOTS + WIN
BUCKETS = 32
MAXDIST = 128
NEG = -1e30

RING = 6
SLOT = KD * C
NPRE = 20
PER_PASS = 3 * NE
N_EARLY = 3
N_SMALL = 16
CHUNK_T = 2
CHUNKS = KD // CHUNK_T
CW = CHUNK_T * C
POOL_LO = (3,)
FREED_SEED = RING * CHUNKS


def bucket_onehot():
    n = T - 1 - np.arange(T)
    exact = BUCKETS // 2
    scaled = np.log(np.maximum(n, exact).astype(np.float32) / exact) / math.log(MAXDIST / exact)
    large = np.minimum(exact + (scaled * (BUCKETS - exact)).astype(np.int32), BUCKETS - 1)
    b = np.where(n < exact, n, large)
    return (b[None, :] == np.arange(BUCKETS)[:, None]).astype(np.float32)


def flat(v):
    names = "abcd"[:len(v.shape) - 1]
    return v.rearrange(f"p {' '.join(names)} -> p ({' '.join(names)})")


def hybrid_block(nc, x, rel_bias_table, norm_mix, w_in, conv_w, conv_b, q_norm, k_norm, w_gla_alpha,
                 b_gla_alpha, gla_out_norm, w_merge_gate, w_branch, w_out, norm_ffn, w_router_group,
                 b_router_group, w_router_expert, b_router_expert, w_expert_gate, w_expert_up,
                 w_expert_down, out):
    ctx = ExitStack()
    top = [16512]

    def place(name, shape, dt, at=None):
        size = int(np.prod(shape[1:])) * mybir.dt.size(dt)
        off = top[0] if at is None else at
        if at is None:
            top[0] = off + (size + 31) // 32 * 32
        assert off + size <= 229344, (name, off + size)
        return nc.alloc_sbuf_tensor_at(name, list(shape), dt, offset=off)

    def sem(name):
        return ctx.enter_context(nc.semaphore(name))

    with ctx:
        ctx.enter_context(nc.allow_non_contiguous_dma("small vectors land one element per partition"))
        onehot_dram = nc.inline_tensor(bucket_onehot(), "bucket_onehot").ap()
        bias_dram = nc.dram_tensor("bias_by_distance", (NH, 384), F32, kind="Internal")
        ysorted = nc.dram_tensor("y_sorted", (SPAD, D), F32, kind="Internal").ap()

        ring = [place(f"ring{s}", [P, SLOT], F32) for s in range(RING)]
        x_tok = place("x_tok", [P, TT, D], F32)
        xn = place("xn_merged", [P, TT, D], F32)
        ident = place("ident", [P, P], F32)
        antid = place("antid", [P, P], F32)
        ones_bf = place("ones_bf", [P, P], BF16)
        tri_bf = place("tri_bf", [P, P], BF16)
        ones_row = place("ones_row", [1, P], F32)
        mergedT = xn[:, :, :].rearrange("p a b -> p (a b)").rearrange("p (k t) -> p k t", k=KD)
        g_mix = place("g_mix", [P, KD], F32)
        g_ffn = place("g_ffn", [P, KD], F32)
        cw_sb = place("cw_sb", [P, 3, KC], F32)
        cb_sb = place("cb_sb", [P, KC], F32)
        qn_w = place("qn_w", [P, 1], F32)
        kn_w = place("kn_w", [P, 1], F32)
        b_al = place("b_al", [P, 2], F32)
        on_w = place("on_w", [P, 1], F32)
        w_al = place("w_al", [16, 256], F32)
        zT = place("zT", [16, T], F32)
        table = place("table", [BUCKETS, NH], F32)
        w_z = place("w_z", [P, KD, 16], F32)
        w_r = place("w_r", [P, KD, NG + NE], F32)
        b_r = place("b_r", [1, NG + NE], F32)
        stat = place("stat", [P, 64], F32)
        reset = place("reset", [P, T], F32)
        qkm = place("qkm", [P, 2, TT, NH], F32)
        qkr = place("qkr", [P, 2, TT, NH], F32)
        nmx = place("nmx", [P, NH, TT], F32)
        rsum = place("rsum", [P, NH, TT], F32)
        lgp = place("lgp", [P, TT, 8], F32)
        le = place("le", [P, TT, NE], F32)
        mg8 = place("mg8", [P, TT, 8], F32)
        ig8 = place("ig8", [P, TT, 8], U32)
        me8 = place("me8", [P, TT, 8], F32)
        ie8 = place("ie8", [P, TT, 8], U32)
        rt = place("rt", [P, TT, 16], F32)
        les = place("les", [P, TT, 8], F32)
        lsel = place("lsel", [P, TT, NE], F32)
        e1h = place("e1h", [P, TT, NE], F32)
        e2h = place("e2h", [P, TT, NE], F32)
        eall = place("eall", [P, TT, NE], F32)
        epre = place("epre", [P, TT, NE], F32)
        eall_bf = place("eall_bf", [P, TT, NE], BF16)
        epre_bf = place("epre_bf", [P, TT, NE], BF16)
        iota_f = place("iota_f", [P, NE], F32)
        slotf = place("slotf", [P, TT, 2], F32)
        slot_u = place("slot_u", [P, TT * 2], U32)
        wts = place("wts", [P, TT, 2], F32)
        offf = place("offf", [1, MAXWIN * NE + 1], F32)
        off_tab = place("off_tab", [1, MAXWIN * NE + 1], I32)
        cntr = place("cntr", [1, 8], F32)
        npass = place("npass", [1, 1], I32)
        region = top[0]

        def here(name, shape, dt):
            nonlocal_at = here_at[0]
            here_at[0] += (int(np.prod(shape[1:])) * mybir.dt.size(dt) + 31) // 32 * 32
            return place(name, shape, dt, at=nonlocal_at)

        here_at = [region]
        sig = here("sig", [P, 2, KD, T], F32)
        onehot = place("onehot", [BUCKETS, T], F32, at=region)
        bias_row = place("bias_row", [NH, 384], F32, at=region + 4 * T)
        hT = here("hT", [P, KD, T], F32)
        ycT = here("ycT", [P, KC, T], F32)
        conv_u = here("conv_u", [P, KC, T + 2], F32)
        aqk = here("aqk", [P, 2, TT, C], F32)
        qTz = here("qTz", [P, NH, T], F32)
        kT = here("kT", [P, KC, T], F32)
        av = here("av", [P, TT, C], F32)
        gqk = here("gqk", [P, 4, T], F32)
        attm = here("attm", [P, 8, P], F32)
        gv = here("gv", [P, TT, C], F32)
        gr = here("gr", [P, TT, C], F32)
        kdn = here("kdn", [P, TT, 256], F32)
        sbd = here("sbd", [P, 3, 2, 256], F32)
        scr = here("scr", [P, 2, C], F32)
        la, e_pos, e_neg, e_rest = (qTz[:, 2 * i:2 * i + 2, :] for i in range(4))
        bias_h = gqk
        yaT = attm[:, :, :].rearrange("p a b -> p (a b)").rearrange("p (a b) -> p a b", a=KC)
        ygT = gv[:, :, :].rearrange("p a b -> p (a b)").rearrange("p (a b) -> p a b", a=KC)
        prob = aqk[:, 0, :, :].rearrange("p a b -> p (a b)")[:, 0:768].rearrange("p (a b) -> p a b", a=2)
        probT = aqk[:, 1, :, :].rearrange("p a b -> p (a b)")[:, 0:768].rearrange("p (a b) -> p a b", a=2)

        here_at = [region]
        xs = here("xs", [P, KD, SPAD], F32)
        w_hi = [here(f"w_hi{c}", [P, CHUNK_T, C], F32R) for c in range(CHUNKS)]
        w_lo = [here(f"w_lo{c}", [P, CHUNK_T, C], F32R) for c in range(CHUNKS)]
        xe = [here(f"xe{b}", [P, KD, 2 * WIN], F32R) for b in range(2)]
        g_lo = here("g_lo", [WIN, C], F32)
        u_lo = here("u_lo", [WIN, C], F32)
        g_sum = here("g_sum", [WIN, C], F32)
        u_sum = here("u_sum", [WIN, C], F32)
        g_act = here("g_act", [WIN, C], F32)
        h_tok = here("h_tok", [WIN, C], F32)
        he = here("he", [P, KC, 2 * WIN], F32R)
        y_lo_at = here_at[0]
        y_lo = here("y_lo", [WIN, D], F32)
        y_at = here_at[0]
        y_tok = here("y_tok", [WIN, 2, D], F32)
        iota_s = place("iota_s", [P, SLOTS], F32, at=y_lo_at)
        perm = place("perm", [P, TT, SLOTS], F32, at=y_at)
        y_back = place("y_back", [P, TT * 2, D], F32, at=region)

        ps = ctx.enter_context(nc.psum_tensor("ps", [P, 8, 512], F32))

        def bank(b, a=None):
            v = ps[:, b, :]
            return v if a is None else v.rearrange("p (a b) -> p a b", a=a)

        x_in = [sem(f"x_in{i}") for i in range(TT)]
        early_in = sem("early_in")
        small_in = sem("small_in")
        wz_in = sem("wz_in")
        landed = [sem(f"landed{s}") for s in range(RING)]
        consts = sem("consts")
        v_chain = sem("v_chain")
        a_chain = sem("a_chain")
        g_chain = sem("g_chain")
        ms_ready = sem("ms_ready")
        rms_ready = sem("rms_ready")
        xn_ready = sem("xn_ready")
        hT_turned = sem("hT_turned")
        biasrow_mm = sem("biasrow_mm")
        biasrow_ready = sem("biasrow_ready")
        bias_stored = sem("bias_stored")
        bias_in = [sem(f"bias_in{i}") for i in range(4)]
        proj_done = sem("proj_done")
        evacuated = [sem(f"evacuated{b}") for b in range(4)]
        hT_act = sem("hT_act")
        hT_dve = sem("hT_dve")
        xs_act = sem("xs_act")
        xs_dve = sem("xs_dve")
        freed = sem("freed")
        y_free = sem("y_free")
        z_mm = sem("z_mm")
        z_ready = sem("z_ready")
        alpha_mm = sem("alpha_mm")
        sigmin_ready = sem("sigmin_ready")
        softplus_ready = sem("softplus_ready")
        cum_ready = sem("cum_ready")
        decay_ready = sem("decay_ready")
        gla_in_ready = sem("gla_in_ready")
        kd_turned = sem("kd_turned")
        kdn_ready = sem("kdn_ready")
        att_mm = sem("att_mm")
        att_copied = sem("att_copied")
        att_ready = sem("att_ready")
        kv_mm = sem("kv_mm")
        state_ready = sem("state_ready")
        sbd_zero = sem("sbd_zero")
        o_mm = sem("o_mm")
        o_sq = sem("o_sq")
        o_ms = sem("o_ms")
        o_rms = sem("o_rms")
        ygla_ready = sem("ygla_ready")
        yg_turned = sem("yg_turned")
        ygT_ready = sem("ygT_ready")
        qk_ms = sem("qk_ms")
        qk_rms = sem("qk_rms")
        qkn_ready = sem("qkn_ready")
        qz_zero = sem("qz_zero")
        qk_turned = sem("qk_turned")
        qT_ready = sem("qT_ready")
        kT_ready = sem("kT_ready")
        score_mm = sem("score_mm")
        rowmax_ready = sem("rowmax_ready")
        exp_ready = sem("exp_ready")
        prob_ready = sem("prob_ready")
        prob_turned = sem("prob_turned")
        probT_ready = sem("probT_ready")
        pv_mm = sem("pv_mm")
        yaT_ready = sem("yaT_ready")
        branch_done = sem("branch_done")
        x1_ready = sem("x1_ready")
        ms2_ready = sem("ms2_ready")
        rms2_ready = sem("rms2_ready")
        h2_ready = sem("h2_ready")
        h2_turned = sem("h2_turned")
        router_mm = sem("router_mm")
        nmax_ready = sem("nmax_ready")
        gexp_ready = sem("gexp_ready")
        e2in_ready = sem("e2in_ready")
        e2_ready = sem("e2_ready")
        assign_ready = sem("assign_ready")
        pos_mm = sem("pos_mm")
        perm_ready = sem("perm_ready")
        route_ready = sem("route_ready")
        gather_mm = sem("gather_mm")
        iota_ready = sem("iota_ready")
        xe_high = sem("xe_high")
        xe_ready = sem("xe_ready")
        hi_ready = sem("hi_ready")
        lo_ready = sem("lo_ready")
        lo_ready_pool = sem("lo_ready_pool")
        gu_lo_out = sem("gu_lo_out")
        gu_free = sem("gu_free")
        silu_ready = sem("silu_ready")
        h_ready = sem("h_ready")
        h_turned = sem("h_turned")
        he_hi = sem("he_hi")
        he_lo = sem("he_lo")
        y_lo_out = sem("y_lo_out")
        y_ready = sem("y_ready")
        y_stored = sem("y_stored")
        back_in = [sem(f"back_in{j}") for j in range(2 * TT)]
        fin_ready = sem("fin_ready")
        stored = sem("stored")

        w_in_v = w_in[0].rearrange("(p k) n -> p k n", k=KD)
        w_out_v = w_out[0].rearrange("(k p) n -> p k n", p=P)
        cols = [3072, 3584, 4096, 1536, 2048, 2560, 512, 1024, 0]
        pre = [("in", c) for c in cols]
        for n in range(3):
            pre += [("gate", n, 0), ("gate", n, 1), ("branch", n)]
        pre += [("out", 0), ("out", 1)]
        first_bank = []
        at = 0
        for s in pre:
            first_bank.append(at)
            at += 4 if s[0] == "branch" else 2
        first_bank.append(at)
        assert len(pre) == NPRE

        def pre_source(g):
            kind = pre[g]
            if kind[0] == "in":
                return w_in_v[:, :, kind[1]:kind[1] + C], C
            if kind[0] == "gate":
                return w_merge_gate[0, kind[1]].rearrange("(p k) n -> p k n", k=KD)[:, :, kind[2] * C:(kind[2] + 1) * C], C
            if kind[0] == "branch":
                return w_branch[0, kind[1]].rearrange("(k p) n -> p k n", p=P), D
            return w_out_v[:, :, kind[1] * C:(kind[1] + 1) * C], C

        wg_v = w_expert_gate[0].rearrange("e (p k) n -> e p (k n)", k=KD)
        wu_v = w_expert_up[0].rearrange("e (p k) n -> e p (k n)", k=KD)
        wd_v = w_expert_down[0].rearrange("e (k p) n -> e p k n", p=P)

        def slot_of(q):
            return (NPRE + q) % RING

        def uses_before(q):
            return (NPRE + q) // RING

        def after_slots(p, n):
            return PER_PASS * CHUNKS * p + CHUNKS * n + FREED_SEED

        def bank_of(g, m):
            r = first_bank[g] + m
            return r % 4, r // 4

        def w3(s):
            return ring[s][:, :].rearrange("p (k n) -> p k n", n=C)

        def w4(s):
            return ring[s][:, :].rearrange("p (k n) -> p k n", n=D)

        block = ctx.enter_context(nc.Block())

        @block.sync
        def _(sp):
            for tt in range(TT):
                sp.dma_start(x_tok[:, tt, :], x[0, tt * P:(tt + 1) * P, :]).then_inc(x_in[tt], 16)

            def load_expert(kind, e, q, p, i, first=False):
                if first and q < RING:
                    sp.wait_ge(proj_done, first_bank[NPRE + q - RING + 1])
                else:
                    sp.wait_ge(freed, (PER_PASS * CHUNKS) * p + RING * CHUNKS * i + CHUNKS * (q - RING + 1)
                               + FREED_SEED)
                s = slot_of(q)
                if kind == "d":
                    src = wd_v[bass.ds(e, 1), :, :, :].rearrange("e p k n -> (e p) k n")
                    sp.dma_start(w4(s), src).then_inc(landed[s], 16)
                else:
                    src = (wg_v if kind == "g" else wu_v)[bass.ds(e, 1), :, :].rearrange("e p n -> (e p) n")
                    sp.dma_start(ring[s][:, :], src).then_inc(landed[s], 16)

            def start_of_pass(p, first):
                load_expert("g", 0, 0, p, 0, first)
                load_expert("u", 0, 1, p, 0, first)
                load_expert("g", 1, 2, p, 0, first)
                load_expert("u", 1, 3, p, 0, first)
                load_expert("d", 0, 4, p, 0, first)

            def pair(p, i):
                for s in range(2):
                    load_expert("g", 2 + 2 * i + s, 5 + 3 * s, p, i)
                    load_expert("u", 2 + 2 * i + s, 6 + 3 * s, p, i)
                    load_expert("d", 1 + 2 * i + s, 7 + 3 * s, p, i)

            for g in range(NPRE):
                if g >= RING:
                    sp.wait_ge(proj_done, first_bank[g - RING + 1])
                src, n = pre_source(g)
                s = g % RING
                sp.dma_start(ring[s][:, :].rearrange("p (k n) -> p k n", n=n), src).then_inc(landed[s], 16)
                if g == 0:
                    sp.wait_ge(early_in, 16 * N_EARLY)
                    sp.dma_start(w_z[:, :, :], w_in_v[:, :, 4608:4624]).then_inc(wz_in, 16)
            start_of_pass(0, True)
            sp.wait_ge(route_ready, 1)
            passes = sp.value_load(npass[0:1, 0:1], min_val=1, max_val=MAXWIN)
            with sp.Fori(0, passes) as p:
                with sp.If(p > 0):
                    start_of_pass(p, False)
                with sp.Fori(0, NE // 2 - 1) as i:
                    pair(p, i)
                load_expert("d", NE - 1, PER_PASS - 1, p, 0)
            for tt in range(TT):
                sp.wait_ge(fin_ready, tt + 1)
                sp.dma_start(out[0, tt * P:(tt + 1) * P, :], x_tok[:, tt, :]).then_inc(stored, 16)
            sp.wait_ge(stored, 16 * TT)

        @block.gpsimd
        def _(pool):
            g = nc.gpsimd
            steps = [0]

            def link(ins):
                steps[0] += 1
                ins.then_inc(g_chain, 1)
                pool.wait_ge(g_chain, steps[0])

            g.memset(ident[:, :], 0.0)
            g.memset(antid[:, :], 0.0)
            g.memset(ones_bf[:, :], 1.0)
            g.memset(ones_row[:, :], 1.0)
            g.memset(tri_bf[:, :], 1.0)
            g.memset(reset[:, :], 1.0)
            g.memset(conv_u[:, :, 0:2], 0.0)
            link(g.memset(bias_row[:, T:384], NEG))
            g.affine_select(out=ident[:, :], in_=ident[:, :], compare_op=ALU.not_equal, fill=1.0, base=0,
                            pattern=[[-1, P]], channel_multiplier=1).then_inc(consts, 1)
            g.affine_select(out=antid[:, :], in_=antid[:, :], compare_op=ALU.not_equal, fill=1.0, base=-(P - 1),
                            pattern=[[1, P]], channel_multiplier=1).then_inc(consts, 1)
            g.affine_select(out=tri_bf[:, :], in_=tri_bf[:, :], compare_op=ALU.is_gt, fill=0.0, base=0,
                            pattern=[[1, P]], channel_multiplier=-1).then_inc(consts, 1)
            g.memset(reset[:, :].rearrange("p (c n) -> p c n", n=CH)[:, :, 0:1], 0.0).then_inc(consts, 1)
            g.iota(iota_f[:, :], pattern=[[1, NE]], base=0, channel_multiplier=0,
                   allow_small_or_imprecise_dtypes=True).then_inc(consts, 1)
            g.memset(sbd[:, :, :, :], 0.0).then_inc(sbd_zero, 1)
            g.memset(offf[:, MAXWIN * NE:], 0.0)
            g.memset(lgp[:, :, NG:], -3e38).then_inc(consts, 1)

            smalls = [
                (w_al[:, :], w_gla_alpha[0]),
                (b_al[:, :], b_gla_alpha[0].rearrange("(a p) -> p a", p=P)),
                (qn_w[0:DH, :], q_norm[0].rearrange("(p a) -> p a", a=1)),
                (qn_w[DH:P, :], q_norm[0].rearrange("(p a) -> p a", a=1)),
                (kn_w[0:DH, :], k_norm[0].rearrange("(p a) -> p a", a=1)),
                (kn_w[DH:P, :], k_norm[0].rearrange("(p a) -> p a", a=1)),
                (on_w[:, :], gla_out_norm[0].rearrange("(p a) -> p a", a=1)),
                (cb_sb[:, :], conv_b[0].rearrange("(k p) -> p k", p=P)),
                (g_ffn[:, :], norm_ffn[0].rearrange("(p k) -> p k", k=KD)),
                (b_r[:, 0:NG], b_router_group),
                (b_r[:, NG:NG + NE], b_router_expert),
                (w_r[:, :, 0:NG], w_router_group[0].rearrange("(p k) n -> p k n", k=KD)),
                (w_r[:, :, NG:NG + NE], w_router_expert[0].rearrange("(p k) n -> p k n", k=KD)),
            ] + [(cw_sb[:, j, :], conv_w[0, j].rearrange("(k p) -> p k", p=P)) for j in range(3)]
            assert len(smalls) == N_SMALL
            for dst, src in smalls:
                pool.dma_start(dst, src).then_inc(small_in, 16)

            pool.wait_ge(biasrow_ready, 1)
            pool.dma_start(bias_dram.ap(), bias_row[:, :]).then_inc(bias_stored, 16)

            pool.wait_ge(att_copied, 2)
            for a in range(4):
                v = attm[:, 2 * a:2 * a + 2, :]
                link(g.affine_select(out=v, in_=v, compare_op=ALU.is_ge, fill=0.0, base=0,
                                     pattern=[[0, 2], [1, P]], channel_multiplier=-1))
            g.memset(attm[0:CH, :, CH:P], 0.0).then_inc(att_ready, 1)
            pool.wait_ge(kd_turned, 1)
            pool.wait_ge(state_ready, 3)
            qz = qTz[:, :, :].rearrange("p (b two) t -> p b two t", two=2)
            g.memset(qz[DH:P, :, 0, :], 0.0).then_inc(qz_zero, 1)
            g.memset(qz[0:DH, :, 1, :], 0.0).then_inc(qz_zero, 1)
            pool.wait_ge(bias_stored, 16)
            pool.wait_ge(o_mm, 2)
            for h in range(NH):
                if h >= 4:
                    pool.wait_ge(score_mm, h - 3)
                pool.dma_start(bias_h[:, h % 4, :], bass.AP(bias_dram, h * 384, [[1, P], [1, T]])
                               ).then_inc(bias_in[h % 4], 16)
            pool.wait_ge(h2_ready, 2)
            g.iota(iota_s[:, :], pattern=[[1, SLOTS]], base=0, channel_multiplier=0,
                   allow_small_or_imprecise_dtypes=True).then_inc(iota_ready, 1)
            pool.wait_ge(router_mm, 1)
            g.memset(xs[:, :, SLOTS:SPAD], 0.0).then_inc(iota_ready, 1)
            pool.sem_inc(y_free, 2)

            pool.wait_ge(route_ready, 1)
            pool.wait_ge(xs_act, KD // 2)
            pool.wait_ge(xs_dve, KD // 2)
            pool.wait_ge(iota_ready, 2)
            passes = pool.value_load(npass[0:1, 0:1], min_val=1, max_val=MAXWIN)

            def offset(p, e):
                return pool.value_load(off_tab[0:1, bass.ds(p * NE + e, 1)], min_val=0, max_val=SLOTS)

            def window(p, e, b):
                n = (NE + 1) * p + e
                off = offset(p, e)
                v = xs[:, :, bass.ds(off, WIN)]
                g.tensor_copy(xe[b][:, :, 0:WIN], v).then_inc(xe_high, 1)
                pool.wait_ge(xe_high, n + 1)
                pool.sem_inc(xe_ready, 1)
                g.tensor_tensor(xe[b][:, :, WIN:2 * WIN], v, xe[b][:, :, 0:WIN].bitcast(F32),
                                ALU.subtract).then_inc(xe_ready, 1)

            def low_part(p, i, q):
                s = slot_of(q)
                for c in POOL_LO:
                    n = PER_PASS * CHUNKS * p + RING * CHUNKS * i + CHUNKS * q + c
                    pool.wait_ge(hi_ready, n + 1)
                    g.tensor_tensor(w_lo[c][:, :, :], w3(s)[:, CHUNK_T * c:CHUNK_T * (c + 1), :],
                                    w_hi[c][:, :, :].bitcast(F32), ALU.subtract).then_inc(lo_ready_pool, 1)

            def store(p, e, b):
                off = offset(p, e)
                pool.wait_ge(y_ready, NE * p + e + 2)
                pool.dma_start(ysorted[bass.ds(off, WIN), :], y_tok[:, b, :]).then_inc(y_stored, 16)
                pool.wait_ge(y_stored, (16 * NE) * p + 16 * e + 16)
                pool.sem_inc(y_free, 1)

            with pool.Fori(0, passes) as p:
                pool.wait_ge(freed, after_slots(p, 0))
                window(p, 0, 0)
                window(p, 1, 1)
                low_part(p, 0, 0)
                low_part(p, 0, 1)
                low_part(p, 0, 2)
                pool.wait_ge(freed, after_slots(p, 2))
                window(p, 2, 0)
                low_part(p, 0, 3)
                low_part(p, 0, 4)
                with pool.Fori(0, NE // 2 - 1) as i:
                    for s in range(2):
                        low_part(p, i, 5 + 3 * s)
                        pool.wait_ge(freed, after_slots(p, 6 * i + (4 + 3 * s)))
                        window(p, 3 + 2 * i + s, (s + 1) % 2)
                        low_part(p, i, 6 + 3 * s)
                        store(p, 2 * i + s, s)
                        low_part(p, i, 7 + 3 * s)
                low_part(p, 0, PER_PASS - 1)
                store(p, NE - 2, 0)
                store(p, NE - 1, 1)
            for j in range(2 * TT):
                g.indirect_dma_start(out=y_back[:, j, :], out_offset=None, in_=ysorted[0:SLOTS, :],
                                     in_offset=bass.IndirectOffsetOnAxis(ap=slot_u[:, j:j + 1], axis=0)
                                     ).then_inc(back_in[j], 16)
            for j in range(2 * TT):
                pool.wait_ge(back_in[j], 16)

        @block.scalar
        def _(act):
            s_ = nc.scalar

            early = [(g_mix[:, :], norm_mix[0].rearrange("(p k) -> p k", k=KD)),
                     (onehot[:, :], onehot_dram),
                     (table[:, :], rel_bias_table)]
            assert len(early) == N_EARLY
            for dst, src in early:
                act.dma_start(dst, src).then_inc(early_in, 16)

            act.wait_ge(ms_ready, 2)
            s_.activation(stat[:, 2:4], stat[:, 0:2], ACT.Sqrt).then_inc(rms_ready, 1)
            act.wait_ge(early_in, 16 * N_EARLY)
            for kp in range(2):
                act.wait_ge(hT_turned, kp + 1)
                for k in range(2):
                    s_.activation(hT[:, 2 * kp + k, :], bank(4 + kp, 2)[:, k, :], ACT.Copy,
                                  scale=g_mix[:, 2 * kp + k:2 * kp + k + 1]).then_inc(hT_act, 1)

            def evac(g, m, dst, func=ACT.Copy, scale=1.0):
                b, _ = bank_of(g, m)
                act.wait_ge(proj_done, first_bank[g] + m + 1)
                s_.activation(dst, bank(b), func, scale=scale).then_inc(evacuated[b], 1)

            evac(0, 0, flat(gqk[:, 0:2, :]), scale=float(GK) ** -0.5)
            evac(0, 1, flat(gqk[:, 2:4, :]))
            act.wait_ge(z_mm, 1)
            s_.activation(zT[:, :], ps[0:16, 4, 0:T], ACT.Copy).then_inc(z_ready, 1)
            evac(1, 0, gv[:, 0, :])
            act.wait_ge(small_in, 16 * N_SMALL)
            act.wait_ge(sigmin_ready, 2)
            for a in range(2):
                s_.activation(e_pos[:, a, :], bank(5, 2)[:, a, :], ACT.Abs,
                              bias=b_al[:, a:a + 1]).then_inc(a_chain, 1)
            act.wait_ge(a_chain, 2)
            s_.activation(e_pos, e_pos, ACT.Exp, scale=-1.0).then_inc(a_chain, 1)
            act.wait_ge(a_chain, 3)
            s_.activation(e_pos, e_pos, ACT.Ln, bias=1.0).then_inc(softplus_ready, 1)
            evac(1, 1, gv[:, 1, :])
            act.wait_ge(cum_ready, 3)
            s_.activation(e_rest, e_rest, ACT.Exp, scale=1.0 / TEMP).then_inc(decay_ready, 1)
            s_.activation(e_pos, la, ACT.Exp, scale=1.0 / TEMP).then_inc(decay_ready, 1)
            s_.activation(e_neg, la, ACT.Exp, scale=-1.0 / TEMP).then_inc(decay_ready, 1)
            evac(2, 0, gr[:, 0, :], func=ACT.Silu)
            act.wait_ge(kd_turned, 1)
            s_.activation(flat(kdn[:, :, :]), bank(6), ACT.Copy).then_inc(kdn_ready, 1)
            evac(2, 1, gr[:, 1, :], func=ACT.Silu)
            for tt in range(TT):
                act.wait_ge(o_mm, tt + 1)
                s_.activation(scr[:, tt, :], bank(4 if tt == 0 else 7), ACT.Square).then_inc(o_sq, 1)
            act.wait_ge(o_ms, 1)
            s_.activation(stat[:, 16:24], stat[:, 8:16], ACT.Sqrt).then_inc(o_rms, 1)
            act.wait_ge(qk_ms, 1)
            s_.activation(qkr[:, :, :, :], qkm[:, :, :, :], ACT.Sqrt).then_inc(qk_rms, 1)
            evac(5, 0, av[:, 0, :])
            evac(5, 1, av[:, 1, :])
            for m in range(2):
                act.wait_ge(yg_turned, 2)
                s_.activation(ygT[:, 2 * m:2 * m + 2, :], bank(5 + m, 2), ACT.Copy,
                              scale=on_w[:, 0:1]).then_inc(ygT_ready, 1)
            for m in range(2):
                act.wait_ge(qk_turned, 3 + m)
                s_.activation(kT[:, 2 * m:2 * m + 2, :], bank(6 + m, 2), ACT.Copy,
                              scale=kn_w[:, 0:1]).then_inc(kT_ready, 1)

            def softmax_exp(h):
                act.wait_ge(rowmax_ready, h + 1)
                if h >= 2:
                    act.wait_ge(prob_turned, h - 1)
                for tt in range(TT):
                    s_.activation(prob[:, h % 2, P * tt:P + 2 * P * tt], ps[:, 4 + h % 2, P * tt:P + 2 * P * tt],
                                  ACT.Exp, bias=nmx[:, h, tt:tt + 1],
                                  accum_out=rsum[:, h, tt:tt + 1]).then_inc(exp_ready, 1)

            def prob_out(h):
                act.wait_ge(prob_turned, h + 1)
                if h >= 2:
                    act.wait_ge(pv_mm, h - 1)
                s_.activation(probT[:, h % 2, :], bank(6)[:, 0:384], ACT.Copy).then_inc(probT_ready, 1)

            def gate_out(n, half, m):
                if n == 2:
                    act.wait_ge(branch_done, 2 * half + m + 1)
                dt = 4 * half + 2 * m
                evac(9 + 3 * n + half, m, flat(sig[:, n % 2, dt:dt + 2, :]), func=ACT.Sigmoid)

            evac(6, 0, flat(ycT[:, 0:2, :]))
            softmax_exp(0)
            evac(6, 1, flat(ycT[:, 2:4, :]))
            for h in range(1, NH):
                softmax_exp(h)
                prob_out(h - 1)
                if h >= 6:
                    gate_out(0, 0, h - 6)
            prob_out(NH - 1)
            gate_out(0, 1, 0)
            gate_out(0, 1, 1)
            for n in range(1, 3):
                for half in range(2):
                    for m in range(2):
                        gate_out(n, half, m)

            act.wait_ge(ms2_ready, 2)
            s_.activation(stat[:, 2:4], stat[:, 0:2], ACT.Sqrt).then_inc(rms2_ready, 1)
            for kp in range(2):
                act.wait_ge(h2_turned, kp + 1)
                for k in range(2):
                    s_.activation(hT[:, 2 * kp + k, :], bank(4 + kp, 2)[:, k, :], ACT.Copy,
                                  scale=g_ffn[:, 2 * kp + k:2 * kp + k + 1]).then_inc(hT_act, 1)
            act.wait_ge(nmax_ready, 1)
            for tt in range(TT):
                s_.activation(rt[:, tt, 8:12], lgp[:, tt, 0:NG], ACT.Exp, bias=rt[:, tt, 0:1],
                              accum_out=rt[:, tt, 1:2]).then_inc(gexp_ready, 1)
            act.wait_ge(e2in_ready, 1)
            s_.activation(rt[:, :, 3:4], rt[:, :, 2:3], ACT.Exp).then_inc(e2_ready, 1)
            for k in range(0, KD, 2):
                act.wait_ge(gather_mm, k + 1)
                s_.activation(xs[:, k, 0:SLOTS], bank(2 + k % 4), ACT.Copy,
                              scale=g_ffn[:, k:k + 1]).then_inc(xs_act, 1)

            act.wait_ge(route_ready, 1)
            passes = act.value_load(npass[0:1, 0:1], min_val=1, max_val=MAXWIN)

            def high_part(p, i, q, cs):
                s = slot_of(q)
                for c in cs:
                    if c == 0:
                        act.wait_ge(landed[s], (16 * PER_PASS // RING) * p + 16 * i + 16 * (uses_before(q) + 1))
                    act.wait_ge(freed, PER_PASS * CHUNKS * p + RING * CHUNKS * i + CHUNKS * (q - 1) + c + 1
                                + FREED_SEED)
                    s_.activation(w_hi[c][:, :, :], w3(s)[:, CHUNK_T * c:CHUNK_T * (c + 1), :],
                                  ACT.Copy).then_inc(hi_ready, 1)

            def gu_low_rows(p, n, b):
                act.wait_ge(freed, after_slots(p, n))
                s_.activation(g_lo[:, :], ps[WIN:P, 2 * b, :], ACT.Copy).then_inc(gu_lo_out, 1)
                s_.activation(u_lo[:, :], ps[WIN:P, 2 * b + 1, :], ACT.Copy).then_inc(gu_lo_out, 1)

            def silu(p, e):
                act.wait_ge(gu_free, 2 * NE * p + 2 * e + 5)
                s_.activation(g_act[:, :], g_sum[:, :], ACT.Silu).then_inc(silu_ready, 1)

            def he_high(p, e):
                act.wait_ge(h_turned, NE * p + e + 1)
                s_.activation(he[:, :, 0:WIN], ps[:, 6, 0:KC * WIN].rearrange("p (k n) -> p k n", n=WIN),
                              ACT.Copy).then_inc(he_hi, 1)

            def y_low_rows(p, n):
                act.wait_ge(freed, after_slots(p, n))
                s_.activation(y_lo[:, :], flat(ps[WIN:P, 4:6, :]), ACT.Copy).then_inc(y_lo_out, 1)

            def step(p, e, i, q, b, before_gu, before_y):
                high_part(p, i, q, (0,))
                gu_low_rows(p, before_gu, 1 - b)
                high_part(p, i, q, (1,))
                silu(p, e - 1)
                high_part(p, i, q, (2,))
                if before_y is not None:
                    y_low_rows(p, before_y)
                high_part(p, i, q, (3,))
                high_part(p, i, q + 1, (0, 1, 2, 3))
                he_high(p, e - 1)
                high_part(p, i, q + 2, (0, 1, 2, 3))

            with act.Fori(0, passes) as p:
                high_part(p, 0, 0, (0, 1, 2, 3))
                high_part(p, 0, 1, (0, 1, 2, 3))
                step(p, 1, 0, 2, 1, 2, None)
                with act.Fori(0, NE // 2 - 1) as i:
                    for s in range(2):
                        step(p, 2 * i + (2 + s), i, 5 + 3 * s, s, 6 * i + (4 + 3 * s), 6 * i + (5 + 3 * s))
                gu_low_rows(p, PER_PASS - 2, 1)
                silu(p, NE - 1)
                high_part(p, 0, PER_PASS - 1, (0,))
                y_low_rows(p, PER_PASS - 1)
                he_high(p, NE - 1)
                high_part(p, 0, PER_PASS - 1, (1, 2, 3))
                y_low_rows(p, PER_PASS)

        @block.tensor
        def _(pe):
            t_ = nc.tensor

            def turn_x(src, ready, signal):
                pe.wait_ge(ready, TT)
                for kp in range(4):
                    for k in range(2):
                        for tt in range(TT):
                            ins = t_.transpose(bank(4 + kp, 2)[:, k, tt * P:(tt + 1) * P],
                                               src[:, tt, 2 * kp + k::KD], ident[:, :])
                    ins.then_inc(signal, 1)

            def begin(g, m):
                b, use = bank_of(g, m)
                if use:
                    pe.wait_ge(evacuated[b], use)
                if m == 0:
                    pe.wait_ge(landed[g % RING], 16 * (g // RING + 1))
                return b

            def by_token(g, tt):
                b = begin(g, tt)
                for k in range(KD):
                    ins = t_.matmul(bank(b), hT[:, k, tt * P:(tt + 1) * P], w3(g % RING)[:, k, :],
                                    start=(k == 0), stop=(k == KD - 1))
                ins.then_inc(proj_done, 1)

            def by_feature(g, m, w, dt, rhs, nk):
                b = begin(g, m)
                for j in range(2):
                    for k in range(nk):
                        ins = t_.matmul(bank(b, 2)[:, j, :], w[:, k, (dt + j) * P:(dt + j + 1) * P], rhs[:, k, :],
                                        start=(k == 0), stop=(k == nk - 1))
                ins.then_inc(proj_done, 1)

            def feat(g, m):
                by_feature(g, m, w3(g % RING), 2 * m, hT, KD)

            pe.wait_ge(early_in, 16 * N_EARLY)
            pe.wait_ge(consts, 6)
            t_.matmul(ps[0:NH, 3, 0:T], table[:, :], onehot[:, :], start=True, stop=True).then_inc(biasrow_mm, 1)
            turn_x(xn, xn_ready, hT_turned)
            pe.wait_ge(hT_act, 4)
            pe.wait_ge(hT_dve, 4)
            feat(0, 0)
            feat(0, 1)
            pe.wait_ge(wz_in, 16)
            for k in range(KD):
                ins = t_.matmul(ps[0:16, 4, 0:T], w_z[:, k, :], hT[:, k, :], start=(k == 0), stop=(k == KD - 1))
            ins.then_inc(z_mm, 1)
            by_token(1, 0)
            pe.wait_ge(z_ready, 1)
            pe.wait_ge(small_in, 16 * N_SMALL)
            for a in range(2):
                ins = t_.matmul(bank(5, 2)[:, a, :], w_al[:, a * P:(a + 1) * P], zT[:, :], start=True, stop=True)
            ins.then_inc(alpha_mm, 1)
            pe.wait_ge(biasrow_ready, 1)
            by_token(1, 1)
            by_token(2, 0)

            pe.wait_ge(gla_in_ready, 1)
            for tt in range(TT):
                for a in range(2):
                    ins = t_.transpose(bank(6, 4)[:, 2 * tt + a, :], e_rest[:, a, tt * P:(tt + 1) * P], ident[:, :])
            ins.then_inc(kd_turned, 1)
            pe.wait_ge(gla_in_ready, 3)
            for par in range(2):
                for tt in range(TT):
                    for a in range(2):
                        rows = slice(GK * par, GK * par + GK)
                        ins = t_.matmul(bank(4 + 3 * par, 4)[:, 2 * tt + a, :], gqk[rows, 2 + a, tt * P:(tt + 1) * P],
                                        gqk[rows, a, tt * P:(tt + 1) * P], start=True, stop=True)
                ins.then_inc(att_mm, 1)
            by_token(2, 1)
            pe.wait_ge(kdn_ready, 1)
            pe.wait_ge(att_copied, 1)
            pe.wait_ge(evacuated[bank_of(1, 0)[0]], bank_of(1, 0)[1] + 1)
            pe.wait_ge(evacuated[bank_of(1, 1)[0]], bank_of(1, 1)[1] + 1)
            for c in range(3):
                rows = slice(CH * (c % 2), CH * (c % 2) + CH)
                for a in range(2):
                    ins = t_.matmul(bank((5, 6, 4)[c], 2)[:, a, :], kdn[rows, c // 2, a * P:(a + 1) * P],
                                    gv[rows, c // 2, a * 256:(a + 1) * 256], start=True, stop=True)
                ins.then_inc(kv_mm, 1)
            by_token(3, 0)
            pe.wait_ge(att_ready, 1)
            pe.wait_ge(state_ready, 3)
            for tt in range(TT):
                b = 4 if tt == 0 else 7
                for h in range(GH):
                    t_.matmul(bank(b, 4)[:, h, :], attm[:, 4 * (h % 2) + 2 * tt + h // 2, :],
                              gv[:, tt, h * GV:(h + 1) * GV], start=(h == 0), stop=False, skip_group_check=True)
                for c in range(max(1, 2 * tt), 2 * tt + 2):
                    rows = slice(CH * (c % 2), CH * (c % 2) + CH)
                    for a in range(2):
                        ins = t_.matmul(bank(b, 2)[rows, a, :], gqk[:, a, c * CH:(c + 1) * CH], sbd[:, c - 1, a, :],
                                        start=False, stop=True, skip_group_check=True)
                ins.then_inc(o_mm, 1)
            by_token(3, 1)
            by_token(4, 0)
            pe.wait_ge(ygla_ready, 2)
            for m in range(2):
                for h in range(2):
                    for tt in range(TT):
                        ins = t_.transpose(bank(5 + m, 2)[:, h, tt * P:(tt + 1) * P],
                                           gr[:, tt, (2 * m + h) * GV:(2 * m + h + 1) * GV], ident[:, :])
                ins.then_inc(yg_turned, 1)
            by_token(4, 1)
            by_token(5, 0)
            by_token(5, 1)
            pe.wait_ge(ygT_ready, 2)
            pe.wait_ge(qkn_ready, 2)
            for w in range(2):
                for m in range(2):
                    for j in range(2):
                        for tt in range(TT):
                            ins = t_.transpose(bank(4 + 2 * w + m, 2)[:, j, tt * P:(tt + 1) * P],
                                               aqk[:, w, tt, (2 * m + j) * P:(2 * m + j + 1) * P], ident[:, :])
                    ins.then_inc(qk_turned, 1)

            def scores(h):
                b = 4 + h % 2
                if h == 0:
                    pe.wait_ge(kT_ready, 2)
                    pe.wait_ge(qT_ready, 4)
                if h >= 2:
                    pe.wait_ge(exp_ready, 2 * (h - 1))
                pe.wait_ge(bias_in[h % 4], 16 * (h // 4 + 1))
                for tt in range(TT):
                    o = ps[:, b, P * tt:P + 2 * P * tt]
                    keys = slice(0, P * (tt + 1))
                    t_.matmul(o, antid[:, :], bias_h[:, h % 4, P * (1 - tt):T], start=True, stop=False)
                    ins = t_.matmul(o, qTz[:, h, tt * P:(tt + 1) * P], kT[:, h // 2, keys], start=False, stop=True)
                ins.then_inc(score_mm, 1)

            def turn_prob(h):
                pe.wait_ge(prob_ready, h + 1)
                if h >= 1:
                    pe.wait_ge(probT_ready, h)
                for j in range(3):
                    ins = t_.transpose(bank(6, 4)[:, j, :], prob[:, h % 2, j * P:(j + 1) * P], ident[:, :])
                ins.then_inc(prob_turned, 1)

            def prob_v(h):
                pe.wait_ge(probT_ready, h + 1)
                if h >= 2:
                    pe.wait_ge(yaT_ready, h // 2)
                rows = slice(DH * (h % 2), DH * (h % 2) + DH)
                o = bank(7, 2)[rows, (h // 2) % 2, :]
                t_.matmul(o, av[:, 0, h * DH:(h + 1) * DH], probT[:, h % 2, 0:T], start=True, stop=False)
                t_.matmul(o[:, P:T], av[:, 1, h * DH:(h + 1) * DH], probT[:, h % 2, T:T + P],
                          start=False, stop=True).then_inc(pv_mm, 1)

            dense = [lambda g=g, m=m: feat(g, m) for g in (6, 7, 8, 9, 10) for m in range(2)]
            pe.wait_ge(evacuated[bank_of(5, 0)[0]], bank_of(5, 0)[1] + 1)
            pe.wait_ge(evacuated[bank_of(5, 1)[0]], bank_of(5, 1)[1] + 1)
            for u in range(NH + 2):
                dense[u]()
                if u < NH:
                    scores(u)
                if 1 <= u <= NH:
                    turn_prob(u - 1)
                if u >= 2:
                    prob_v(u - 2)

            def branch(n, yT):
                g = 11 + 3 * n
                for m in range(4):
                    by_feature(g, m, w4(g % RING), 2 * m, yT, KC)

            pe.wait_ge(evacuated[bank_of(8, 0)[0]], bank_of(8, 0)[1] + 1)
            pe.wait_ge(evacuated[bank_of(8, 1)[0]], bank_of(8, 1)[1] + 1)
            branch(0, ycT)
            for n in range(1, 3):
                for half in range(2):
                    for m in range(2):
                        feat(9 + 3 * n + half, m)
                if n == 1:
                    pe.wait_ge(yaT_ready, 4)
                branch(n, (None, yaT, ygT)[n])
            pe.wait_ge(branch_done, 12)
            for half in range(2):
                for tt in range(TT):
                    g = 18 + half
                    b = begin(g, tt)
                    for k in range(KD):
                        ins = t_.matmul(bank(b), mergedT[:, k, tt * P:(tt + 1) * P], w3(g % RING)[:, k, :],
                                        start=(k == 0), stop=(k == KD - 1))
                    ins.then_inc(proj_done, 1)

            turn_x(xn, h2_ready, h2_turned)
            pe.wait_ge(hT_act, 8)
            pe.wait_ge(hT_dve, 8)
            for tt in range(TT):
                o = ps[:, 0, tt * 36:(tt + 1) * 36]
                t_.matmul(o, ones_row[:, :], b_r[:, :], start=True, stop=False)
                for k in range(KD):
                    ins = t_.matmul(o, hT[:, k, tt * P:(tt + 1) * P], w_r[:, k, :], start=False, stop=(k == KD - 1))
            ins.then_inc(router_mm, 1)
            pe.wait_ge(assign_ready, 2)
            for tt in range(TT):
                o = ps[:, 1, tt * NE:(tt + 1) * NE]
                t_.matmul(o, tri_bf[:, :], eall_bf[:, tt, :], start=True, stop=False)
                if tt:
                    t_.matmul(o, ones_bf[:, :], eall_bf[:, 0, :], start=False, stop=False)
                t_.matmul(o, ones_bf[:, :], epre_bf[:, 0, :], start=False, stop=False)
                t_.matmul(o, ones_bf[:, :], epre_bf[:, 1, :], start=False, stop=True)
            for j, src in enumerate((epre_bf, eall_bf)):
                o = ps[:, 1, (2 + j) * NE:(3 + j) * NE]
                t_.matmul(o, ones_bf[:, :], src[:, 0, :], start=True, stop=False)
                ins = t_.matmul(o, ones_bf[:, :], src[:, 1, :], start=False, stop=True)
            ins.then_inc(pos_mm, 1)
            pe.wait_ge(perm_ready, 2)
            for k in range(KD):
                if k >= 4:
                    pe.wait_ge((xs_act, xs_dve)[k % 2], (k - 4) // 2 + 1)
                for tt in range(TT):
                    ins = t_.matmul(bank(2 + k % 4), xn[:, tt, k::KD], perm[:, tt, :], start=(tt == 0), stop=(tt == 1))
                ins.then_inc(gather_mm, 1)
            pe.wait_ge(route_ready, 1)
            pe.sem_inc(freed, FREED_SEED)
            passes = pe.value_load(npass[0:1, 0:1], min_val=1, max_val=MAXWIN)

            def products(p, i, q, lhs, out_of, tile_of):
                for c in range(CHUNKS):
                    n = PER_PASS * CHUNKS * p + RING * CHUNKS * i + CHUNKS * q + c
                    pe.wait_ge(hi_ready, n + 1)
                    if c in POOL_LO:
                        pe.wait_ge(lo_ready_pool, PER_PASS * len(POOL_LO) * p + RING * len(POOL_LO) * i
                                   + len(POOL_LO) * q + POOL_LO.index(c) + 1)
                    else:
                        nd = CHUNKS - len(POOL_LO)
                        pe.wait_ge(lo_ready, PER_PASS * nd * p + RING * nd * i + nd * q + c + 1)
                    for j in range(CHUNK_T):
                        k, o, first, last = tile_of(CHUNK_T * c + j)
                        t_.matmul(out_of(o), lhs[:, k, :], w_hi[c][:, j, :], start=first, stop=False)
                        ins = t_.matmul(out_of(o), lhs[:, k, :], w_lo[c][:, j, :], start=False, stop=last)
                    ins.then_inc(freed, 1)

            def gate_up(p, i, q, b, up):
                products(p, i, q, xe[b], lambda o: ps[:, 2 * b + up, :], lambda k: (k, 0, k == 0, k == KD - 1))

            def down(p, i, q):
                products(p, i, q, he, lambda o: ps[:, 4 + o, :],
                         lambda n: (n // 2, n % 2, n // 2 == 0, n // 2 == KC - 1))

            def start_gate(p, e):
                pe.wait_ge(xe_ready, 2 * (NE + 1) * p + 2 * e + 2)
                pe.wait_ge(gu_free, 2 * NE * p + 2 * e + 2)

            def turn_h(p, e):
                pe.wait_ge(h_ready, NE * p + e + 1)
                for j in range(KC):
                    ins = t_.matmul(ps[:, 6, j * WIN:(j + 1) * WIN], h_tok[:, j * P:(j + 1) * P],
                                    ident[0:WIN, 0:WIN], start=True, stop=True)
                ins.then_inc(h_turned, 1)

            def start_down(p, e):
                pe.wait_ge(he_hi, NE * p + e + 1)
                pe.wait_ge(he_lo, NE * p + e + 1)
                pe.wait_ge(y_ready, NE * p + e + 1)

            def step(p, e, i, q, b):
                start_gate(p, e)
                gate_up(p, i, q, b, 0)
                turn_h(p, e - 1)
                gate_up(p, i, q + 1, b, 1)
                start_down(p, e - 1)
                down(p, i, q + 2)

            with pe.Fori(0, passes) as p:
                start_gate(p, 0)
                gate_up(p, 0, 0, 0, 0)
                gate_up(p, 0, 1, 0, 1)
                step(p, 1, 0, 2, 1)
                with pe.Fori(0, NE // 2 - 1) as i:
                    for s in range(2):
                        step(p, 2 * i + (2 + s), i, 5 + 3 * s, s)
                turn_h(p, NE - 1)
                start_down(p, NE - 1)
                down(p, 0, PER_PASS - 1)

        @block.vector
        def _(dve):
            v = nc.vector
            steps = [0]

            def link(ins):
                steps[0] += 1
                ins.then_inc(v_chain, 1)
                dve.wait_ge(v_chain, steps[0])

            def norm_stats(src, dst, signal):
                for tt in range(TT):
                    if src is x_tok and signal is ms_ready:
                        dve.wait_ge(x_in[tt], 16)
                    link(v.tensor_tensor_reduce(dst[:, tt, :], src[:, tt, :], src[:, tt, :], 1.0, 0.0, ALU.mult,
                                                ALU.add, stat[:, tt:tt + 1]))
                    v.tensor_scalar(stat[:, tt:tt + 1], stat[:, tt:tt + 1], 1.0 / D, EPS, ALU.mult,
                                    ALU.add).then_inc(signal, 1)

            def norm_apply(src, dst, rms, signal):
                dve.wait_ge(rms, 1)
                link(v.reciprocal(stat[:, 4:6], stat[:, 2:4]))
                for tt in range(TT):
                    v.tensor_scalar(dst[:, tt, :], src[:, tt, :], stat[:, 4 + tt:5 + tt], None,
                                    ALU.mult).then_inc(signal, 1)

            def turned_out(turned, gain):
                for kp in range(2, 4):
                    dve.wait_ge(turned, kp + 1)
                    for k in range(2):
                        c = 2 * kp + k
                        v.tensor_scalar(hT[:, c, :], bank(4 + kp, 2)[:, k, :], gain[:, c:c + 1], None,
                                        ALU.mult).then_inc(hT_dve, 1)

            norm_stats(x_tok, xn, ms_ready)
            norm_apply(x_tok, xn, rms_ready, xn_ready)
            dve.wait_ge(consts, 6)
            dve.wait_ge(biasrow_mm, 1)
            v.tensor_copy(bias_row[:, 0:T], ps[0:NH, 3, 0:T]).then_inc(biasrow_ready, 1)
            dve.wait_ge(early_in, 16 * N_EARLY)
            turned_out(hT_turned, g_mix)
            dve.wait_ge(small_in, 16 * N_SMALL)

            dve.wait_ge(alpha_mm, 1)
            for a in range(2):
                v.tensor_scalar(e_neg[:, a, :], bank(5, 2)[:, a, :], b_al[:, a:a + 1], 0.0, ALU.add,
                                ALU.min).then_inc(sigmin_ready, 1)
            dve.wait_ge(sigmin_ready, 2)
            dve.wait_ge(softplus_ready, 1)
            link(v.tensor_tensor(e_rest, e_neg, e_pos, ALU.subtract))
            for a in range(2):
                v.tensor_tensor_scan(la[:, a, :], reset[:, :], e_rest[:, a, :], 0.0, ALU.mult,
                                     ALU.add).then_inc(cum_ready, 1)
            dve.wait_ge(cum_ready, 2)
            for a in range(2):
                run = la[:, a, :].rearrange("p (c n) -> p c n", n=CH)
                ins = v.tensor_tensor(e_rest[:, a, :].rearrange("p (c n) -> p c n", n=CH),
                                      run[:, :, CH - 1:CH].broadcast_to([P, T // CH, CH]), run, ALU.subtract)
                if a == 0:
                    link(ins)
            ins.then_inc(cum_ready, 1)
            dve.wait_ge(evacuated[bank_of(0, 1)[0]], 1)
            dve.wait_ge(decay_ready, 1)
            v.tensor_tensor(e_rest, gqk[:, 2:4, :], e_rest, ALU.mult).then_inc(gla_in_ready, 1)
            dve.wait_ge(decay_ready, 2)
            v.tensor_tensor(gqk[:, 0:2, :], gqk[:, 0:2, :], e_pos, ALU.mult).then_inc(gla_in_ready, 1)
            dve.wait_ge(decay_ready, 3)
            v.tensor_tensor(gqk[:, 2:4, :], gqk[:, 2:4, :], e_neg, ALU.mult).then_inc(gla_in_ready, 1)
            for par in range(2):
                dve.wait_ge(att_mm, par + 1)
                v.tensor_copy(attm[:, 4 * par:4 * par + 4, :], bank(4 + 3 * par, 4)).then_inc(att_copied, 1)
            dve.wait_ge(sbd_zero, 1)
            for c in range(3):
                dve.wait_ge(kv_mm, c + 1)
                kv = bank((5, 6, 4)[c], 2)
                if c:
                    dve.wait_ge(state_ready, c)
                for h in range(2):
                    rows = slice(GK * h, GK * h + GK)
                    blk = slice(GV * h, GV * h + GV)
                    if c == 0:
                        ins = v.tensor_copy(sbd[rows, 0, :, blk], kv[rows, :, blk])
                    else:
                        for a in range(2):
                            ins = v.scalar_tensor_tensor(out=sbd[rows, c, a, blk], in0=sbd[rows, c - 1, a, blk],
                                                         scalar=e_pos[rows, a, CH * c + CH - 1:CH * c + CH],
                                                         in1=kv[rows, a, blk], op0=ALU.mult, op1=ALU.add)
                ins.then_inc(state_ready, 1)

            def take(g, m, w, tt):
                b, _ = bank_of(g, m)
                dve.wait_ge(proj_done, first_bank[g] + m + 1)
                v.tensor_copy(aqk[:, w, tt, :], bank(b)).then_inc(evacuated[b], 1)

            take(3, 0, 0, 0)
            for tt in range(TT):
                dve.wait_ge(o_sq, tt + 1)
                link(v.tensor_reduce(stat[:, 8 + 4 * tt:12 + 4 * tt], scr[:, tt, :].rearrange("p (h n) -> p h n", n=GV),
                                     AX_X, ALU.add))
            v.tensor_scalar(stat[:, 8:16], stat[:, 8:16], 1.0 / GV, EPS, ALU.mult, ALU.add).then_inc(o_ms, 1)
            take(3, 1, 0, 1)
            dve.wait_ge(o_rms, 1)
            link(v.reciprocal(stat[:, 24:32], stat[:, 16:24]))
            for tt in range(TT):
                o3 = scr[:, tt, :].rearrange("p (h n) -> p h n", n=GV)
                link(v.tensor_tensor(o3, bank(4 if tt == 0 else 7, 4),
                                     stat[:, 24 + 4 * tt:28 + 4 * tt].unsqueeze(2).broadcast_to([P, GH, GV]), ALU.mult))
                dve.wait_ge(evacuated[bank_of(2, tt)[0]], bank_of(2, tt)[1] + 1)
                v.tensor_tensor(gr[:, tt, :], scr[:, tt, :], gr[:, tt, :], ALU.mult).then_inc(ygla_ready, 1)
            take(4, 0, 1, 0)
            take(4, 1, 1, 1)
            for w in range(2):
                if w == 1:
                    dve.wait_ge(evacuated[bank_of(4, 0)[0]], bank_of(4, 0)[1] + 1)
                    dve.wait_ge(evacuated[bank_of(4, 1)[0]], bank_of(4, 1)[1] + 1)
                else:
                    dve.wait_ge(evacuated[bank_of(3, 0)[0]], bank_of(3, 0)[1] + 1)
                    dve.wait_ge(evacuated[bank_of(3, 1)[0]], bank_of(3, 1)[1] + 1)
                link(v.tensor_tensor(flat(scr[:, :, :]), flat(aqk[:, w, :, :]), flat(aqk[:, w, :, :]), ALU.mult))
                link(v.tensor_reduce(qkm[:, w, :, :], scr[:, :, :].rearrange("p t (h n) -> p t h n", n=DH),
                                     AX_X, ALU.add))
            v.tensor_scalar(qkm[:, :, :, :], qkm[:, :, :, :], 1.0 / DH, EPS, ALU.mult, ALU.add).then_inc(qk_ms, 1)
            dve.wait_ge(qk_rms, 1)
            link(v.reciprocal(qkm[:, :, :, :], qkr[:, :, :, :]))
            for w in range(2):
                for tt in range(TT):
                    a3 = aqk[:, w, tt, :].rearrange("p (h n) -> p h n", n=DH)
                    ins = v.tensor_tensor(a3, a3, qkm[:, w, tt, :].unsqueeze(2).broadcast_to([P, NH, DH]), ALU.mult)
                ins.then_inc(qkn_ready, 1)
            link(v.tensor_scalar(qn_w[:, :], qn_w[:, :], float(DH) ** -0.5, None, ALU.mult))
            dve.wait_ge(qz_zero, 2)
            qz = qTz[:, :, :].rearrange("p (b two) t -> p b two t", two=2)
            for m in range(2):
                dve.wait_ge(qk_turned, m + 1)
                for h in range(2):
                    rows = slice(DH * h, DH * h + DH)
                    v.tensor_scalar(qz[rows, 2 * m:2 * m + 2, h, :], bank(4 + m, 2)[rows, :, :], qn_w[rows, 0:1], None,
                                    ALU.mult).then_inc(qT_ready, 1)

            def row_max(h):
                dve.wait_ge(score_mm, h + 1)
                for tt in range(TT):
                    ins = v.tensor_reduce(nmx[:, h, tt:tt + 1], ps[:, 4 + h % 2, P * tt:P + 2 * P * tt], AX_X, ALU.max,
                                          negate=True)
                ins.then_inc(rowmax_ready, 1)

            def prob_scale(h):
                dve.wait_ge(exp_ready, 2 * h + 2)
                link(v.reciprocal(rsum[:, h, :], rsum[:, h, :]))
                for tt in range(TT):
                    pr = prob[:, h % 2, P * tt:P + 2 * P * tt]
                    ins = v.tensor_scalar(pr, pr, rsum[:, h, tt:tt + 1], None, ALU.mult)
                ins.then_inc(prob_ready, 1)

            def pair_out(b):
                dve.wait_ge(pv_mm, 2 * b + 2)
                v.tensor_copy(yaT[:, b, :], bank(7, 2)[:, b % 2, :]).then_inc(yaT_ready, 1)

            def conv_in(m):
                b, _ = bank_of(7, m)
                dve.wait_ge(proj_done, first_bank[7] + m + 1)
                cb, cu = bank_of(6, m)
                dve.wait_ge(evacuated[cb], cu + 1)
                v.tensor_tensor(conv_u[:, 2 * m:2 * m + 2, 2:T + 2], ycT[:, 2 * m:2 * m + 2, :], bank(b, 2),
                                ALU.mult).then_inc(evacuated[b], 1)

            def conv_taps(m):
                b, u = bank_of(7, m)
                dve.wait_ge(evacuated[b], u + 1)
                for k in (2 * m, 2 * m + 1):
                    link(v.tensor_scalar(ycT[:, k, :], conv_u[:, k, 0:T], cw_sb[:, 0, k:k + 1], cb_sb[:, k:k + 1],
                                         ALU.mult, ALU.add))
                    for j in (1, 2):
                        link(v.scalar_tensor_tensor(out=ycT[:, k, :], in0=conv_u[:, k, j:j + T],
                                                    scalar=cw_sb[:, j, k:k + 1], in1=ycT[:, k, :], op0=ALU.mult,
                                                    op1=ALU.add))

            def conv_out(m):
                b, _ = bank_of(8, m)
                dve.wait_ge(proj_done, first_bank[8] + m + 1)
                v.tensor_tensor(ycT[:, 2 * m:2 * m + 2, :], ycT[:, 2 * m:2 * m + 2, :], bank(b, 2), ALU.mult
                                ).then_inc(evacuated[b], 1)

            row_max(0)
            for h in range(1, NH):
                if h in (2, 3):
                    conv_in(h - 2)
                if h in (4, 5):
                    conv_out(h - 4)
                if h >= 4 and h % 2 == 0:
                    pair_out(h // 2 - 2)
                row_max(h)
                prob_scale(h - 1)
                if h in (2, 3):
                    conv_taps(h - 2)
            prob_scale(NH - 1)
            pair_out(2)
            pair_out(3)

            for n in range(3):
                for m in range(4):
                    r = first_bank[11 + 3 * n] + m
                    sb, su = bank_of(9 + 3 * n + m // 2, m % 2)
                    dve.wait_ge(evacuated[sb], su + 1)
                    dve.wait_ge(proj_done, r + 1)
                    dst = flat(mergedT[:, 2 * m:2 * m + 2, :])
                    gate = flat(sig[:, n % 2, 2 * m:2 * m + 2, :])
                    if n == 0:
                        v.tensor_tensor(dst, gate, bank(r % 4), ALU.mult).then_inc(evacuated[r % 4], 1)
                        dve.wait_ge(evacuated[r % 4], r // 4 + 1)
                        v.engine_nop().then_inc(branch_done, 1)
                    else:
                        v.tensor_tensor(scr[:, m % 2, :], gate, bank(r % 4), ALU.mult).then_inc(evacuated[r % 4], 1)
                        dve.wait_ge(evacuated[r % 4], r // 4 + 1)
                        v.tensor_tensor(dst, dst, scr[:, m % 2, :], ALU.add).then_inc(branch_done, 1)
            for half in range(2):
                for tt in range(TT):
                    r = first_bank[18 + half] + tt
                    dve.wait_ge(proj_done, r + 1)
                    xv = x_tok[:, tt, half * C:(half + 1) * C]
                    v.tensor_tensor(xv, xv, bank(r % 4), ALU.add).then_inc(x1_ready, 1)
            dve.wait_ge(x1_ready, 4)
            norm_stats(x_tok, xn, ms2_ready)
            norm_apply(x_tok, xn, rms2_ready, h2_ready)
            turned_out(h2_turned, g_ffn)

            dve.wait_ge(router_mm, 1)
            lg = ps[:, 0, 0:72].rearrange("p (t n) -> p t n", t=TT)
            v.tensor_copy(lgp[:, :, 0:NG], lg[:, :, 0:NG])
            link(v.tensor_copy(le[:, :, :], lg[:, :, NG:NG + NE]))
            for tt in range(TT):
                link(v.max(mg8[:, tt, :], lgp[:, tt, :]))
                link(v.max_index(ig8[:, tt, :], mg8[:, tt, :], lgp[:, tt, :]))
            v.tensor_scalar(rt[:, :, 0:1], mg8[:, :, 0:1], -1.0, None, ALU.mult).then_inc(nmax_ready, 1)
            link(v.tensor_copy(rt[:, :, 4:5], ig8[:, :, 0:1]))
            for tt in range(TT):
                link(v.tensor_scalar(rt[:, tt, 12:16], iota_f[:, 0:NG], rt[:, tt, 4:5], None, ALU.is_equal))
                link(v.tensor_tensor(lsel[:, tt, :].rearrange("p (g e) -> p g e", e=EPG),
                                     le[:, tt, :].rearrange("p (g e) -> p g e", e=EPG),
                                     rt[:, tt, 12:16].unsqueeze(2).broadcast_to([P, NG, EPG]), ALU.mult))
                link(v.tensor_reduce(les[:, tt, :], lsel[:, tt, :].rearrange("p (g e) -> p e g", e=EPG), AX_X, ALU.add))
                link(v.max(me8[:, tt, :], les[:, tt, :]))
                link(v.max_index(ie8[:, tt, :], me8[:, tt, :], les[:, tt, :]))
            v.tensor_tensor(rt[:, :, 2:3], me8[:, :, 1:2], me8[:, :, 0:1], ALU.subtract).then_inc(e2in_ready, 1)
            link(v.tensor_copy(rt[:, :, 5:7], ie8[:, :, 0:2]))
            link(v.scalar_tensor_tensor(out=rt[:, :, 5:7], in0=rt[:, :, 4:5].broadcast_to([P, TT, 2]), scalar=float(EPG),
                                        in1=rt[:, :, 5:7], op0=ALU.mult, op1=ALU.add))
            for tt in range(TT):
                v.tensor_scalar(e1h[:, tt, :], iota_f[:, :], rt[:, tt, 5:6], None, ALU.is_equal)
                link(v.tensor_scalar(e2h[:, tt, :], iota_f[:, :], rt[:, tt, 6:7], None, ALU.is_equal))
            link(v.tensor_tensor(eall[:, :, :], e1h[:, :, :], e2h[:, :, :], ALU.add))
            v.tensor_copy(eall_bf[:, :, :], eall[:, :, :]).then_inc(assign_ready, 1)
            for tt in range(TT):
                link(v.tensor_tensor_scan(epre[:, tt, :], reset[:, 1:1 + NE], eall[:, tt, :], 0.0, ALU.mult, ALU.add))
            v.tensor_tensor(epre_bf[:, :, :], epre[:, :, :], eall[:, :, :], ALU.subtract).then_inc(assign_ready, 1)
            dve.wait_ge(pos_mm, 1)
            for tt in range(TT):
                for k, eh in enumerate((e1h, e2h)):
                    link(v.tensor_tensor_reduce(eh[:, tt, :], eh[:, tt, :], ps[:, 1, tt * NE:(tt + 1) * NE], 1.0, 0.0,
                                                ALU.mult, ALU.add, slotf[:, tt, k:k + 1]))
            dve.wait_ge(iota_ready, 1)
            for tt in range(TT):
                link(v.tensor_scalar(perm[:, tt, :], iota_s[:, :], slotf[:, tt, 0:1], None, ALU.is_equal))
                v.scalar_tensor_tensor(out=perm[:, tt, :], in0=iota_s[:, :], scalar=slotf[:, tt, 1:2],
                                       in1=perm[:, tt, :], op0=ALU.is_equal, op1=ALU.add).then_inc(perm_ready, 1)
            link(v.tensor_reduce(cntr[:, 0:1], ps[0:1, 1, 3 * NE:4 * NE], AX_X, ALU.max))
            link(v.tensor_scalar(cntr[:, 1:2], cntr[:, 0:1], float(WIN), 1.0, ALU.is_gt, ALU.add))
            for r in range(2, MAXWIN):
                link(v.scalar_tensor_tensor(out=cntr[:, r:r + 1], in0=cntr[:, 0:1], scalar=float(WIN * r),
                                            in1=cntr[:, r - 1:r], op0=ALU.is_gt, op1=ALU.add))
            for p in range(MAXWIN):
                link(v.tensor_scalar(cntr[:, 4 + p:5 + p], cntr[:, MAXWIN - 1:MAXWIN], float(WIN), -float(WIN * (p + 1)),
                                     ALU.mult, ALU.add))
                link(v.tensor_scalar(cntr[:, 4 + p:5 + p], cntr[:, 4 + p:5 + p], 0.0, None, ALU.max))
                link(v.tensor_scalar(offf[:, p * NE:(p + 1) * NE], ps[0:1, 1, 2 * NE:3 * NE], cntr[:, 4 + p:5 + p],
                                     float(SLOTS), ALU.add, ALU.min))
            link(v.tensor_copy(off_tab[:, :], offf[:, :]))
            v.tensor_copy(npass[:, :], cntr[:, MAXWIN - 1:MAXWIN]).then_inc(route_ready, 1)
            link(v.tensor_copy(slot_u[:, :], flat(slotf[:, :, :])))
            for k in range(1, KD, 2):
                dve.wait_ge(gather_mm, k + 1)
                v.tensor_scalar(xs[:, k, 0:SLOTS], bank(2 + k % 4), g_ffn[:, k:k + 1], None, ALU.mult).then_inc(xs_dve, 1)
            dve.wait_ge(gexp_ready, 2)
            dve.wait_ge(e2_ready, 1)
            link(v.tensor_scalar(rt[:, :, 7:8], rt[:, :, 3:4], 1.0, None, ALU.add))
            link(v.tensor_tensor(rt[:, :, 7:8], rt[:, :, 7:8], rt[:, :, 1:2], ALU.mult))
            link(v.reciprocal(wts[:, :, 0:1], rt[:, :, 7:8]))
            link(v.tensor_tensor(wts[:, :, 1:2], wts[:, :, 0:1], rt[:, :, 3:4], ALU.mult))

            passes = dve.value_load(npass[0:1, 0:1], min_val=1, max_val=MAXWIN)
            dve.wait_ge(route_ready, 1)
            dve.sem_inc(gu_free, 4)
            dve.sem_inc(y_ready, 1)

            def low_part(p, i, q, cs):
                s = slot_of(q)
                for c in cs:
                    if c in POOL_LO:
                        continue
                    dve.wait_ge(hi_ready, PER_PASS * CHUNKS * p + RING * CHUNKS * i + CHUNKS * q + c + 1)
                    v.tensor_tensor(w_lo[c][:, :, :], w3(s)[:, CHUNK_T * c:CHUNK_T * (c + 1), :],
                                    w_hi[c][:, :, :].bitcast(F32), ALU.subtract).then_inc(lo_ready, 1)

            def gu_fold(p, e, b):
                dve.wait_ge(gu_lo_out, 2 * NE * p + 2 * e + 1)
                v.tensor_tensor(g_sum[:, :], g_lo[:, :], ps[0:WIN, 2 * b, :], ALU.add).then_inc(gu_free, 1)
                dve.wait_ge(gu_lo_out, 2 * NE * p + 2 * e + 2)
                v.tensor_tensor(u_sum[:, :], u_lo[:, :], ps[0:WIN, 2 * b + 1, :], ALU.add).then_inc(gu_free, 1)

            def gated(p, e):
                dve.wait_ge(silu_ready, NE * p + e + 1)
                dve.wait_ge(gu_free, 2 * NE * p + 2 * e + 6)
                v.tensor_tensor(h_tok[:, :], g_act[:, :], u_sum[:, :], ALU.mult).then_inc(h_ready, 1)

            def he_low(p, e):
                dve.wait_ge(he_hi, NE * p + e + 1)
                v.tensor_tensor(he[:, :, WIN:2 * WIN], ps[:, 6, 0:KC * WIN].rearrange("p (k n) -> p k n", n=WIN),
                                he[:, :, 0:WIN].bitcast(F32), ALU.subtract).then_inc(he_lo, 1)

            def y_fold(p, e, b):
                dve.wait_ge(y_lo_out, NE * p + e + 1)
                dve.wait_ge(y_free, NE * p + e + 1)
                v.tensor_tensor(y_tok[:, b, :], y_lo[:, :], flat(ps[0:WIN, 4:6, :]), ALU.add).then_inc(y_ready, 1)

            def step(p, e, i, q, b, y_too):
                low_part(p, i, q, (0,))
                gu_fold(p, e - 1, 1 - b)
                low_part(p, i, q, (1,))
                gated(p, e - 1)
                low_part(p, i, q, (2,))
                if y_too:
                    y_fold(p, e - 2, b)
                low_part(p, i, q, (3,))
                low_part(p, i, q + 1, (0, 1, 2, 3))
                he_low(p, e - 1)
                low_part(p, i, q + 2, (0, 1, 2, 3))

            with dve.Fori(0, passes) as p:
                low_part(p, 0, 0, (0, 1, 2, 3))
                low_part(p, 0, 1, (0, 1, 2, 3))
                step(p, 1, 0, 2, 1, False)
                with dve.Fori(0, NE // 2 - 1) as i:
                    for s in range(2):
                        step(p, 2 * i + (2 + s), i, 5 + 3 * s, s, True)
                gu_fold(p, NE - 1, 1)
                gated(p, NE - 1)
                low_part(p, 0, PER_PASS - 1, (0,))
                y_fold(p, NE - 2, 0)
                he_low(p, NE - 1)
                low_part(p, 0, PER_PASS - 1, (1, 2, 3))
                y_fold(p, NE - 1, 1)
            for tt in range(TT):
                for k in range(2):
                    j = 2 * tt + k
                    dve.wait_ge(back_in[j], 16)
                    ins = v.scalar_tensor_tensor(out=x_tok[:, tt, :], in0=y_back[:, j, :], scalar=wts[:, tt, k:k + 1],
                                                 in1=x_tok[:, tt, :], op0=ALU.mult, op1=ALU.add)
                    if k == 0:
                        link(ins)
                ins.then_inc(fin_ready, 1)


_INS = ['x', 'rel_bias_table', 'norm_mix', 'w_in', 'conv_w', 'conv_b', 'q_norm', 'k_norm', 'w_gla_alpha',
        'b_gla_alpha', 'gla_out_norm', 'w_merge_gate', 'w_branch', 'w_out', 'norm_ffn', 'w_router_group',
        'b_router_group', 'w_router_expert', 'b_router_expert', 'w_expert_gate', 'w_expert_up', 'w_expert_down']


def kernel(**inputs):
    import concourse.bacc as _bacc
    from concourse.bass_utils import run_bass_kernel_spmd as _run

    nc = _bacc.Bacc("TRN2", target_bir_lowering=False, num_devices=1)
    arrays, args = {}, []
    for name in _INS:
        a = np.ascontiguousarray(inputs[name])
        arrays[f"in_{name}"] = a
        args.append(nc.dram_tensor(f"in_{name}", a.shape, mybir.dt.from_np(a.dtype), kind="ExternalInput").ap())
    out = nc.dram_tensor("out_x", (1, T, D), F32, kind="ExternalOutput").ap()
    hybrid_block(nc, *args, out)
    r = _run(nc, [arrays], core_ids=[0])
    return r.results[0]["out_x"]
```

```python
import math
from contextlib import ExitStack

import numpy as np

import concourse.bass as bass
from concourse import mybir

F32 = mybir.dt.float32
F32R = mybir.dt.float32r
BF16 = mybir.dt.bfloat16
I32 = mybir.dt.int32
U32 = mybir.dt.uint32
ALU = mybir.AluOpType
ACT = mybir.ActivationFunctionType
AX_X = mybir.AxisListType.X

P = 128
T = 256
TT = T // P
D = 1024
KD = D // P
C = 512
KC = C // P
EPS = 1e-6
NH = 8
DH = 64
GH = 4
GK = 64
GV = 128
CH = 64
TEMP = 16.0
NG = 4
EPG = 8
NE = NG * EPG
TOPK = 2
SLOTS = T * TOPK
WIN = 64
MAXWIN = T // WIN
SPAD = SLOTS + WIN
BUCKETS = 32
MAXDIST = 128
NEG = -1e30

PRE_RING = 5
RING = 6
SLOT = KD * C
NPRE = 20
PER_PASS = 3 * NE
N_EARLY = 3
N_SMALL = 16
CHUNK_T = 2
CHUNKS = KD // CHUNK_T
CW = CHUNK_T * C
HI_BUFS = 6
POOL_LO = (3,)
FREED_SEED = RING * CHUNKS


def bucket_onehot():
    n = T - 1 - np.arange(T)
    exact = BUCKETS // 2
    scaled = np.log(np.maximum(n, exact).astype(np.float32) / exact) / math.log(MAXDIST / exact)
    large = np.minimum(exact + (scaled * (BUCKETS - exact)).astype(np.int32), BUCKETS - 1)
    b = np.where(n < exact, n, large)
    return (b[None, :] == np.arange(BUCKETS)[:, None]).astype(np.float32)


def flat(v):
    names = "abcd"[:len(v.shape) - 1]
    return v.rearrange(f"p {' '.join(names)} -> p ({' '.join(names)})")


def hybrid_block(nc, x, rel_bias_table, norm_mix, w_in, conv_w, conv_b, q_norm, k_norm, w_gla_alpha,
                 b_gla_alpha, gla_out_norm, w_merge_gate, w_branch, w_out, norm_ffn, w_router_group,
                 b_router_group, w_router_expert, b_router_expert, w_expert_gate, w_expert_up,
                 w_expert_down, out):
    ctx = ExitStack()
    top = [16512]

    def place(name, shape, dt, at=None):
        size = int(np.prod(shape[1:])) * mybir.dt.size(dt)
        off = top[0] if at is None else at
        if at is None:
            top[0] = off + (size + 31) // 32 * 32
        assert off + size <= 229344, (name, off + size)
        return nc.alloc_sbuf_tensor_at(name, list(shape), dt, offset=off)

    def sem(name):
        return ctx.enter_context(nc.semaphore(name))

    with ctx:
        ctx.enter_context(nc.allow_non_contiguous_dma("small vectors land one element per partition"))
        onehot_dram = nc.inline_tensor(bucket_onehot(), "bucket_onehot").ap()
        bias_dram = nc.dram_tensor("bias_by_distance", (NH, 384), F32, kind="Internal")
        ysorted = nc.dram_tensor("y_sorted", (SPAD, D), F32, kind="Internal").ap()

        ring_at, ring, ring_lo = [], [], []

        def ring_slot(i, at):
            ring_at.append(at)
            ring.append(place(f"ring{i}", [P, SLOT], F32, at=at))
            ring_lo.append(place(f"ring_lo{i}", [P, SLOT], F32R, at=at))

        for i in range(PRE_RING):
            ring_slot(i, top[0])
            top[0] += 4 * SLOT
        w_hi = [place(f"w_hi{c}", [P, CW], F32R) for c in range(CHUNKS)]
        x_tok = place("x_tok", [P, TT, D], F32)
        xn_at = top[0]
        xn = place("xn_merged", [P, TT, D], F32)
        merged_lo = place("merged_lo", [P, KD, T], F32R, at=xn_at)
        ident = place("ident", [P, P], F32)
        antid = place("antid", [P, P], F32)
        ones_bf = place("ones_bf", [P, P], BF16)
        tri_bf = place("tri_bf", [P, P], BF16)
        ones_row = place("ones_row", [1, P], F32)
        mergedT = xn[:, :, :].rearrange("p a b -> p (a b)").rearrange("p (k t) -> p k t", k=KD)
        g_mix = place("g_mix", [P, KD], F32)
        g_ffn = place("g_ffn", [P, KD], F32)
        cw_sb = place("cw_sb", [P, 3, KC], F32)
        cb_sb = place("cb_sb", [P, KC], F32)
        qn_w = place("qn_w", [P, 1], F32)
        kn_w = place("kn_w", [P, 1], F32)
        b_al = place("b_al", [P, 2], F32)
        on_w = place("on_w", [P, 1], F32)
        w_al = place("w_al", [16, 256], F32)
        zT = place("zT", [16, T], F32)
        table = place("table", [BUCKETS, NH], F32)
        w_z_at = top[0]
        w_z = place("w_z", [P, KD, 16], F32)
        w_z_hi = place("w_z_hi", [P, KD, 16], F32R)
        w_z_lo = place("w_z_lo", [P, KD, 16], F32R, at=w_z_at)
        w_r = place("w_r", [P, KD, NG + NE], F32)
        b_r = place("b_r", [1, NG + NE], F32)
        stat = place("stat", [P, 64], F32)
        reset = place("reset", [P, T], F32)
        qkm = place("qkm", [P, 2, TT, NH], F32)
        qkr = place("qkr", [P, 2, TT, NH], F32)
        nmx = place("nmx", [P, NH, TT], F32)
        rsum = place("rsum", [P, NH, TT], F32)
        lgp = place("lgp", [P, TT, 8], F32)
        le = place("le", [P, TT, NE], F32)
        mg8 = place("mg8", [P, TT, 8], F32)
        ig8 = place("ig8", [P, TT, 8], U32)
        me8 = place("me8", [P, TT, 8], F32)
        ie8 = place("ie8", [P, TT, 8], U32)
        rt = place("rt", [P, TT, 16], F32)
        les = place("les", [P, TT, 8], F32)
        lsel = place("lsel", [P, TT, NE], F32)
        e1h = place("e1h", [P, TT, NE], F32)
        e2h = place("e2h", [P, TT, NE], F32)
        eall = place("eall", [P, TT, NE], F32)
        epre = place("epre", [P, TT, NE], F32)
        eall_bf = place("eall_bf", [P, TT, NE], BF16)
        epre_bf = place("epre_bf", [P, TT, NE], BF16)
        iota_f = place("iota_f", [P, NE], F32)
        slotf = place("slotf", [P, TT, 2], F32)
        slot_u = place("slot_u", [P, TT * 2], U32)
        wts = place("wts", [P, TT, 2], F32)
        offf = place("offf", [1, MAXWIN * NE + 1], F32)
        off_tab = place("off_tab", [1, MAXWIN * NE + 1], I32)
        cntr = place("cntr", [1, 8], F32)
        npass = place("npass", [1, 1], I32)
        region = top[0]

        def here(name, shape, dt):
            nonlocal_at = here_at[0]
            here_at[0] += (int(np.prod(shape[1:])) * mybir.dt.size(dt) + 31) // 32 * 32
            return place(name, shape, dt, at=nonlocal_at)

        here_at = [region]
        sig0 = here("sig0", [P, KD, T], F32)
        onehot = place("onehot", [BUCKETS, T], F32, at=region)
        bias_row = place("bias_row", [NH, 384], F32, at=region + 4 * T)
        yc_at = here_at[0]
        ycT = here("ycT", [P, KC, T], F32)
        yc_lo = place("yc_lo", [P, KC, T], F32R, at=yc_at)
        conv_u = here("conv_u", [P, KC, T + 2], F32)
        hT_at = here_at[0]
        hT_hi = here("hT_hi", [P, KD, T], F32R)
        h2T_at = here_at[0]
        hT_lo = here("hT_lo", [P, KD, T], F32R)
        h2T = place("h2T", [P, KD, T], F32, at=h2T_at)
        merged_hi = place("merged_hi", [P, KD, T], F32R, at=hT_at)
        aqk = here("aqk", [P, 2, TT, C], F32)
        q_at = here_at[0]
        qTz = here("qTz", [P, NH, T], F32)
        sig = (sig0, place("sig1", [P, KD, T], F32, at=q_at), sig0)
        kT = here("kT", [P, KC, T], F32)
        av = here("av", [P, TT, C], F32)
        gqk = here("gqk", [P, 4, T], F32)
        att_at = here_at[0]
        attm = here("attm", [P, 8, P], F32)
        gv_at = here_at[0]
        gv = here("gv", [P, TT, C], F32)
        gr_at = here_at[0]
        gr = here("gr", [P, TT, C], F32)
        kdn = here("kdn", [P, TT, 256], F32)
        sbd_at = here_at[0]
        sbd = here("sbd", [P, 3, 2, 256], F32)
        scr_at = here_at[0]
        scr = here("scr", [P, 2, C], F32)
        la, e_pos, e_neg, e_rest = (qTz[:, 2 * i:2 * i + 2, :] for i in range(4))
        bias_h = gqk
        yc_hi = place("yc_hi", [P, KC, T], F32R, at=scr_at)
        ya_hi = place("ya_hi", [P, KC, T], F32R, at=att_at)
        ya_lo = place("ya_lo", [P, KC, T], F32R, at=gr_at)
        yg_hi = place("yg_hi", [P, KC, T], F32R, at=gv_at)
        yg_lo = place("yg_lo", [P, KC, T], F32R, at=sbd_at)
        prob = aqk[:, 0, :, :].rearrange("p a b -> p (a b)")[:, 0:768].rearrange("p (a b) -> p a b", a=2)
        probT = aqk[:, 1, :, :].rearrange("p a b -> p (a b)")[:, 0:768].rearrange("p (a b) -> p a b", a=2)

        here_at = [region]
        ring_slot(PRE_RING, here_at[0])
        here_at[0] += 4 * SLOT
        xs = here("xs", [P, KD, SPAD], F32)
        w_hi += [here(f"w_hi{c}", [P, CW], F32R) for c in range(CHUNKS, HI_BUFS)]
        xe = [here(f"xe{b}", [P, KD, 2 * WIN], F32R) for b in range(2)]
        g_lo = here("g_lo", [WIN, C], F32)
        u_lo = here("u_lo", [WIN, C], F32)
        g_sum = here("g_sum", [WIN, C], F32)
        u_sum = here("u_sum", [WIN, C], F32)
        g_act = here("g_act", [WIN, C], F32)
        h_tok = here("h_tok", [WIN, C], F32)
        he = here("he", [P, KC, 2 * WIN], F32R)
        y_lo_at = here_at[0]
        y_lo = here("y_lo", [WIN, D], F32)
        y_at = here_at[0]
        y_tok = here("y_tok", [WIN, 2, D], F32)
        iota_s = place("iota_s", [P, SLOTS], F32, at=y_lo_at)
        perm = place("perm", [P, TT, SLOTS], F32, at=y_at)
        y_back = place("y_back", [P, TT * 2, D], F32, at=region)

        ps = ctx.enter_context(nc.psum_tensor("ps", [P, 8, 512], F32))

        def bank(b, a=None):
            v = ps[:, b, :]
            return v if a is None else v.rearrange("p (a b) -> p a b", a=a)

        x_in = [sem(f"x_in{i}") for i in range(TT)]
        early_in = sem("early_in")
        small_in = sem("small_in")
        wz_in = sem("wz_in")
        landed = [sem(f"landed{s}") for s in range(RING)]
        consts = sem("consts")
        v_chain = sem("v_chain")
        a_chain = sem("a_chain")
        g_chain = sem("g_chain")
        ms_ready = sem("ms_ready")
        rms_ready = sem("rms_ready")
        xn_ready = sem("xn_ready")
        hT_turned = sem("hT_turned")
        biasrow_mm = sem("biasrow_mm")
        biasrow_ready = sem("biasrow_ready")
        bias_stored = sem("bias_stored")
        bias_in = [sem(f"bias_in{i}") for i in range(4)]
        proj_done = sem("proj_done")
        evacuated = [sem(f"evacuated{b}") for b in range(4)]
        wpre_hi = sem("wpre_hi")
        wpre_lo = sem("wpre_lo")
        chunk_done = sem("chunk_done")
        wz_hi_ready = sem("wz_hi_ready")
        wz_lo_ready = sem("wz_lo_ready")
        hT_lo_ready = sem("hT_lo_ready")
        yg_hi_ready = sem("yg_hi_ready")
        ycT_ready = sem("ycT_ready")
        merged_hi_ready = sem("merged_hi_ready")
        merged_lo_ready = sem("merged_lo_ready")
        hT_act = sem("hT_act")
        hT_dve = sem("hT_dve")
        xs_act = sem("xs_act")
        xs_dve = sem("xs_dve")
        freed = sem("freed")
        y_free = sem("y_free")
        z_mm = sem("z_mm")
        z_ready = sem("z_ready")
        alpha_mm = sem("alpha_mm")
        sigmin_ready = sem("sigmin_ready")
        softplus_ready = sem("softplus_ready")
        cum_ready = sem("cum_ready")
        decay_ready = sem("decay_ready")
        gla_in_ready = sem("gla_in_ready")
        kd_turned = sem("kd_turned")
        kdn_ready = sem("kdn_ready")
        att_mm = sem("att_mm")
        att_copied = sem("att_copied")
        att_ready = sem("att_ready")
        kv_mm = sem("kv_mm")
        state_ready = sem("state_ready")
        sbd_zero = sem("sbd_zero")
        o_mm = sem("o_mm")
        o_sq = sem("o_sq")
        o_ms = sem("o_ms")
        o_rms = sem("o_rms")
        ygla_ready = sem("ygla_ready")
        yg_turned = sem("yg_turned")
        ygT_ready = sem("ygT_ready")
        qk_ms = sem("qk_ms")
        qk_rms = sem("qk_rms")
        qkn_ready = sem("qkn_ready")
        qz_zero = sem("qz_zero")
        qk_turned = sem("qk_turned")
        qT_ready = sem("qT_ready")
        kT_ready = sem("kT_ready")
        score_mm = sem("score_mm")
        rowmax_ready = sem("rowmax_ready")
        exp_ready = sem("exp_ready")
        prob_ready = sem("prob_ready")
        prob_turned = sem("prob_turned")
        probT_ready = sem("probT_ready")
        pv_mm = sem("pv_mm")
        yaT_ready = sem("yaT_ready")
        branch_done = sem("branch_done")
        x1_ready = sem("x1_ready")
        ms2_ready = sem("ms2_ready")
        rms2_ready = sem("rms2_ready")
        h2_ready = sem("h2_ready")
        h2_turned = sem("h2_turned")
        router_mm = sem("router_mm")
        nmax_ready = sem("nmax_ready")
        gexp_ready = sem("gexp_ready")
        e2in_ready = sem("e2in_ready")
        e2_ready = sem("e2_ready")
        assign_ready = sem("assign_ready")
        pos_mm = sem("pos_mm")
        perm_ready = sem("perm_ready")
        route_ready = sem("route_ready")
        gather_mm = sem("gather_mm")
        iota_ready = sem("iota_ready")
        xe_high = sem("xe_high")
        xe_ready = sem("xe_ready")
        hi_ready = sem("hi_ready")
        lo_ready = sem("lo_ready")
        lo_ready_pool = sem("lo_ready_pool")
        gu_lo_out = sem("gu_lo_out")
        gu_free = sem("gu_free")
        silu_ready = sem("silu_ready")
        h_ready = sem("h_ready")
        h_turned = sem("h_turned")
        he_hi = sem("he_hi")
        he_lo = sem("he_lo")
        y_lo_out = sem("y_lo_out")
        y_ready = sem("y_ready")
        y_stored = sem("y_stored")
        back_in = [sem(f"back_in{j}") for j in range(2 * TT)]
        fin_ready = sem("fin_ready")
        stored = sem("stored")

        w_in_v = w_in[0].rearrange("(p k) n -> p k n", k=KD)
        w_out_v = w_out[0].rearrange("(k p) n -> p k n", p=P)
        cols = [3072, 3584, 4096, 1536, 2048, 2560, 512, 1024, 0]
        pre = [("in", c) for c in cols]
        for n in range(3):
            pre += [("gate", n, 0), ("gate", n, 1), ("branch", n)]
        pre += [("out", 0), ("out", 1)]
        first_bank = []
        at = 0
        for s in pre:
            first_bank.append(at)
            at += 4 if s[0] == "branch" else 2
        first_bank.append(at)
        assert len(pre) == NPRE

        def pre_source(g):
            kind = pre[g]
            if kind[0] == "in":
                return w_in_v[:, :, kind[1]:kind[1] + C], C
            if kind[0] == "gate":
                return w_merge_gate[0, kind[1]].rearrange("(p k) n -> p k n", k=KD)[:, :, kind[2] * C:(kind[2] + 1) * C], C
            if kind[0] == "branch":
                return w_branch[0, kind[1]].rearrange("(k p) n -> p k n", p=P), D
            return w_out_v[:, :, kind[1] * C:(kind[1] + 1) * C], C

        wg_v = w_expert_gate[0].rearrange("e (p k) n -> e p (k n)", k=KD)
        wu_v = w_expert_up[0].rearrange("e (p k) n -> e p (k n)", k=KD)
        wd_v = w_expert_down[0].rearrange("e (k p) n -> e p k n", p=P)

        def slot_of(q):
            return q % RING

        def uses_before(q):
            return (NPRE // PRE_RING if q % RING < PRE_RING else 0) + q // RING

        def hi_buf(q, c):
            return w_hi[(CHUNKS * q + c) % HI_BUFS][:, :]

        def after_slots(p, n):
            return PER_PASS * CHUNKS * p + CHUNKS * n + FREED_SEED

        def bank_of(g, m):
            r = first_bank[g] + m
            return r % 4, r // 4

        def w3(s):
            return ring[s][:, :].rearrange("p (k n) -> p k n", n=C)

        def w4(s):
            return ring[s][:, :].rearrange("p (k n) -> p k n", n=D)

        def chunk(c):
            return slice(CW * c, CW * (c + 1))

        block = ctx.enter_context(nc.Block())

        @block.sync
        def _(sp):
            for tt in range(TT):
                sp.dma_start(x_tok[:, tt, :], x[0, tt * P:(tt + 1) * P, :]).then_inc(x_in[tt], 16)

            def load_expert(kind, e, q, p, i, first=False):
                if first and q < PRE_RING:
                    sp.wait_ge(proj_done, first_bank[NPRE + q - PRE_RING + 1])
                elif first:
                    sp.wait_ge(branch_done, 12)
                else:
                    sp.wait_ge(freed, (PER_PASS * CHUNKS) * p + RING * CHUNKS * i + CHUNKS * (q - RING + 1)
                               + FREED_SEED)
                s = slot_of(q)
                if kind == "d":
                    src = wd_v[bass.ds(e, 1), :, :, :].rearrange("e p k n -> (e p) k n")
                    sp.dma_start(w4(s), src).then_inc(landed[s], 16)
                else:
                    src = (wg_v if kind == "g" else wu_v)[bass.ds(e, 1), :, :].rearrange("e p n -> (e p) n")
                    sp.dma_start(ring[s][:, :], src).then_inc(landed[s], 16)

            def start_of_pass(p, first):
                load_expert("g", 0, 0, p, 0, first)
                load_expert("u", 0, 1, p, 0, first)
                load_expert("g", 1, 2, p, 0, first)
                load_expert("u", 1, 3, p, 0, first)
                load_expert("d", 0, 4, p, 0, first)
                load_expert("g", 2, 5, p, 0, first)

            def pair(p, i, e):
                for s in range(2):
                    load_expert("u", e + (2 + s), 6 + 3 * s, p, i)
                    load_expert("d", e + (1 + s), 7 + 3 * s, p, i)
                    if isinstance(e, int) and s == 1:
                        load_expert("d", NE - 1, 11, p, i)
                    else:
                        load_expert("g", e + (3 + s), 8 + 3 * s, p, i)

            for g in range(NPRE):
                if g >= PRE_RING:
                    sp.wait_ge(proj_done, first_bank[g - PRE_RING + 1])
                src, n = pre_source(g)
                s = g % PRE_RING
                sp.dma_start(ring[s][:, :].rearrange("p (k n) -> p k n", n=n), src).then_inc(landed[s], 16)
                if g == 0:
                    sp.wait_ge(early_in, 16 * N_EARLY)
                    sp.dma_start(w_z[:, :, :], w_in_v[:, :, 4608:4624]).then_inc(wz_in, 16)
            start_of_pass(0, True)
            sp.wait_ge(route_ready, 1)
            passes = sp.value_load(npass[0:1, 0:1], min_val=1, max_val=MAXWIN)
            with sp.Fori(0, passes) as p:
                with sp.If(p > 0):
                    start_of_pass(p, False)
                with sp.Fori(0, NE // 2 - 2) as i:
                    pair(p, i, 2 * i)
                pair(p, NE // 2 - 2, NE - 4)
            for tt in range(TT):
                sp.wait_ge(fin_ready, tt + 1)
                sp.dma_start(out[0, tt * P:(tt + 1) * P, :], x_tok[:, tt, :]).then_inc(stored, 16)
            sp.wait_ge(stored, 16 * TT)

        @block.gpsimd
        def _(pool):
            g = nc.gpsimd
            steps = [0]

            def link(ins):
                steps[0] += 1
                ins.then_inc(g_chain, 1)
                pool.wait_ge(g_chain, steps[0])

            g.memset(ident[:, :], 0.0)
            g.memset(antid[:, :], 0.0)
            g.memset(ones_bf[:, :], 1.0)
            g.memset(ones_row[:, :], 1.0)
            g.memset(tri_bf[:, :], 1.0)
            g.memset(reset[:, :], 1.0)
            g.memset(conv_u[:, :, 0:2], 0.0)
            link(g.memset(bias_row[:, T:384], NEG))
            g.affine_select(out=ident[:, :], in_=ident[:, :], compare_op=ALU.not_equal, fill=1.0, base=0,
                            pattern=[[-1, P]], channel_multiplier=1).then_inc(consts, 1)
            g.affine_select(out=antid[:, :], in_=antid[:, :], compare_op=ALU.not_equal, fill=1.0, base=-(P - 1),
                            pattern=[[1, P]], channel_multiplier=1).then_inc(consts, 1)
            g.affine_select(out=tri_bf[:, :], in_=tri_bf[:, :], compare_op=ALU.is_gt, fill=0.0, base=0,
                            pattern=[[1, P]], channel_multiplier=-1).then_inc(consts, 1)
            g.memset(reset[:, :].rearrange("p (c n) -> p c n", n=CH)[:, :, 0:1], 0.0).then_inc(consts, 1)
            g.iota(iota_f[:, :], pattern=[[1, NE]], base=0, channel_multiplier=0,
                   allow_small_or_imprecise_dtypes=True).then_inc(consts, 1)
            g.memset(sbd[:, :, :, :], 0.0).then_inc(sbd_zero, 1)
            g.memset(offf[:, MAXWIN * NE:], 0.0)
            g.memset(lgp[:, :, NG:], -3e38).then_inc(consts, 1)

            smalls = [
                (w_al[:, :], w_gla_alpha[0]),
                (b_al[:, :], b_gla_alpha[0].rearrange("(a p) -> p a", p=P)),
                (qn_w[0:DH, :], q_norm[0].rearrange("(p a) -> p a", a=1)),
                (qn_w[DH:P, :], q_norm[0].rearrange("(p a) -> p a", a=1)),
                (kn_w[0:DH, :], k_norm[0].rearrange("(p a) -> p a", a=1)),
                (kn_w[DH:P, :], k_norm[0].rearrange("(p a) -> p a", a=1)),
                (on_w[:, :], gla_out_norm[0].rearrange("(p a) -> p a", a=1)),
                (cb_sb[:, :], conv_b[0].rearrange("(k p) -> p k", p=P)),
                (g_ffn[:, :], norm_ffn[0].rearrange("(p k) -> p k", k=KD)),
                (b_r[:, 0:NG], b_router_group),
                (b_r[:, NG:NG + NE], b_router_expert),
                (w_r[:, :, 0:NG], w_router_group[0].rearrange("(p k) n -> p k n", k=KD)),
                (w_r[:, :, NG:NG + NE], w_router_expert[0].rearrange("(p k) n -> p k n", k=KD)),
            ] + [(cw_sb[:, j, :], conv_w[0, j].rearrange("(k p) -> p k", p=P)) for j in range(3)]
            assert len(smalls) == N_SMALL
            for dst, src in smalls:
                pool.dma_start(dst, src).then_inc(small_in, 16)

            pool.wait_ge(biasrow_ready, 1)
            pool.dma_start(bias_dram.ap(), bias_row[:, :]).then_inc(bias_stored, 16)

            pool.wait_ge(att_copied, 2)
            for a in range(4):
                v = attm[:, 2 * a:2 * a + 2, :]
                link(g.affine_select(out=v, in_=v, compare_op=ALU.is_ge, fill=0.0, base=0,
                                     pattern=[[0, 2], [1, P]], channel_multiplier=-1))
            g.memset(attm[0:CH, :, CH:P], 0.0).then_inc(att_ready, 1)
            pool.wait_ge(kd_turned, 1)
            pool.wait_ge(state_ready, 3)
            qz = qTz[:, :, :].rearrange("p (b two) t -> p b two t", two=2)
            g.memset(qz[DH:P, :, 0, :], 0.0).then_inc(qz_zero, 1)
            g.memset(qz[0:DH, :, 1, :], 0.0).then_inc(qz_zero, 1)
            pool.wait_ge(bias_stored, 16)
            pool.wait_ge(o_mm, 2)
            for h in range(NH):
                if h >= 4:
                    pool.wait_ge(score_mm, h - 3)
                pool.dma_start(bias_h[:, h % 4, :], bass.AP(bias_dram, h * 384, [[1, P], [1, T]])
                               ).then_inc(bias_in[h % 4], 16)
            pool.wait_ge(h2_ready, 2)
            g.iota(iota_s[:, :], pattern=[[1, SLOTS]], base=0, channel_multiplier=0,
                   allow_small_or_imprecise_dtypes=True).then_inc(iota_ready, 1)
            pool.wait_ge(router_mm, 1)
            g.memset(xs[:, :, SLOTS:SPAD], 0.0).then_inc(iota_ready, 1)
            pool.wait_ge(iota_ready, 2)
            pool.dma_start(ysorted[SLOTS:SPAD, 0:KD * WIN].rearrange("r (k n) -> r k n", k=KD),
                           xs[0:WIN, :, SLOTS:SPAD]).then_inc(y_stored, 16)
            pool.sem_inc(y_free, 1)

            pool.wait_ge(route_ready, 1)
            pool.wait_ge(xs_act, KD // 2)
            pool.wait_ge(xs_dve, KD // 2)
            pool.wait_ge(iota_ready, 2)
            passes = pool.value_load(npass[0:1, 0:1], min_val=1, max_val=MAXWIN)

            def offset(p, e):
                return pool.value_load(off_tab[0:1, bass.ds(p * NE + e, 1)], min_val=0, max_val=SLOTS)

            def window(p, e, b):
                n = (NE + 1) * p + e
                off = offset(p, e)
                v = xs[:, :, bass.ds(off, WIN)]
                g.tensor_copy(xe[b][:, :, 0:WIN], v).then_inc(xe_high, 1)
                pool.wait_ge(xe_high, n + 1)
                pool.sem_inc(xe_ready, 1)
                g.tensor_tensor(xe[b][:, :, WIN:2 * WIN], v, xe[b][:, :, 0:WIN].bitcast(F32),
                                ALU.subtract).then_inc(xe_ready, 1)

            def low_part(p, i, q):
                s = slot_of(q)
                for c in POOL_LO:
                    n = PER_PASS * CHUNKS * p + RING * CHUNKS * i + CHUNKS * q + c
                    pool.wait_ge(hi_ready, n + 1)
                    g.tensor_tensor(ring_lo[s][:, chunk(c)], ring[s][:, chunk(c)], hi_buf(q, c).bitcast(F32),
                                    ALU.subtract).then_inc(lo_ready_pool, 1)

            def store(p, e, b):
                off = offset(p, e)
                pool.wait_ge(y_ready, NE * p + e + 2)
                pool.wait_ge(y_stored, (16 * NE) * p + 16 * e + 16)
                pool.sem_inc(y_free, 1)
                pool.dma_start(ysorted[bass.ds(off, WIN), :], y_tok[:, b, :]).then_inc(y_stored, 16)

            with pool.Fori(0, passes) as p:
                pool.wait_ge(freed, after_slots(p, 0))
                window(p, 0, 0)
                window(p, 1, 1)
                low_part(p, 0, 0)
                low_part(p, 0, 1)
                low_part(p, 0, 2)
                pool.wait_ge(freed, after_slots(p, 2))
                window(p, 2, 0)
                low_part(p, 0, 3)
                low_part(p, 0, 4)
                with pool.Fori(0, NE // 2 - 1) as i:
                    for s in range(2):
                        low_part(p, i, 5 + 3 * s)
                        pool.wait_ge(freed, after_slots(p, 6 * i + (4 + 3 * s)))
                        window(p, 3 + 2 * i + s, (s + 1) % 2)
                        low_part(p, i, 6 + 3 * s)
                        store(p, 2 * i + s, s)
                        low_part(p, i, 7 + 3 * s)
                low_part(p, 0, PER_PASS - 1)
                store(p, NE - 2, 0)
                store(p, NE - 1, 1)
                pool.wait_ge(y_stored, (16 * NE) * p + (16 * NE + 16))
            for j in range(2 * TT):
                g.indirect_dma_start(out=y_back[:, j, :], out_offset=None, in_=ysorted[0:SLOTS, :],
                                     in_offset=bass.IndirectOffsetOnAxis(ap=slot_u[:, j:j + 1], axis=0)
                                     ).then_inc(back_in[j], 16)
            for j in range(2 * TT):
                pool.wait_ge(back_in[j], 16)

        @block.scalar
        def _(act):
            s_ = nc.scalar

            early = [(g_mix[:, :], norm_mix[0].rearrange("(p k) -> p k", k=KD)),
                     (onehot[:, :], onehot_dram),
                     (table[:, :], rel_bias_table)]
            assert len(early) == N_EARLY
            for dst, src in early:
                act.dma_start(dst, src).then_inc(early_in, 16)

            act.wait_ge(ms_ready, 2)
            s_.activation(stat[:, 2:4], stat[:, 0:2], ACT.Sqrt).then_inc(rms_ready, 1)

            def high_pre(g):
                act.wait_ge(landed[g % PRE_RING], 16 * (g // PRE_RING + 1))
                for c in range(CHUNKS):
                    if g and c < CHUNKS - 1:
                        act.wait_ge(chunk_done, (CHUNKS - 1) * (g - 1) + c + 1)
                    elif g:
                        act.wait_ge(proj_done, first_bank[g])
                    s_.activation(w_hi[c][:, :], ring[g % PRE_RING][:, chunk(c)], ACT.Copy).then_inc(wpre_hi, 1)

            act.wait_ge(early_in, 16 * N_EARLY)
            high_pre(0)
            for kp in range(4):
                act.wait_ge(hT_turned, kp + 1)
                for k in range(2):
                    s_.activation(hT_hi[:, 2 * kp + k, :], bank(4 + kp, 2)[:, k, :], ACT.Copy,
                                  scale=g_mix[:, 2 * kp + k:2 * kp + k + 1]).then_inc(hT_act, 1)
            act.wait_ge(wz_in, 16)
            s_.activation(w_z_hi[:, :, :], w_z[:, :, :], ACT.Copy).then_inc(wz_hi_ready, 1)

            def evac(g, m, dst, func=ACT.Copy, scale=1.0):
                b, _ = bank_of(g, m)
                act.wait_ge(proj_done, first_bank[g] + m + 1)
                s_.activation(dst, bank(b), func, scale=scale).then_inc(evacuated[b], 1)

            evac(0, 0, flat(gqk[:, 0:2, :]), scale=float(GK) ** -0.5)
            high_pre(1)
            evac(0, 1, flat(gqk[:, 2:4, :]))
            act.wait_ge(z_mm, 1)
            s_.activation(zT[:, :], ps[0:16, 4, 0:T], ACT.Copy).then_inc(z_ready, 1)
            evac(1, 0, gv[:, 0, :])
            act.wait_ge(small_in, 16 * N_SMALL)
            act.wait_ge(sigmin_ready, 2)
            for a in range(2):
                s_.activation(e_pos[:, a, :], bank(5, 2)[:, a, :], ACT.Abs,
                              bias=b_al[:, a:a + 1]).then_inc(a_chain, 1)
            act.wait_ge(a_chain, 2)
            s_.activation(e_pos, e_pos, ACT.Exp, scale=-1.0).then_inc(a_chain, 1)
            act.wait_ge(a_chain, 3)
            s_.activation(e_pos, e_pos, ACT.Ln, bias=1.0).then_inc(softplus_ready, 1)
            high_pre(2)
            evac(1, 1, gv[:, 1, :])
            act.wait_ge(cum_ready, 3)
            s_.activation(e_rest, e_rest, ACT.Exp, scale=1.0 / TEMP).then_inc(decay_ready, 1)
            s_.activation(e_pos, la, ACT.Exp, scale=1.0 / TEMP).then_inc(decay_ready, 1)
            s_.activation(e_neg, la, ACT.Exp, scale=-1.0 / TEMP).then_inc(decay_ready, 1)
            evac(2, 0, gr[:, 0, :], func=ACT.Silu)
            act.wait_ge(kd_turned, 1)
            s_.activation(flat(kdn[:, :, :]), bank(6), ACT.Copy).then_inc(kdn_ready, 1)
            high_pre(3)
            evac(2, 1, gr[:, 1, :], func=ACT.Silu)
            for tt in range(TT):
                act.wait_ge(o_mm, tt + 1)
                s_.activation(scr[:, tt, :], bank(4 if tt == 0 else 7), ACT.Square).then_inc(o_sq, 1)
            act.wait_ge(o_ms, 1)
            s_.activation(stat[:, 16:24], stat[:, 8:16], ACT.Sqrt).then_inc(o_rms, 1)
            high_pre(4)
            for m in range(2):
                act.wait_ge(yg_turned, 2)
                s_.activation(yg_hi[:, 2 * m:2 * m + 2, :], bank(5 + m, 2), ACT.Copy,
                              scale=on_w[:, 0:1]).then_inc(yg_hi_ready, 1)
            high_pre(5)
            act.wait_ge(qk_ms, 1)
            s_.activation(qkr[:, :, :, :], qkm[:, :, :, :], ACT.Sqrt).then_inc(qk_rms, 1)
            evac(5, 0, av[:, 0, :])
            high_pre(6)
            evac(5, 1, av[:, 1, :])
            for m in range(2):
                act.wait_ge(qk_turned, 3 + m)
                s_.activation(kT[:, 2 * m:2 * m + 2, :], bank(6 + m, 2), ACT.Copy,
                              scale=kn_w[:, 0:1]).then_inc(kT_ready, 1)

            def softmax_exp(h):
                act.wait_ge(rowmax_ready, h + 1)
                if h >= 2:
                    act.wait_ge(prob_turned, h - 1)
                for tt in range(TT):
                    s_.activation(prob[:, h % 2, P * tt:P + 2 * P * tt], ps[:, 4 + h % 2, P * tt:P + 2 * P * tt],
                                  ACT.Exp, bias=nmx[:, h, tt:tt + 1],
                                  accum_out=rsum[:, h, tt:tt + 1]).then_inc(exp_ready, 1)

            def prob_out(h):
                act.wait_ge(prob_turned, h + 1)
                if h >= 2:
                    act.wait_ge(pv_mm, h - 1)
                s_.activation(probT[:, h % 2, :], bank(6)[:, 0:384], ACT.Copy).then_inc(probT_ready, 1)

            def gate_out(n, half, m):
                if n == 2:
                    act.wait_ge(branch_done, 2 * half + m + 1)
                dt = 4 * half + 2 * m
                evac(9 + 3 * n + half, m, flat(sig[n][:, dt:dt + 2, :]), func=ACT.Sigmoid)

            evac(6, 0, flat(ycT[:, 0:2, :]))
            softmax_exp(0)
            for h in range(1, NH):
                if h % 2:
                    high_pre(7 + h // 2)
                if h == 1:
                    evac(6, 1, flat(ycT[:, 2:4, :]))
                softmax_exp(h)
                prob_out(h - 1)
                if h >= 6:
                    gate_out(0, 0, h - 6)
            prob_out(NH - 1)
            gate_out(0, 1, 0)
            high_pre(11)
            gate_out(0, 1, 1)
            for n in range(1, 3):
                high_pre(9 + 3 * n)
                for half in range(2):
                    gate_out(n, half, 0)
                    high_pre(10 + 3 * n + half)
                    gate_out(n, half, 1)

            def merged_high(m):
                act.wait_ge(branch_done, 8 + m + 1)
                s_.activation(merged_hi[:, 2 * m:2 * m + 2, :], mergedT[:, 2 * m:2 * m + 2, :],
                              ACT.Copy).then_inc(merged_hi_ready, 1)

            merged_high(0)
            merged_high(1)
            high_pre(18)
            merged_high(2)
            merged_high(3)
            high_pre(19)

            act.wait_ge(ms2_ready, 2)
            s_.activation(stat[:, 2:4], stat[:, 0:2], ACT.Sqrt).then_inc(rms2_ready, 1)
            for kp in range(2):
                act.wait_ge(h2_turned, kp + 1)
                for k in range(2):
                    s_.activation(h2T[:, 2 * kp + k, :], bank(4 + kp, 2)[:, k, :], ACT.Copy,
                                  scale=g_ffn[:, 2 * kp + k:2 * kp + k + 1]).then_inc(hT_act, 1)
            act.wait_ge(nmax_ready, 1)
            for tt in range(TT):
                s_.activation(rt[:, tt, 8:12], lgp[:, tt, 0:NG], ACT.Exp, bias=rt[:, tt, 0:1],
                              accum_out=rt[:, tt, 1:2]).then_inc(gexp_ready, 1)
            act.wait_ge(e2in_ready, 1)
            s_.activation(rt[:, :, 3:4], rt[:, :, 2:3], ACT.Exp).then_inc(e2_ready, 1)
            for k in range(0, KD, 2):
                act.wait_ge(gather_mm, k + 1)
                s_.activation(xs[:, k, 0:SLOTS], bank(2 + k % 4), ACT.Copy,
                              scale=g_ffn[:, k:k + 1]).then_inc(xs_act, 1)

            act.wait_ge(route_ready, 1)
            passes = act.value_load(npass[0:1, 0:1], min_val=1, max_val=MAXWIN)

            def high_part(p, i, q, cs):
                s = slot_of(q)
                for c in cs:
                    if c == 0:
                        act.wait_ge(landed[s], (16 * PER_PASS // RING) * p + 16 * i + 16 * (uses_before(q) + 1))
                    act.wait_ge(freed, PER_PASS * CHUNKS * p + RING * CHUNKS * i + CHUNKS * q + c + 1 - HI_BUFS
                                + FREED_SEED)
                    s_.activation(hi_buf(q, c), ring[s][:, chunk(c)], ACT.Copy).then_inc(hi_ready, 1)

            def gu_low_rows(p, n, b):
                act.wait_ge(freed, after_slots(p, n))
                s_.activation(g_lo[:, :], ps[WIN:P, 2 * b, :], ACT.Copy).then_inc(gu_lo_out, 1)
                s_.activation(u_lo[:, :], ps[WIN:P, 2 * b + 1, :], ACT.Copy).then_inc(gu_lo_out, 1)

            def silu(p, e):
                act.wait_ge(gu_free, 2 * NE * p + 2 * e + 5)
                s_.activation(g_act[:, :], g_sum[:, :], ACT.Silu).then_inc(silu_ready, 1)

            def he_high(p, e):
                act.wait_ge(h_turned, NE * p + e + 1)
                s_.activation(he[:, :, 0:WIN], ps[:, 6, 0:KC * WIN].rearrange("p (k n) -> p k n", n=WIN),
                              ACT.Copy).then_inc(he_hi, 1)

            def y_low_rows(p, n):
                act.wait_ge(freed, after_slots(p, n))
                s_.activation(y_lo[:, :], flat(ps[WIN:P, 4:6, :]), ACT.Copy).then_inc(y_lo_out, 1)

            def step(p, e, i, q, b, before_gu, before_y):
                high_part(p, i, q, (0,))
                gu_low_rows(p, before_gu, 1 - b)
                high_part(p, i, q, (1,))
                silu(p, e - 1)
                high_part(p, i, q, (2,))
                high_part(p, i, q, (3,))
                high_part(p, i, q + 1, (0,))
                if before_y is not None:
                    y_low_rows(p, before_y)
                high_part(p, i, q + 1, (1, 2, 3))
                high_part(p, i, q + 2, (0,))
                he_high(p, e - 1)
                high_part(p, i, q + 2, (1, 2, 3))

            with act.Fori(0, passes) as p:
                high_part(p, 0, 0, (0, 1, 2, 3))
                high_part(p, 0, 1, (0, 1, 2, 3))
                step(p, 1, 0, 2, 1, 2, None)
                with act.Fori(0, NE // 2 - 1) as i:
                    for s in range(2):
                        step(p, 2 * i + (2 + s), i, 5 + 3 * s, s, 6 * i + (4 + 3 * s), 6 * i + (5 + 3 * s))
                gu_low_rows(p, PER_PASS - 2, 1)
                silu(p, NE - 1)
                high_part(p, 0, PER_PASS - 1, (0,))
                y_low_rows(p, PER_PASS - 1)
                he_high(p, NE - 1)
                high_part(p, 0, PER_PASS - 1, (1, 2, 3))
                y_low_rows(p, PER_PASS)

        @block.tensor
        def _(pe):
            t_ = nc.tensor

            def turn_x(src, ready, signal):
                pe.wait_ge(ready, TT)
                for kp in range(4):
                    for k in range(2):
                        for tt in range(TT):
                            ins = t_.transpose(bank(4 + kp, 2)[:, k, tt * P:(tt + 1) * P],
                                               src[:, tt, 2 * kp + k::KD], ident[:, :])
                    ins.then_inc(signal, 1)

            def begin(g, m):
                b, use = bank_of(g, m)
                if use:
                    pe.wait_ge(evacuated[b], use)
                return b

            def weights(g, at, n):
                c = at // CW
                return w_hi[c][:, at - CW * c:at - CW * c + n], ring_lo[g % PRE_RING][:, at:at + n]

            def by_token(g, tt, x_hi, x_lo):
                b = begin(g, tt)
                rows = slice(tt * P, (tt + 1) * P)
                for k in range(KD):
                    if tt == 0 and k % CHUNK_T == 0:
                        pe.wait_ge(wpre_lo, CHUNKS * g + k // CHUNK_T + 1)
                    wh, wl = weights(g, k * C, C)
                    t_.matmul(bank(b), x_hi[:, k, rows], wh, start=(k == 0), stop=False)
                    t_.matmul(bank(b), x_hi[:, k, rows], wl, start=False, stop=False)
                    ins = t_.matmul(bank(b), x_lo[:, k, rows], wh, start=False, stop=(k == KD - 1))
                    if tt == TT - 1 and k % CHUNK_T == CHUNK_T - 1 and k < KD - 1:
                        ins.then_inc(chunk_done, 1)
                ins.then_inc(proj_done, 1)

            def by_feature(g, m, banks, n, x_hi, x_lo):
                b = begin(g, m)
                nk = SLOT // n
                for k in range(nk):
                    c = k * n // CW
                    first_of_chunk = k * n % CW == 0
                    if m == 0 and first_of_chunk:
                        pe.wait_ge(wpre_lo, CHUNKS * g + c + 1)
                    for j in range(2):
                        wh, wl = weights(g, k * n + (2 * m + j) * P, P)
                        o = bank(b, 2)[:, j, :]
                        t_.matmul(o, wh, x_hi[:, k, :], start=(k == 0 and j == 0), stop=False, skip_group_check=True)
                        t_.matmul(o, wh, x_lo[:, k, :], start=False, stop=False, skip_group_check=True)
                        ins = t_.matmul(o, wl, x_hi[:, k, :], start=False, stop=(k == nk - 1), skip_group_check=True)
                    if m == banks - 1 and (k + 1) * n % CW == 0 and k < nk - 1:
                        ins.then_inc(chunk_done, 1)
                ins.then_inc(proj_done, 1)

            def feat(g, m):
                by_feature(g, m, 2, C, hT_hi, hT_lo)

            def tok(g, tt):
                by_token(g, tt, hT_hi, hT_lo)

            pe.wait_ge(early_in, 16 * N_EARLY)
            pe.wait_ge(consts, 6)
            t_.matmul(ps[0:NH, 3, 0:T], table[:, :], onehot[:, :], start=True, stop=True).then_inc(biasrow_mm, 1)
            turn_x(xn, xn_ready, hT_turned)
            pe.wait_ge(hT_lo_ready, 8)
            feat(0, 0)
            feat(0, 1)
            pe.wait_ge(wz_lo_ready, 1)
            for k in range(KD):
                o = ps[0:16, 4, 0:T]
                t_.matmul(o, w_z_hi[:, k, :], hT_hi[:, k, :], start=(k == 0), stop=False)
                t_.matmul(o, w_z_hi[:, k, :], hT_lo[:, k, :], start=False, stop=False)
                ins = t_.matmul(o, w_z_lo[:, k, :], hT_hi[:, k, :], start=False, stop=(k == KD - 1))
            ins.then_inc(z_mm, 1)
            tok(1, 0)
            pe.wait_ge(z_ready, 1)
            pe.wait_ge(small_in, 16 * N_SMALL)
            for a in range(2):
                ins = t_.matmul(bank(5, 2)[:, a, :], w_al[:, a * P:(a + 1) * P], zT[:, :], start=True, stop=True)
            ins.then_inc(alpha_mm, 1)
            pe.wait_ge(biasrow_ready, 1)
            tok(1, 1)
            tok(2, 0)

            pe.wait_ge(gla_in_ready, 1)
            for tt in range(TT):
                for a in range(2):
                    ins = t_.transpose(bank(6, 4)[:, 2 * tt + a, :], e_rest[:, a, tt * P:(tt + 1) * P], ident[:, :])
            ins.then_inc(kd_turned, 1)
            pe.wait_ge(gla_in_ready, 3)
            for par in range(2):
                for tt in range(TT):
                    for a in range(2):
                        rows = slice(GK * par, GK * par + GK)
                        ins = t_.matmul(bank(4 + 3 * par, 4)[:, 2 * tt + a, :], gqk[rows, 2 + a, tt * P:(tt + 1) * P],
                                        gqk[rows, a, tt * P:(tt + 1) * P], start=True, stop=True)
                ins.then_inc(att_mm, 1)
            tok(2, 1)
            pe.wait_ge(kdn_ready, 1)
            pe.wait_ge(att_copied, 1)
            pe.wait_ge(evacuated[bank_of(1, 0)[0]], bank_of(1, 0)[1] + 1)
            pe.wait_ge(evacuated[bank_of(1, 1)[0]], bank_of(1, 1)[1] + 1)
            for c in range(3):
                rows = slice(CH * (c % 2), CH * (c % 2) + CH)
                for a in range(2):
                    ins = t_.matmul(bank((5, 6, 4)[c], 2)[:, a, :], kdn[rows, c // 2, a * P:(a + 1) * P],
                                    gv[rows, c // 2, a * 256:(a + 1) * 256], start=True, stop=True)
                ins.then_inc(kv_mm, 1)
            tok(3, 0)
            pe.wait_ge(att_ready, 1)
            pe.wait_ge(state_ready, 3)
            for tt in range(TT):
                b = 4 if tt == 0 else 7
                for h in range(GH):
                    t_.matmul(bank(b, 4)[:, h, :], attm[:, 4 * (h % 2) + 2 * tt + h // 2, :],
                              gv[:, tt, h * GV:(h + 1) * GV], start=(h == 0), stop=False, skip_group_check=True)
                for c in range(max(1, 2 * tt), 2 * tt + 2):
                    rows = slice(CH * (c % 2), CH * (c % 2) + CH)
                    for a in range(2):
                        ins = t_.matmul(bank(b, 2)[rows, a, :], gqk[:, a, c * CH:(c + 1) * CH], sbd[:, c - 1, a, :],
                                        start=False, stop=True, skip_group_check=True)
                ins.then_inc(o_mm, 1)
            tok(3, 1)
            tok(4, 0)
            pe.wait_ge(ygla_ready, 2)
            for m in range(2):
                for h in range(2):
                    for tt in range(TT):
                        ins = t_.transpose(bank(5 + m, 2)[:, h, tt * P:(tt + 1) * P],
                                           gr[:, tt, (2 * m + h) * GV:(2 * m + h + 1) * GV], ident[:, :])
                ins.then_inc(yg_turned, 1)
            tok(4, 1)
            tok(5, 0)
            tok(5, 1)
            pe.wait_ge(ygT_ready, 2)
            pe.wait_ge(qkn_ready, 2)
            for w in range(2):
                for m in range(2):
                    for j in range(2):
                        for tt in range(TT):
                            ins = t_.transpose(bank(4 + 2 * w + m, 2)[:, j, tt * P:(tt + 1) * P],
                                               aqk[:, w, tt, (2 * m + j) * P:(2 * m + j + 1) * P], ident[:, :])
                    ins.then_inc(qk_turned, 1)

            def scores(h):
                b = 4 + h % 2
                if h == 0:
                    pe.wait_ge(kT_ready, 2)
                    pe.wait_ge(qT_ready, 4)
                if h >= 2:
                    pe.wait_ge(exp_ready, 2 * (h - 1))
                pe.wait_ge(bias_in[h % 4], 16 * (h // 4 + 1))
                for tt in range(TT):
                    o = ps[:, b, P * tt:P + 2 * P * tt]
                    keys = slice(0, P * (tt + 1))
                    t_.matmul(o, antid[:, :], bias_h[:, h % 4, P * (1 - tt):T], start=True, stop=False)
                    ins = t_.matmul(o, qTz[:, h, tt * P:(tt + 1) * P], kT[:, h // 2, keys], start=False, stop=True)
                ins.then_inc(score_mm, 1)

            def turn_prob(h):
                pe.wait_ge(prob_ready, h + 1)
                if h >= 1:
                    pe.wait_ge(probT_ready, h)
                for j in range(3):
                    ins = t_.transpose(bank(6, 4)[:, j, :], prob[:, h % 2, j * P:(j + 1) * P], ident[:, :])
                ins.then_inc(prob_turned, 1)

            def prob_v(h):
                pe.wait_ge(probT_ready, h + 1)
                if h >= 2:
                    pe.wait_ge(yaT_ready, h // 2)
                rows = slice(DH * (h % 2), DH * (h % 2) + DH)
                o = bank(7, 2)[rows, (h // 2) % 2, :]
                t_.matmul(o, av[:, 0, h * DH:(h + 1) * DH], probT[:, h % 2, 0:T], start=True, stop=False)
                t_.matmul(o[:, P:T], av[:, 1, h * DH:(h + 1) * DH], probT[:, h % 2, T:T + P],
                          start=False, stop=True).then_inc(pv_mm, 1)

            dense = [lambda g=g, m=m: feat(g, m) for g in (6, 7, 8, 9, 10) for m in range(2)]
            pe.wait_ge(evacuated[bank_of(5, 0)[0]], bank_of(5, 0)[1] + 1)
            pe.wait_ge(evacuated[bank_of(5, 1)[0]], bank_of(5, 1)[1] + 1)
            for u in range(NH + 2):
                dense[u]()
                if u < NH:
                    scores(u)
                if 1 <= u <= NH:
                    turn_prob(u - 1)
                if u >= 2:
                    prob_v(u - 2)

            def branch(n, y_hi, y_lo):
                for m in range(4):
                    by_feature(11 + 3 * n, m, 4, D, y_hi, y_lo)

            pe.wait_ge(ycT_ready, 2)
            branch(0, yc_hi, yc_lo)
            for n in range(1, 3):
                for half in range(2):
                    for m in range(2):
                        feat(9 + 3 * n + half, m)
                if n == 1:
                    pe.wait_ge(yaT_ready, 4)
                    branch(1, ya_hi, ya_lo)
                else:
                    branch(2, yg_hi, yg_lo)
            pe.wait_ge(merged_lo_ready, 4)
            for half in range(2):
                for tt in range(TT):
                    by_token(18 + half, tt, merged_hi, merged_lo)

            turn_x(xn, h2_ready, h2_turned)
            pe.wait_ge(hT_act, 8 + 4)
            pe.wait_ge(hT_dve, 4)
            for tt in range(TT):
                o = ps[:, 0, tt * 36:(tt + 1) * 36]
                t_.matmul(o, ones_row[:, :], b_r[:, :], start=True, stop=False)
                for k in range(KD):
                    ins = t_.matmul(o, h2T[:, k, tt * P:(tt + 1) * P], w_r[:, k, :], start=False, stop=(k == KD - 1))
            ins.then_inc(router_mm, 1)
            pe.wait_ge(assign_ready, 2)
            for tt in range(TT):
                o = ps[:, 1, tt * NE:(tt + 1) * NE]
                t_.matmul(o, tri_bf[:, :], eall_bf[:, tt, :], start=True, stop=False)
                if tt:
                    t_.matmul(o, ones_bf[:, :], eall_bf[:, 0, :], start=False, stop=False)
                t_.matmul(o, ones_bf[:, :], epre_bf[:, 0, :], start=False, stop=False)
                t_.matmul(o, ones_bf[:, :], epre_bf[:, 1, :], start=False, stop=True)
            for j, src in enumerate((epre_bf, eall_bf)):
                o = ps[:, 1, (2 + j) * NE:(3 + j) * NE]
                t_.matmul(o, ones_bf[:, :], src[:, 0, :], start=True, stop=False)
                ins = t_.matmul(o, ones_bf[:, :], src[:, 1, :], start=False, stop=True)
            ins.then_inc(pos_mm, 1)
            pe.wait_ge(perm_ready, 2)
            for k in range(KD):
                if k >= 4:
                    pe.wait_ge((xs_act, xs_dve)[k % 2], (k - 4) // 2 + 1)
                for tt in range(TT):
                    ins = t_.matmul(bank(2 + k % 4), xn[:, tt, k::KD], perm[:, tt, :], start=(tt == 0), stop=(tt == 1))
                ins.then_inc(gather_mm, 1)
            pe.wait_ge(route_ready, 1)
            pe.sem_inc(freed, FREED_SEED)
            passes = pe.value_load(npass[0:1, 0:1], min_val=1, max_val=MAXWIN)

            def products(p, i, q, lhs, out_of, tile_of):
                for c in range(CHUNKS):
                    n = PER_PASS * CHUNKS * p + RING * CHUNKS * i + CHUNKS * q + c
                    pe.wait_ge(hi_ready, n + 1)
                    if c in POOL_LO:
                        pe.wait_ge(lo_ready_pool, PER_PASS * len(POOL_LO) * p + RING * len(POOL_LO) * i
                                   + len(POOL_LO) * q + POOL_LO.index(c) + 1)
                    else:
                        nd = CHUNKS - len(POOL_LO)
                        pe.wait_ge(lo_ready, PER_PASS * nd * p + RING * nd * i + nd * q + c + 1)
                    for j in range(CHUNK_T):
                        k, o, first, last = tile_of(CHUNK_T * c + j)
                        at = CW * c + C * j
                        t_.matmul(out_of(o), lhs[:, k, :], hi_buf(q, c)[:, C * j:C * (j + 1)], start=first, stop=False)
                        ins = t_.matmul(out_of(o), lhs[:, k, :], ring_lo[slot_of(q)][:, at:at + C], start=False,
                                        stop=last)
                    ins.then_inc(freed, 1)

            def gate_up(p, i, q, b, up):
                products(p, i, q, xe[b], lambda o: ps[:, 2 * b + up, :], lambda k: (k, 0, k == 0, k == KD - 1))

            def down(p, i, q):
                products(p, i, q, he, lambda o: ps[:, 4 + o, :],
                         lambda n: (n // 2, n % 2, n // 2 == 0, n // 2 == KC - 1))

            def start_gate(p, e):
                pe.wait_ge(xe_ready, 2 * (NE + 1) * p + 2 * e + 2)
                pe.wait_ge(gu_free, 2 * NE * p + 2 * e + 2)

            def turn_h(p, e):
                pe.wait_ge(h_ready, NE * p + e + 1)
                for j in range(KC):
                    ins = t_.matmul(ps[:, 6, j * WIN:(j + 1) * WIN], h_tok[:, j * P:(j + 1) * P],
                                    ident[0:WIN, 0:WIN], start=True, stop=True)
                ins.then_inc(h_turned, 1)

            def start_down(p, e):
                pe.wait_ge(he_hi, NE * p + e + 1)
                pe.wait_ge(he_lo, NE * p + e + 1)
                pe.wait_ge(y_ready, NE * p + e + 1)

            def step(p, e, i, q, b):
                start_gate(p, e)
                gate_up(p, i, q, b, 0)
                turn_h(p, e - 1)
                gate_up(p, i, q + 1, b, 1)
                start_down(p, e - 1)
                down(p, i, q + 2)

            with pe.Fori(0, passes) as p:
                start_gate(p, 0)
                gate_up(p, 0, 0, 0, 0)
                gate_up(p, 0, 1, 0, 1)
                step(p, 1, 0, 2, 1)
                with pe.Fori(0, NE // 2 - 1) as i:
                    for s in range(2):
                        step(p, 2 * i + (2 + s), i, 5 + 3 * s, s)
                turn_h(p, NE - 1)
                start_down(p, NE - 1)
                down(p, 0, PER_PASS - 1)

        @block.vector
        def _(dve):
            v = nc.vector
            steps = [0]

            def link(ins):
                steps[0] += 1
                ins.then_inc(v_chain, 1)
                dve.wait_ge(v_chain, steps[0])

            def norm_stats(src, dst, signal):
                for tt in range(TT):
                    if src is x_tok and signal is ms_ready:
                        dve.wait_ge(x_in[tt], 16)
                    link(v.tensor_tensor_reduce(dst[:, tt, :], src[:, tt, :], src[:, tt, :], 1.0, 0.0, ALU.mult,
                                                ALU.add, stat[:, tt:tt + 1]))
                    v.tensor_scalar(stat[:, tt:tt + 1], stat[:, tt:tt + 1], 1.0 / D, EPS, ALU.mult,
                                    ALU.add).then_inc(signal, 1)

            def norm_apply(src, dst, rms, signal):
                dve.wait_ge(rms, 1)
                link(v.reciprocal(stat[:, 4:6], stat[:, 2:4]))
                for tt in range(TT):
                    v.tensor_scalar(dst[:, tt, :], src[:, tt, :], stat[:, 4 + tt:5 + tt], None,
                                    ALU.mult).then_inc(signal, 1)

            def low_pre(g):
                for c in range(CHUNKS):
                    dve.wait_ge(wpre_hi, CHUNKS * g + c + 1)
                    v.tensor_tensor(ring_lo[g % PRE_RING][:, chunk(c)], ring[g % PRE_RING][:, chunk(c)],
                                    w_hi[c][:, :].bitcast(F32), ALU.subtract).then_inc(wpre_lo, 1)

            norm_stats(x_tok, xn, ms_ready)
            norm_apply(x_tok, xn, rms_ready, xn_ready)
            dve.wait_ge(consts, 6)
            dve.wait_ge(biasrow_mm, 1)
            v.tensor_copy(bias_row[:, 0:T], ps[0:NH, 3, 0:T]).then_inc(biasrow_ready, 1)
            dve.wait_ge(early_in, 16 * N_EARLY)
            low_pre(0)
            for kp in range(4):
                dve.wait_ge(hT_act, 2 * (kp + 1))
                for k in (2 * kp, 2 * kp + 1):
                    v.scalar_tensor_tensor(out=hT_lo[:, k, :], in0=bank(4 + kp, 2)[:, k % 2, :],
                                           scalar=g_mix[:, k:k + 1], in1=hT_hi[:, k, :].bitcast(F32), op0=ALU.mult,
                                           op1=ALU.subtract).then_inc(hT_lo_ready, 1)
            dve.wait_ge(wz_hi_ready, 1)
            v.tensor_tensor(w_z_lo[:, :, :], w_z[:, :, :], w_z_hi[:, :, :].bitcast(F32),
                            ALU.subtract).then_inc(wz_lo_ready, 1)
            low_pre(1)
            dve.wait_ge(small_in, 16 * N_SMALL)

            dve.wait_ge(alpha_mm, 1)
            for a in range(2):
                v.tensor_scalar(e_neg[:, a, :], bank(5, 2)[:, a, :], b_al[:, a:a + 1], 0.0, ALU.add,
                                ALU.min).then_inc(sigmin_ready, 1)
            dve.wait_ge(sigmin_ready, 2)
            dve.wait_ge(softplus_ready, 1)
            link(v.tensor_tensor(e_rest, e_neg, e_pos, ALU.subtract))
            for a in range(2):
                v.tensor_tensor_scan(la[:, a, :], reset[:, :], e_rest[:, a, :], 0.0, ALU.mult,
                                     ALU.add).then_inc(cum_ready, 1)
            dve.wait_ge(cum_ready, 2)
            for a in range(2):
                run = la[:, a, :].rearrange("p (c n) -> p c n", n=CH)
                ins = v.tensor_tensor(e_rest[:, a, :].rearrange("p (c n) -> p c n", n=CH),
                                      run[:, :, CH - 1:CH].broadcast_to([P, T // CH, CH]), run, ALU.subtract)
                if a == 0:
                    link(ins)
            ins.then_inc(cum_ready, 1)
            low_pre(2)
            dve.wait_ge(evacuated[bank_of(0, 1)[0]], 1)
            dve.wait_ge(decay_ready, 1)
            v.tensor_tensor(e_rest, gqk[:, 2:4, :], e_rest, ALU.mult).then_inc(gla_in_ready, 1)
            dve.wait_ge(decay_ready, 2)
            v.tensor_tensor(gqk[:, 0:2, :], gqk[:, 0:2, :], e_pos, ALU.mult).then_inc(gla_in_ready, 1)
            dve.wait_ge(decay_ready, 3)
            v.tensor_tensor(gqk[:, 2:4, :], gqk[:, 2:4, :], e_neg, ALU.mult).then_inc(gla_in_ready, 1)
            for par in range(2):
                dve.wait_ge(att_mm, par + 1)
                v.tensor_copy(attm[:, 4 * par:4 * par + 4, :], bank(4 + 3 * par, 4)).then_inc(att_copied, 1)
            low_pre(3)
            dve.wait_ge(sbd_zero, 1)
            for c in range(3):
                dve.wait_ge(kv_mm, c + 1)
                kv = bank((5, 6, 4)[c], 2)
                if c:
                    dve.wait_ge(state_ready, c)
                for h in range(2):
                    rows = slice(GK * h, GK * h + GK)
                    blk = slice(GV * h, GV * h + GV)
                    if c == 0:
                        ins = v.tensor_copy(sbd[rows, 0, :, blk], kv[rows, :, blk])
                    else:
                        for a in range(2):
                            ins = v.scalar_tensor_tensor(out=sbd[rows, c, a, blk], in0=sbd[rows, c - 1, a, blk],
                                                         scalar=e_pos[rows, a, CH * c + CH - 1:CH * c + CH],
                                                         in1=kv[rows, a, blk], op0=ALU.mult, op1=ALU.add)
                ins.then_inc(state_ready, 1)

            def take(g, m, w, tt):
                b, _ = bank_of(g, m)
                dve.wait_ge(proj_done, first_bank[g] + m + 1)
                v.tensor_copy(aqk[:, w, tt, :], bank(b)).then_inc(evacuated[b], 1)

            take(3, 0, 0, 0)
            for tt in range(TT):
                dve.wait_ge(o_sq, tt + 1)
                link(v.tensor_reduce(stat[:, 8 + 4 * tt:12 + 4 * tt], scr[:, tt, :].rearrange("p (h n) -> p h n", n=GV),
                                     AX_X, ALU.add))
            v.tensor_scalar(stat[:, 8:16], stat[:, 8:16], 1.0 / GV, EPS, ALU.mult, ALU.add).then_inc(o_ms, 1)
            low_pre(4)
            take(3, 1, 0, 1)
            dve.wait_ge(o_rms, 1)
            link(v.reciprocal(stat[:, 24:32], stat[:, 16:24]))
            for tt in range(TT):
                o3 = scr[:, tt, :].rearrange("p (h n) -> p h n", n=GV)
                link(v.tensor_tensor(o3, bank(4 if tt == 0 else 7, 4),
                                     stat[:, 24 + 4 * tt:28 + 4 * tt].unsqueeze(2).broadcast_to([P, GH, GV]), ALU.mult))
                dve.wait_ge(evacuated[bank_of(2, tt)[0]], bank_of(2, tt)[1] + 1)
                v.tensor_tensor(gr[:, tt, :], scr[:, tt, :], gr[:, tt, :], ALU.mult).then_inc(ygla_ready, 1)
            take(4, 0, 1, 0)
            low_pre(5)
            take(4, 1, 1, 1)
            for m in range(2):
                dve.wait_ge(yg_hi_ready, m + 1)
                v.scalar_tensor_tensor(out=yg_lo[:, 2 * m:2 * m + 2, :], in0=bank(5 + m, 2), scalar=on_w[:, 0:1],
                                       in1=yg_hi[:, 2 * m:2 * m + 2, :].bitcast(F32), op0=ALU.mult,
                                       op1=ALU.subtract).then_inc(ygT_ready, 1)
            for w in range(2):
                if w == 1:
                    dve.wait_ge(evacuated[bank_of(4, 0)[0]], bank_of(4, 0)[1] + 1)
                    dve.wait_ge(evacuated[bank_of(4, 1)[0]], bank_of(4, 1)[1] + 1)
                else:
                    dve.wait_ge(evacuated[bank_of(3, 0)[0]], bank_of(3, 0)[1] + 1)
                    dve.wait_ge(evacuated[bank_of(3, 1)[0]], bank_of(3, 1)[1] + 1)
                link(v.tensor_tensor(flat(scr[:, :, :]), flat(aqk[:, w, :, :]), flat(aqk[:, w, :, :]), ALU.mult))
                link(v.tensor_reduce(qkm[:, w, :, :], scr[:, :, :].rearrange("p t (h n) -> p t h n", n=DH),
                                     AX_X, ALU.add))
            v.tensor_scalar(qkm[:, :, :, :], qkm[:, :, :, :], 1.0 / DH, EPS, ALU.mult, ALU.add).then_inc(qk_ms, 1)
            dve.wait_ge(qk_rms, 1)
            link(v.reciprocal(qkm[:, :, :, :], qkr[:, :, :, :]))
            for w in range(2):
                for tt in range(TT):
                    a3 = aqk[:, w, tt, :].rearrange("p (h n) -> p h n", n=DH)
                    ins = v.tensor_tensor(a3, a3, qkm[:, w, tt, :].unsqueeze(2).broadcast_to([P, NH, DH]), ALU.mult)
                ins.then_inc(qkn_ready, 1)
            low_pre(6)
            link(v.tensor_scalar(qn_w[:, :], qn_w[:, :], float(DH) ** -0.5, None, ALU.mult))
            dve.wait_ge(qz_zero, 2)
            qz = qTz[:, :, :].rearrange("p (b two) t -> p b two t", two=2)
            for m in range(2):
                dve.wait_ge(qk_turned, m + 1)
                for h in range(2):
                    rows = slice(DH * h, DH * h + DH)
                    v.tensor_scalar(qz[rows, 2 * m:2 * m + 2, h, :], bank(4 + m, 2)[rows, :, :], qn_w[rows, 0:1], None,
                                    ALU.mult).then_inc(qT_ready, 1)

            def row_max(h):
                dve.wait_ge(score_mm, h + 1)
                for tt in range(TT):
                    ins = v.tensor_reduce(nmx[:, h, tt:tt + 1], ps[:, 4 + h % 2, P * tt:P + 2 * P * tt], AX_X, ALU.max,
                                          negate=True)
                ins.then_inc(rowmax_ready, 1)

            def prob_scale(h):
                dve.wait_ge(exp_ready, 2 * h + 2)
                link(v.reciprocal(rsum[:, h, :], rsum[:, h, :]))
                for tt in range(TT):
                    pr = prob[:, h % 2, P * tt:P + 2 * P * tt]
                    ins = v.tensor_scalar(pr, pr, rsum[:, h, tt:tt + 1], None, ALU.mult)
                ins.then_inc(prob_ready, 1)

            def pair_out(b):
                dve.wait_ge(pv_mm, 2 * b + 2)
                o = bank(7, 2)[:, b % 2, :]
                link(v.tensor_copy(ya_hi[:, b, :], o))
                v.tensor_tensor(ya_lo[:, b, :], o, ya_hi[:, b, :].bitcast(F32), ALU.subtract).then_inc(yaT_ready, 1)

            def conv_in(m):
                b, _ = bank_of(7, m)
                dve.wait_ge(proj_done, first_bank[7] + m + 1)
                cb, cu = bank_of(6, m)
                dve.wait_ge(evacuated[cb], cu + 1)
                v.tensor_tensor(conv_u[:, 2 * m:2 * m + 2, 2:T + 2], ycT[:, 2 * m:2 * m + 2, :], bank(b, 2),
                                ALU.mult).then_inc(evacuated[b], 1)

            def conv_taps(m):
                b, u = bank_of(7, m)
                dve.wait_ge(evacuated[b], u + 1)
                for k in (2 * m, 2 * m + 1):
                    link(v.tensor_scalar(ycT[:, k, :], conv_u[:, k, 0:T], cw_sb[:, 0, k:k + 1], cb_sb[:, k:k + 1],
                                         ALU.mult, ALU.add))
                    for j in (1, 2):
                        link(v.scalar_tensor_tensor(out=ycT[:, k, :], in0=conv_u[:, k, j:j + T],
                                                    scalar=cw_sb[:, j, k:k + 1], in1=ycT[:, k, :], op0=ALU.mult,
                                                    op1=ALU.add))

            def conv_out(m):
                b, _ = bank_of(8, m)
                dve.wait_ge(proj_done, first_bank[8] + m + 1)
                y = ycT[:, 2 * m:2 * m + 2, :]
                hi = yc_hi[:, 2 * m:2 * m + 2, :]
                v.tensor_tensor(y, y, bank(b, 2), ALU.mult).then_inc(evacuated[b], 1)
                dve.wait_ge(evacuated[b], bank_of(8, m)[1] + 1)
                link(v.tensor_copy(hi, y))
                v.tensor_tensor(yc_lo[:, 2 * m:2 * m + 2, :], y, hi.bitcast(F32), ALU.subtract).then_inc(ycT_ready, 1)

            row_max(0)
            for h in range(1, NH):
                prob_scale(h - 1)
                if h % 2:
                    low_pre(7 + h // 2)
                if h in (2, 3):
                    conv_in(h - 2)
                if h in (4, 5):
                    conv_out(h - 4)
                if h >= 4 and h % 2 == 0:
                    pair_out(h // 2 - 2)
                row_max(h)
                if h in (2, 3):
                    conv_taps(h - 2)
            prob_scale(NH - 1)
            pair_out(2)
            low_pre(11)
            pair_out(3)

            def merged_low(m):
                dve.wait_ge(merged_hi_ready, m + 1)
                v.tensor_tensor(merged_lo[:, 2 * m:2 * m + 2, :], mergedT[:, 2 * m:2 * m + 2, :],
                                merged_hi[:, 2 * m:2 * m + 2, :].bitcast(F32),
                                ALU.subtract).then_inc(merged_lo_ready, 1)

            for n in range(3):
                for m in range(4):
                    if n == 2 and m == 3:
                        merged_low(0)
                        merged_low(1)
                    if m == 3:
                        low_pre(12 + 3 * n)
                    r = first_bank[11 + 3 * n] + m
                    sb, su = bank_of(9 + 3 * n + m // 2, m % 2)
                    dve.wait_ge(evacuated[sb], su + 1)
                    dve.wait_ge(proj_done, r + 1)
                    dst = flat(mergedT[:, 2 * m:2 * m + 2, :])
                    gate = flat(sig[n][:, 2 * m:2 * m + 2, :])
                    if n == 0:
                        v.tensor_tensor(dst, gate, bank(r % 4), ALU.mult).then_inc(evacuated[r % 4], 1)
                        dve.wait_ge(evacuated[r % 4], r // 4 + 1)
                        v.engine_nop().then_inc(branch_done, 1)
                    else:
                        v.tensor_tensor(scr[:, m % 2, :], gate, bank(r % 4), ALU.mult).then_inc(evacuated[r % 4], 1)
                        dve.wait_ge(evacuated[r % 4], r // 4 + 1)
                        v.tensor_tensor(dst, dst, scr[:, m % 2, :], ALU.add).then_inc(branch_done, 1)
                if n < 2:
                    low_pre(13 + 3 * n)
                    low_pre(14 + 3 * n)
            merged_low(2)
            merged_low(3)
            for half in range(2):
                for tt in range(TT):
                    if half == 0 and tt == 1:
                        low_pre(19)
                    r = first_bank[18 + half] + tt
                    dve.wait_ge(proj_done, r + 1)
                    xv = x_tok[:, tt, half * C:(half + 1) * C]
                    v.tensor_tensor(xv, xv, bank(r % 4), ALU.add).then_inc(x1_ready, 1)
            dve.wait_ge(x1_ready, 4)
            norm_stats(x_tok, xn, ms2_ready)
            norm_apply(x_tok, xn, rms2_ready, h2_ready)
            for kp in range(2, 4):
                dve.wait_ge(h2_turned, kp + 1)
                for k in (2 * kp, 2 * kp + 1):
                    v.tensor_scalar(h2T[:, k, :], bank(4 + kp, 2)[:, k % 2, :], g_ffn[:, k:k + 1], None,
                                    ALU.mult).then_inc(hT_dve, 1)

            dve.wait_ge(router_mm, 1)
            lg = ps[:, 0, 0:72].rearrange("p (t n) -> p t n", t=TT)
            v.tensor_copy(lgp[:, :, 0:NG], lg[:, :, 0:NG])
            link(v.tensor_copy(le[:, :, :], lg[:, :, NG:NG + NE]))
            for tt in range(TT):
                link(v.max(mg8[:, tt, :], lgp[:, tt, :]))
                link(v.max_index(ig8[:, tt, :], mg8[:, tt, :], lgp[:, tt, :]))
            v.tensor_scalar(rt[:, :, 0:1], mg8[:, :, 0:1], -1.0, None, ALU.mult).then_inc(nmax_ready, 1)
            link(v.tensor_copy(rt[:, :, 4:5], ig8[:, :, 0:1]))
            for tt in range(TT):
                link(v.tensor_scalar(rt[:, tt, 12:16], iota_f[:, 0:NG], rt[:, tt, 4:5], None, ALU.is_equal))
                link(v.tensor_tensor(lsel[:, tt, :].rearrange("p (g e) -> p g e", e=EPG),
                                     le[:, tt, :].rearrange("p (g e) -> p g e", e=EPG),
                                     rt[:, tt, 12:16].unsqueeze(2).broadcast_to([P, NG, EPG]), ALU.mult))
                link(v.tensor_reduce(les[:, tt, :], lsel[:, tt, :].rearrange("p (g e) -> p e g", e=EPG), AX_X, ALU.add))
                link(v.max(me8[:, tt, :], les[:, tt, :]))
                link(v.max_index(ie8[:, tt, :], me8[:, tt, :], les[:, tt, :]))
            v.tensor_tensor(rt[:, :, 2:3], me8[:, :, 1:2], me8[:, :, 0:1], ALU.subtract).then_inc(e2in_ready, 1)
            link(v.tensor_copy(rt[:, :, 5:7], ie8[:, :, 0:2]))
            link(v.scalar_tensor_tensor(out=rt[:, :, 5:7], in0=rt[:, :, 4:5].broadcast_to([P, TT, 2]), scalar=float(EPG),
                                        in1=rt[:, :, 5:7], op0=ALU.mult, op1=ALU.add))
            for tt in range(TT):
                v.tensor_scalar(e1h[:, tt, :], iota_f[:, :], rt[:, tt, 5:6], None, ALU.is_equal)
                link(v.tensor_scalar(e2h[:, tt, :], iota_f[:, :], rt[:, tt, 6:7], None, ALU.is_equal))
            link(v.tensor_tensor(eall[:, :, :], e1h[:, :, :], e2h[:, :, :], ALU.add))
            v.tensor_copy(eall_bf[:, :, :], eall[:, :, :]).then_inc(assign_ready, 1)
            for tt in range(TT):
                link(v.tensor_tensor_scan(epre[:, tt, :], reset[:, 1:1 + NE], eall[:, tt, :], 0.0, ALU.mult, ALU.add))
            v.tensor_tensor(epre_bf[:, :, :], epre[:, :, :], eall[:, :, :], ALU.subtract).then_inc(assign_ready, 1)
            dve.wait_ge(pos_mm, 1)
            for tt in range(TT):
                for k, eh in enumerate((e1h, e2h)):
                    link(v.tensor_tensor_reduce(eh[:, tt, :], eh[:, tt, :], ps[:, 1, tt * NE:(tt + 1) * NE], 1.0, 0.0,
                                                ALU.mult, ALU.add, slotf[:, tt, k:k + 1]))
            dve.wait_ge(iota_ready, 1)
            for tt in range(TT):
                link(v.tensor_scalar(perm[:, tt, :], iota_s[:, :], slotf[:, tt, 0:1], None, ALU.is_equal))
                v.scalar_tensor_tensor(out=perm[:, tt, :], in0=iota_s[:, :], scalar=slotf[:, tt, 1:2],
                                       in1=perm[:, tt, :], op0=ALU.is_equal, op1=ALU.add).then_inc(perm_ready, 1)
            link(v.tensor_reduce(cntr[:, 0:1], ps[0:1, 1, 3 * NE:4 * NE], AX_X, ALU.max))
            link(v.tensor_scalar(cntr[:, 1:2], cntr[:, 0:1], float(WIN), 1.0, ALU.is_gt, ALU.add))
            for r in range(2, MAXWIN):
                link(v.scalar_tensor_tensor(out=cntr[:, r:r + 1], in0=cntr[:, 0:1], scalar=float(WIN * r),
                                            in1=cntr[:, r - 1:r], op0=ALU.is_gt, op1=ALU.add))
            for p in range(MAXWIN):
                link(v.tensor_scalar(cntr[:, 4 + p:5 + p], cntr[:, MAXWIN - 1:MAXWIN], float(WIN), -float(WIN * (p + 1)),
                                     ALU.mult, ALU.add))
                link(v.tensor_scalar(cntr[:, 4 + p:5 + p], cntr[:, 4 + p:5 + p], 0.0, None, ALU.max))
                link(v.tensor_scalar(offf[:, p * NE:(p + 1) * NE], ps[0:1, 1, 2 * NE:3 * NE], cntr[:, 4 + p:5 + p],
                                     float(SLOTS), ALU.add, ALU.min))
            link(v.tensor_copy(off_tab[:, :], offf[:, :]))
            v.tensor_copy(npass[:, :], cntr[:, MAXWIN - 1:MAXWIN]).then_inc(route_ready, 1)
            link(v.tensor_copy(slot_u[:, :], flat(slotf[:, :, :])))
            for k in range(1, KD, 2):
                dve.wait_ge(gather_mm, k + 1)
                v.tensor_scalar(xs[:, k, 0:SLOTS], bank(2 + k % 4), g_ffn[:, k:k + 1], None, ALU.mult).then_inc(xs_dve, 1)
            dve.wait_ge(gexp_ready, 2)
            dve.wait_ge(e2_ready, 1)
            link(v.tensor_scalar(rt[:, :, 7:8], rt[:, :, 3:4], 1.0, None, ALU.add))
            link(v.tensor_tensor(rt[:, :, 7:8], rt[:, :, 7:8], rt[:, :, 1:2], ALU.mult))
            link(v.reciprocal(wts[:, :, 0:1], rt[:, :, 7:8]))
            link(v.tensor_tensor(wts[:, :, 1:2], wts[:, :, 0:1], rt[:, :, 3:4], ALU.mult))

            passes = dve.value_load(npass[0:1, 0:1], min_val=1, max_val=MAXWIN)
            dve.wait_ge(route_ready, 1)
            dve.sem_inc(gu_free, 4)
            dve.sem_inc(y_ready, 1)

            def low_part(p, i, q, cs):
                s = slot_of(q)
                for c in cs:
                    if c in POOL_LO:
                        continue
                    dve.wait_ge(hi_ready, PER_PASS * CHUNKS * p + RING * CHUNKS * i + CHUNKS * q + c + 1)
                    v.tensor_tensor(ring_lo[s][:, chunk(c)], ring[s][:, chunk(c)], hi_buf(q, c).bitcast(F32),
                                    ALU.subtract).then_inc(lo_ready, 1)

            def gu_fold(p, e, b):
                dve.wait_ge(gu_lo_out, 2 * NE * p + 2 * e + 1)
                v.tensor_tensor(g_sum[:, :], g_lo[:, :], ps[0:WIN, 2 * b, :], ALU.add).then_inc(gu_free, 1)
                dve.wait_ge(gu_lo_out, 2 * NE * p + 2 * e + 2)
                v.tensor_tensor(u_sum[:, :], u_lo[:, :], ps[0:WIN, 2 * b + 1, :], ALU.add).then_inc(gu_free, 1)

            def gated(p, e):
                dve.wait_ge(silu_ready, NE * p + e + 1)
                dve.wait_ge(gu_free, 2 * NE * p + 2 * e + 6)
                v.tensor_tensor(h_tok[:, :], g_act[:, :], u_sum[:, :], ALU.mult).then_inc(h_ready, 1)

            def he_low(p, e):
                dve.wait_ge(he_hi, NE * p + e + 1)
                v.tensor_tensor(he[:, :, WIN:2 * WIN], ps[:, 6, 0:KC * WIN].rearrange("p (k n) -> p k n", n=WIN),
                                he[:, :, 0:WIN].bitcast(F32), ALU.subtract).then_inc(he_lo, 1)

            def y_fold(p, e, b):
                dve.wait_ge(y_lo_out, NE * p + e + 1)
                dve.wait_ge(y_free, NE * p + e + 1)
                v.tensor_tensor(y_tok[:, b, :], y_lo[:, :], flat(ps[0:WIN, 4:6, :]), ALU.add).then_inc(y_ready, 1)

            def step(p, e, i, q, b, y_too):
                low_part(p, i, q, (0,))
                gu_fold(p, e - 1, 1 - b)
                low_part(p, i, q, (1,))
                gated(p, e - 1)
                low_part(p, i, q, (2,))
                low_part(p, i, q, (3,))
                low_part(p, i, q + 1, (0,))
                if y_too:
                    y_fold(p, e - 2, b)
                low_part(p, i, q + 1, (1, 2, 3))
                low_part(p, i, q + 2, (0,))
                he_low(p, e - 1)
                low_part(p, i, q + 2, (1, 2, 3))

            with dve.Fori(0, passes) as p:
                low_part(p, 0, 0, (0, 1, 2, 3))
                low_part(p, 0, 1, (0, 1, 2, 3))
                step(p, 1, 0, 2, 1, False)
                with dve.Fori(0, NE // 2 - 1) as i:
                    for s in range(2):
                        step(p, 2 * i + (2 + s), i, 5 + 3 * s, s, True)
                gu_fold(p, NE - 1, 1)
                gated(p, NE - 1)
                low_part(p, 0, PER_PASS - 1, (0,))
                y_fold(p, NE - 2, 0)
                he_low(p, NE - 1)
                low_part(p, 0, PER_PASS - 1, (1, 2, 3))
                y_fold(p, NE - 1, 1)
            for tt in range(TT):
                for k in range(2):
                    j = 2 * tt + k
                    dve.wait_ge(back_in[j], 16)
                    ins = v.scalar_tensor_tensor(out=x_tok[:, tt, :], in0=y_back[:, j, :], scalar=wts[:, tt, k:k + 1],
                                                 in1=x_tok[:, tt, :], op0=ALU.mult, op1=ALU.add)
                    if k == 0:
                        link(ins)
                ins.then_inc(fin_ready, 1)


_INS = ['x', 'rel_bias_table', 'norm_mix', 'w_in', 'conv_w', 'conv_b', 'q_norm', 'k_norm', 'w_gla_alpha',
        'b_gla_alpha', 'gla_out_norm', 'w_merge_gate', 'w_branch', 'w_out', 'norm_ffn', 'w_router_group',
        'b_router_group', 'w_router_expert', 'b_router_expert', 'w_expert_gate', 'w_expert_up', 'w_expert_down']


def kernel(**inputs):
    import concourse.bacc as _bacc
    from concourse.bass_utils import run_bass_kernel_spmd as _run

    nc = _bacc.Bacc("TRN2", target_bir_lowering=False, num_devices=1)
    arrays, args = {}, []
    for name in _INS:
        a = np.ascontiguousarray(inputs[name])
        arrays[f"in_{name}"] = a
        args.append(nc.dram_tensor(f"in_{name}", a.shape, mybir.dt.from_np(a.dtype), kind="ExternalInput").ap())
    out = nc.dram_tensor("out_x", (1, T, D), F32, kind="ExternalOutput").ap()
    hybrid_block(nc, *args, out)
    r = _run(nc, [arrays], core_ids=[0])
    return r.results[0]["out_x"]
```

```python
import math
from contextlib import ExitStack

import numpy as np

import concourse.bass as bass
from concourse import mybir

F32 = mybir.dt.float32
F32R = mybir.dt.float32r
BF16 = mybir.dt.bfloat16
I32 = mybir.dt.int32
U32 = mybir.dt.uint32
ALU = mybir.AluOpType
ACT = mybir.ActivationFunctionType
AX_X = mybir.AxisListType.X

P = 128
T = 256
TT = T // P
D = 1024
KD = D // P
C = 512
KC = C // P
EPS = 1e-6
NH = 8
DH = 64
GH = 4
GK = 64
GV = 128
CH = 64
TEMP = 16.0
NG = 4
EPG = 8
NE = NG * EPG
TOPK = 2
SLOTS = T * TOPK
WIN = 64
MAXWIN = T // WIN
SPAD = SLOTS + WIN
BUCKETS = 32
MAXDIST = 128
NEG = -1e30

PRE_RING = 5
RING = 6
SLOT = KD * C
NPRE = 20
PER_PASS = 3 * NE
N_EARLY = 2
N_SMALL = 14
CHUNK_T = 2
CHUNKS = KD // CHUNK_T
CW = CHUNK_T * C
HI_BUFS = 6
POOL_LO = (3,)
FREED_SEED = RING * CHUNKS


def bucket_onehot():
    n = T - 1 - np.arange(T)
    exact = BUCKETS // 2
    scaled = np.log(np.maximum(n, exact).astype(np.float32) / exact) / math.log(MAXDIST / exact)
    large = np.minimum(exact + (scaled * (BUCKETS - exact)).astype(np.int32), BUCKETS - 1)
    b = np.where(n < exact, n, large)
    return (b[None, :] == np.arange(BUCKETS)[:, None]).astype(np.float32)


def flat(v):
    names = "abcd"[:len(v.shape) - 1]
    return v.rearrange(f"p {' '.join(names)} -> p ({' '.join(names)})")


def hybrid_block(nc, x, rel_bias_table, norm_mix, w_in, conv_w, conv_b, q_norm, k_norm, w_gla_alpha,
                 b_gla_alpha, gla_out_norm, w_merge_gate, w_branch, w_out, norm_ffn, w_router_group,
                 b_router_group, w_router_expert, b_router_expert, w_expert_gate, w_expert_up,
                 w_expert_down, out):
    ctx = ExitStack()
    top = [16512]

    def place(name, shape, dt, at=None):
        size = int(np.prod(shape[1:])) * mybir.dt.size(dt)
        off = top[0] if at is None else at
        if at is None:
            top[0] = off + (size + 31) // 32 * 32
        assert off + size <= 229344, (name, off + size)
        return nc.alloc_sbuf_tensor_at(name, list(shape), dt, offset=off)

    def sem(name):
        return ctx.enter_context(nc.semaphore(name))

    with ctx:
        ctx.enter_context(nc.allow_non_contiguous_dma("small vectors land one element per partition"))
        onehot_dram = nc.inline_tensor(bucket_onehot(), "bucket_onehot").ap()
        bias_dram = nc.dram_tensor("bias_by_distance", (NH, 384), F32, kind="Internal")
        y_rows = nc.dram_tensor("y_rows", ((NE + 2) * WIN, D), F32, kind="Internal").ap()

        ring_at, ring, ring_lo = [], [], []

        def ring_slot(i, at):
            ring_at.append(at)
            ring.append(place(f"ring{i}", [P, SLOT], F32, at=at))
            ring_lo.append(place(f"ring_lo{i}", [P, SLOT], F32R, at=at))

        for i in range(PRE_RING):
            ring_slot(i, top[0])
            top[0] += 4 * SLOT
        w_hi = [place(f"w_hi{c}", [P, CW], F32R) for c in range(CHUNKS)]
        x_tok = place("x_tok", [P, TT, D], F32)
        xn_at = top[0]
        xn = place("xn_merged", [P, TT, D], F32)
        merged_lo = place("merged_lo", [P, KD, T], F32R, at=xn_at)
        xn_lo = place("xn_lo", [P, TT, D], F32R, at=xn_at)
        ident = place("ident", [P, P], F32)
        antid = place("antid", [P, P], F32)
        ones_bf = place("ones_bf", [P, P], BF16)
        tri_bf = place("tri_bf", [P, P], BF16)
        mergedT = xn[:, :, :].rearrange("p a b -> p (a b)").rearrange("p (k t) -> p k t", k=KD)
        g_mix = place("g_mix", [P, KD], F32)
        g_ffn = place("g_ffn", [P, KD], F32)
        cw_sb = place("cw_sb", [P, 3, KC], F32)
        cb_sb = place("cb_sb", [P, KC], F32)
        qn_w = place("qn_w", [P, 1], F32)
        kn_w = place("kn_w", [P, 1], F32)
        b_al = place("b_al", [P, 2], F32)
        on_w = place("on_w", [P, 1], F32)
        w_al = place("w_al", [16, 256], F32)
        z_at = top[0]
        zT = place("zT", [16, T], F32)
        lgT = place("lgT", [NG + NE, T], F32, at=z_at)
        pick_at = z_at

        def pick_place(name, n, dt):
            nonlocal pick_at
            at, pick_at = pick_at, pick_at + (4 * n + 31) // 32 * 32
            return place(name, [P, n], dt, at=at)

        rem = pick_place("rem", MAXWIN * TT * TOPK, F32)
        rowf = pick_place("rowf", MAXWIN * TT * TOPK, F32)
        row_u = pick_place("row_u", MAXWIN * TT * TOPK, U32)
        inside = pick_place("inside", MAXWIN * TT * TOPK, F32)
        w_pass = pick_place("w_pass", MAXWIN * TT * TOPK, F32)
        startf = pick_place("startf", TT * TOPK, F32)
        placef = pick_place("placef", TT * TOPK, F32)
        row_now = pick_place("row_now", TT * TOPK, U32)
        w_now = pick_place("w_now", TT * TOPK, F32)
        table = place("table", [BUCKETS, NH], F32)
        w_z_at = top[0]
        w_z = place("w_z", [P, KD, 16], F32)
        w_z_hi = place("w_z_hi", [P, KD, 16], F32R)
        w_z_lo = place("w_z_lo", [P, KD, 16], F32R, at=w_z_at)
        w_r = place("w_r", [P, KD, NG + NE], F32)
        b_r = place("b_r", [P, NG + NE], F32)
        stat = place("stat", [P, 64], F32)
        reset = place("reset", [P, T], F32)
        qkm = place("qkm", [P, 2, TT, NH], F32)
        qkr = place("qkr", [P, 2, TT, NH], F32)
        nmx = place("nmx", [P, NH, TT], F32)
        rsum = place("rsum", [P, NH, TT], F32)
        lgp = place("lgp", [P, TT, 8], F32)
        le = place("le", [P, TT, NE], F32)
        mg8 = place("mg8", [P, TT, 8], F32)
        ig8 = place("ig8", [P, TT, 8], U32)
        me8 = place("me8", [P, TT, 8], F32)
        ie8 = place("ie8", [P, TT, 8], U32)
        rt = place("rt", [P, TT, 16], F32)
        les = place("les", [P, TT, 8], F32)
        lsel = place("lsel", [P, TT, NE], F32)
        e1h = place("e1h", [P, TT, NE], F32)
        e2h = place("e2h", [P, TT, NE], F32)
        eall = place("eall", [P, TT, NE], F32)
        epre = place("epre", [P, TT, NE], F32)
        eall_bf = place("eall_bf", [P, TT, NE], BF16)
        epre_bf = place("epre_bf", [P, TT, NE], BF16)
        iota_f = place("iota_f", [P, NE], F32)
        slotf = place("slotf", [P, TT, 2], F32)
        wts = place("wts", [P, TT, 2], F32)
        offf = place("offf", [1, MAXWIN * NE + 1], F32)
        off_tab = place("off_tab", [1, MAXWIN * NE + 1], I32)
        cntr = place("cntr", [1, 8], F32)
        npass = place("npass", [1, 1], I32)
        region = top[0]

        def here(name, shape, dt):
            nonlocal_at = here_at[0]
            here_at[0] += (int(np.prod(shape[1:])) * mybir.dt.size(dt) + 31) // 32 * 32
            return place(name, shape, dt, at=nonlocal_at)

        here_at = [region]
        sig0 = here("sig0", [P, KD, T], F32)
        onehot = place("onehot", [BUCKETS, T], F32, at=region)
        bias_row = place("bias_row", [NH, 384], F32, at=region + 4 * T)
        yc_at = here_at[0]
        ycT = here("ycT", [P, KC, T], F32)
        yc_lo = place("yc_lo", [P, KC, T], F32R, at=yc_at)
        conv_u = here("conv_u", [P, KC, T + 2], F32)
        hT_at = here_at[0]
        hT_hi = here("hT_hi", [P, KD, T], F32R)
        h2T_at = here_at[0]
        hT_lo = here("hT_lo", [P, KD, T], F32R)
        h2T = place("h2T", [P, KD, T], F32, at=h2T_at)
        merged_hi = place("merged_hi", [P, KD, T], F32R, at=hT_at)
        aqk = here("aqk", [P, 2, TT, C], F32)
        q_at = here_at[0]
        qTz = here("qTz", [P, NH, T], F32)
        sig = (sig0, place("sig1", [P, KD, T], F32, at=q_at), sig0)
        kT = here("kT", [P, KC, T], F32)
        av = here("av", [P, TT, C], F32)
        gqk = here("gqk", [P, 4, T], F32)
        att_at = here_at[0]
        attm = here("attm", [P, 8, P], F32)
        gv_at = here_at[0]
        gv = here("gv", [P, TT, C], F32)
        gr_at = here_at[0]
        gr = here("gr", [P, TT, C], F32)
        kdn = here("kdn", [P, TT, 256], F32)
        sbd_at = here_at[0]
        sbd = here("sbd", [P, 3, 2, 256], F32)
        scr_at = here_at[0]
        scr = here("scr", [P, 2, C], F32)
        la, e_pos, e_neg, e_rest = (qTz[:, 2 * i:2 * i + 2, :] for i in range(4))
        bias_h = gqk
        yc_hi = place("yc_hi", [P, KC, T], F32R, at=scr_at)
        ya_hi = place("ya_hi", [P, KC, T], F32R, at=att_at)
        ya_lo = place("ya_lo", [P, KC, T], F32R, at=gr_at)
        yg_hi = place("yg_hi", [P, KC, T], F32R, at=gv_at)
        yg_lo = place("yg_lo", [P, KC, T], F32R, at=sbd_at)
        prob = aqk[:, 0, :, :].rearrange("p a b -> p (a b)")[:, 0:768].rearrange("p (a b) -> p a b", a=2)
        probT = aqk[:, 1, :, :].rearrange("p a b -> p (a b)")[:, 0:768].rearrange("p (a b) -> p a b", a=2)

        here_at = [region]
        ring_slot(PRE_RING, here_at[0])
        here_at[0] += 4 * SLOT
        xs = here("xs", [P, KD, SPAD], F32)
        w_hi += [here(f"w_hi{c}", [P, CW], F32R) for c in range(CHUNKS, HI_BUFS)]
        xn_hi = place("xn_hi", [P, TT, D], F32R, at=here_at[0])
        xe = [here(f"xe{b}", [P, KD, 2 * WIN], F32R) for b in range(2)]
        g_lo = here("g_lo", [WIN, C], F32)
        u_lo = here("u_lo", [WIN, C], F32)
        g_sum = here("g_sum", [WIN, C], F32)
        u_sum = here("u_sum", [WIN, C], F32)
        g_act = here("g_act", [WIN, C], F32)
        h_tok = here("h_tok", [WIN, C], F32)
        he = here("he", [P, KC, 2 * WIN], F32R)
        y_lo_at = here_at[0]
        y_lo = here("y_lo", [WIN, D], F32)
        y_at = here_at[0]
        y_tok = here("y_tok", [WIN, 2, D], F32)
        iota_s = place("iota_s", [P, SLOTS], F32, at=y_lo_at)
        perm = place("perm", [P, TT, SLOTS], F32R, at=y_at)
        y_back = (place("y_back0", [P, TOPK, D], F32, at=xn_at), here("y_back1", [P, TOPK, D], F32))

        ps = ctx.enter_context(nc.psum_tensor("ps", [P, 8, 512], F32))

        def bank(b, a=None):
            v = ps[:, b, :]
            return v if a is None else v.rearrange("p (a b) -> p a b", a=a)

        x_in = [sem(f"x_in{i}") for i in range(TT)]
        gain_in = sem("gain_in")
        alpha_in = sem("alpha_in")
        early_in = sem("early_in")
        small_in = sem("small_in")
        wz_in = sem("wz_in")
        landed = [sem(f"landed{s}") for s in range(PRE_RING)]
        chunk_in = [[sem(f"chunk_in{s}_{c}") for c in range(CHUNKS)] for s in range(RING)]
        consts = sem("consts")
        v_chain = sem("v_chain")
        a_chain = sem("a_chain")
        g_chain = sem("g_chain")
        ms_ready = sem("ms_ready")
        rms_ready = sem("rms_ready")
        xn_ready = sem("xn_ready")
        hT_turned = sem("hT_turned")
        biasrow_mm = sem("biasrow_mm")
        biasrow_ready = sem("biasrow_ready")
        bias_stored = sem("bias_stored")
        bias_in = [sem(f"bias_in{i}") for i in range(4)]
        proj_done = sem("proj_done")
        evacuated = [sem(f"evacuated{b}") for b in range(4)]
        wpre_hi = sem("wpre_hi")
        wpre_lo = sem("wpre_lo")
        chunk_done = sem("chunk_done")
        wz_hi_ready = sem("wz_hi_ready")
        wz_lo_ready = sem("wz_lo_ready")
        hT_lo_ready = sem("hT_lo_ready")
        yg_hi_ready = sem("yg_hi_ready")
        ycT_ready = sem("ycT_ready")
        xn_hi_ready = sem("xn_hi_ready")
        xn_lo_ready = sem("xn_lo_ready")
        merged_hi_ready = sem("merged_hi_ready")
        merged_lo_ready = sem("merged_lo_ready")
        hT_act = sem("hT_act")
        hT_dve = sem("hT_dve")
        xs_act = sem("xs_act")
        xs_dve = sem("xs_dve")
        freed = sem("freed")
        storing = sem("storing")
        gathering = sem("gathering")
        picked = sem("picked")
        picks = sem("picks")
        z_mm = sem("z_mm")
        z_ready = sem("z_ready")
        alpha_mm = sem("alpha_mm")
        sigmin_ready = sem("sigmin_ready")
        softplus_ready = sem("softplus_ready")
        cum_ready = sem("cum_ready")
        decay_ready = sem("decay_ready")
        gla_in_ready = sem("gla_in_ready")
        kd_turned = sem("kd_turned")
        kdn_ready = sem("kdn_ready")
        att_mm = sem("att_mm")
        att_copied = sem("att_copied")
        att_ready = sem("att_ready")
        kv_mm = sem("kv_mm")
        state_ready = sem("state_ready")
        sbd_zero = sem("sbd_zero")
        o_mm = sem("o_mm")
        o_sq = sem("o_sq")
        o_ms = sem("o_ms")
        o_rms = sem("o_rms")
        ygla_ready = sem("ygla_ready")
        yg_turned = sem("yg_turned")
        ygT_ready = sem("ygT_ready")
        qk_ms = sem("qk_ms")
        qk_rms = sem("qk_rms")
        qkn_ready = sem("qkn_ready")
        qz_zero = sem("qz_zero")
        qk_turned = sem("qk_turned")
        qT_ready = sem("qT_ready")
        kT_ready = sem("kT_ready")
        score_mm = sem("score_mm")
        rowmax_ready = sem("rowmax_ready")
        exp_ready = sem("exp_ready")
        prob_ready = sem("prob_ready")
        prob_turned = sem("prob_turned")
        probT_ready = sem("probT_ready")
        pv_mm = sem("pv_mm")
        yaT_ready = sem("yaT_ready")
        branch_done = sem("branch_done")
        x1_ready = sem("x1_ready")
        ms2_ready = sem("ms2_ready")
        rms2_ready = sem("rms2_ready")
        h2_ready = sem("h2_ready")
        h2_turned = sem("h2_turned")
        router_mm = sem("router_mm")
        logits_ready = sem("logits_ready")
        nmax_ready = sem("nmax_ready")
        gexp_ready = sem("gexp_ready")
        e2in_ready = sem("e2in_ready")
        e2_ready = sem("e2_ready")
        assign_ready = sem("assign_ready")
        pos_mm = sem("pos_mm")
        perm_ready = sem("perm_ready")
        route_ready = sem("route_ready")
        gather_mm = sem("gather_mm")
        iota_ready = sem("iota_ready")
        first_high = sem("first_high")
        first_window = sem("first_window")
        xe_high = sem("xe_high")
        xe_ready = sem("xe_ready")
        hi_ready = sem("hi_ready")
        lo_ready = sem("lo_ready")
        lo_ready_pool = sem("lo_ready_pool")
        gu_lo_out = sem("gu_lo_out")
        gu_free = sem("gu_free")
        silu_ready = sem("silu_ready")
        h_ready = sem("h_ready")
        h_turned = sem("h_turned")
        he_hi = sem("he_hi")
        he_lo = sem("he_lo")
        y_lo_out = sem("y_lo_out")
        y_ready = sem("y_ready")
        y_stored = [sem(f"y_stored{b}") for b in range(2)]
        back_in = [sem(f"back_in{j}") for j in range(2 * TT)]
        fin_ready = sem("fin_ready")
        stored = sem("stored")

        w_in_v = w_in[0].rearrange("(p k) n -> p k n", k=KD)
        w_out_v = w_out[0].rearrange("(k p) n -> p k n", p=P)
        cols = [3072, 3584, 4096, 1536, 2048, 2560, 512, 1024, 0]
        pre = [("in", c) for c in cols]
        for n in range(3):
            pre += [("gate", n, 0), ("gate", n, 1), ("branch", n)]
        pre += [("out", 0), ("out", 1)]
        first_bank = []
        at = 0
        for s in pre:
            first_bank.append(at)
            at += 4 if s[0] == "branch" else 2
        first_bank.append(at)
        assert len(pre) == NPRE

        def pre_source(g):
            kind = pre[g]
            if kind[0] == "in":
                return w_in_v[:, :, kind[1]:kind[1] + C], C
            if kind[0] == "gate":
                return w_merge_gate[0, kind[1]].rearrange("(p k) n -> p k n", k=KD)[:, :, kind[2] * C:(kind[2] + 1) * C], C
            if kind[0] == "branch":
                return w_branch[0, kind[1]].rearrange("(k p) n -> p k n", p=P), D
            return w_out_v[:, :, kind[1] * C:(kind[1] + 1) * C], C

        wg_v = w_expert_gate[0].rearrange("e (p k) n -> e p (k n)", k=KD)
        wu_v = w_expert_up[0].rearrange("e (p k) n -> e p (k n)", k=KD)
        wd_v = w_expert_down[0].rearrange("e (k p) n -> e p k n", p=P)

        def slot_of(q):
            return q % RING

        def hi_buf(q, c):
            return w_hi[(CHUNKS * q + c) % HI_BUFS][:, :]

        def after_slots(p, n):
            return PER_PASS * CHUNKS * p + CHUNKS * n + FREED_SEED

        def bank_of(g, m):
            r = first_bank[g] + m
            return r % 4, r // 4

        def w3(s):
            return ring[s][:, :].rearrange("p (k n) -> p k n", n=C)

        def w4(s):
            return ring[s][:, :].rearrange("p (k n) -> p k n", n=D)

        def chunk(c):
            return slice(CW * c, CW * (c + 1))

        block = ctx.enter_context(nc.Block())

        @block.sync
        def _(sp):
            for tt in range(TT):
                sp.dma_start(x_tok[:, tt, :], x[0, tt * P:(tt + 1) * P, :]).then_inc(x_in[tt], 16)

            def load_expert(kind, e, q, p, i, first=False):
                s = slot_of(q)
                for c in range(CHUNKS):
                    if not first:
                        sp.wait_ge(freed, (PER_PASS * CHUNKS) * p + RING * CHUNKS * i + CHUNKS * (q - RING) + c + 1
                                   + FREED_SEED)
                    elif c == 0 and q < PRE_RING:
                        sp.wait_ge(proj_done, first_bank[NPRE + q - PRE_RING + 1])
                    elif c == 0:
                        sp.wait_ge(branch_done, 12)
                    if kind == "d":
                        src = wd_v[bass.ds(e, 1), :, c, :]
                    else:
                        src = (wg_v if kind == "g" else wu_v)[bass.ds(e, 1), :, chunk(c)]
                    sp.dma_start(ring[s][:, chunk(c)], src.rearrange("e p n -> (e p) n")).then_inc(chunk_in[s][c], 16)

            def start_of_pass(p, first):
                load_expert("g", 0, 0, p, 0, first)
                load_expert("u", 0, 1, p, 0, first)
                load_expert("g", 1, 2, p, 0, first)
                load_expert("u", 1, 3, p, 0, first)
                load_expert("d", 0, 4, p, 0, first)
                load_expert("g", 2, 5, p, 0, first)

            def pair(p, i, e):
                for s in range(2):
                    load_expert("u", e + (2 + s), 6 + 3 * s, p, i)
                    load_expert("d", e + (1 + s), 7 + 3 * s, p, i)
                    if isinstance(e, int) and s == 1:
                        load_expert("d", NE - 1, 11, p, i)
                    else:
                        load_expert("g", e + (3 + s), 8 + 3 * s, p, i)

            for g in range(NPRE):
                if g >= PRE_RING:
                    sp.wait_ge(proj_done, first_bank[g - PRE_RING + 1])
                src, n = pre_source(g)
                s = g % PRE_RING
                sp.dma_start(ring[s][:, :].rearrange("p (k n) -> p k n", n=n), src).then_inc(landed[s], 16)
                if g == 0:
                    sp.wait_ge(early_in, 16 * N_EARLY)
                    sp.dma_start(w_z[:, :, :], w_in_v[:, :, 4608:4624]).then_inc(wz_in, 16)
            start_of_pass(0, True)
            sp.wait_ge(route_ready, 1)
            passes = sp.value_load(npass[0:1, 0:1], min_val=1, max_val=MAXWIN)
            with sp.Fori(0, passes) as p:
                with sp.If(p > 0):
                    start_of_pass(p, False)
                with sp.Fori(0, NE // 2 - 2) as i:
                    pair(p, i, 2 * i)
                pair(p, NE // 2 - 2, NE - 4)
            for tt in range(TT):
                sp.wait_ge(fin_ready, passes * (TT * TOPK) + TOPK * (tt + 1))
                sp.dma_start(out[0, tt * P:(tt + 1) * P, :], x_tok[:, tt, :]).then_inc(stored, 16)
            sp.wait_ge(stored, 16 * TT)

        @block.gpsimd
        def _(pool):
            g = nc.gpsimd
            steps = [0]

            def link(ins):
                steps[0] += 1
                ins.then_inc(g_chain, 1)
                pool.wait_ge(g_chain, steps[0])

            g.memset(ident[:, :], 0.0)
            g.memset(antid[:, :], 0.0)
            g.memset(ones_bf[:, :], 1.0)
            g.memset(tri_bf[:, :], 1.0)
            g.memset(reset[:, :], 1.0)
            g.memset(conv_u[:, :, 0:2], 0.0)
            link(g.memset(bias_row[:, T:384], NEG))
            g.affine_select(out=ident[:, :], in_=ident[:, :], compare_op=ALU.not_equal, fill=1.0, base=0,
                            pattern=[[-1, P]], channel_multiplier=1).then_inc(consts, 1)
            g.affine_select(out=antid[:, :], in_=antid[:, :], compare_op=ALU.not_equal, fill=1.0, base=-(P - 1),
                            pattern=[[1, P]], channel_multiplier=1).then_inc(consts, 1)
            g.affine_select(out=tri_bf[:, :], in_=tri_bf[:, :], compare_op=ALU.is_gt, fill=0.0, base=0,
                            pattern=[[1, P]], channel_multiplier=-1).then_inc(consts, 1)
            g.memset(reset[:, :].rearrange("p (c n) -> p c n", n=CH)[:, :, 0:1], 0.0).then_inc(consts, 1)
            g.iota(iota_f[:, :], pattern=[[1, NE]], base=0, channel_multiplier=0,
                   allow_small_or_imprecise_dtypes=True).then_inc(consts, 1)
            g.memset(sbd[:, :, :, :], 0.0).then_inc(sbd_zero, 1)
            g.memset(offf[:, MAXWIN * NE:], 0.0)
            g.memset(lgp[:, :, NG:], -3e38).then_inc(consts, 1)

            smalls = [
                (qn_w[0:DH, :], q_norm[0].rearrange("(p a) -> p a", a=1)),
                (qn_w[DH:P, :], q_norm[0].rearrange("(p a) -> p a", a=1)),
                (kn_w[0:DH, :], k_norm[0].rearrange("(p a) -> p a", a=1)),
                (kn_w[DH:P, :], k_norm[0].rearrange("(p a) -> p a", a=1)),
                (on_w[:, :], gla_out_norm[0].rearrange("(p a) -> p a", a=1)),
                (cb_sb[:, :], conv_b[0].rearrange("(k p) -> p k", p=P)),
                (g_ffn[:, :], norm_ffn[0].rearrange("(p k) -> p k", k=KD)),
                (b_r[:, 0:NG], b_router_group.broadcast_to([P, NG])),
                (b_r[:, NG:NG + NE], b_router_expert.broadcast_to([P, NE])),
                (w_r[:, :, 0:NG], w_router_group[0].rearrange("(p k) n -> p k n", k=KD)),
                (w_r[:, :, NG:NG + NE], w_router_expert[0].rearrange("(p k) n -> p k n", k=KD)),
            ] + [(cw_sb[:, j, :], conv_w[0, j].rearrange("(k p) -> p k", p=P)) for j in range(3)]
            assert len(smalls) == N_SMALL
            for dst, src in smalls:
                pool.dma_start(dst, src).then_inc(small_in, 16)

            pool.wait_ge(biasrow_ready, 1)
            pool.dma_start(bias_dram.ap(), bias_row[:, :]).then_inc(bias_stored, 16)

            pool.wait_ge(att_copied, 2)
            for a in range(4):
                v = attm[:, 2 * a:2 * a + 2, :]
                link(g.affine_select(out=v, in_=v, compare_op=ALU.is_ge, fill=0.0, base=0,
                                     pattern=[[0, 2], [1, P]], channel_multiplier=-1))
            g.memset(attm[0:CH, :, CH:P], 0.0).then_inc(att_ready, 1)
            pool.wait_ge(kd_turned, 1)
            pool.wait_ge(state_ready, 3)
            qz = qTz[:, :, :].rearrange("p (b two) t -> p b two t", two=2)
            g.memset(qz[DH:P, :, 0, :], 0.0).then_inc(qz_zero, 1)
            g.memset(qz[0:DH, :, 1, :], 0.0).then_inc(qz_zero, 1)
            pool.wait_ge(bias_stored, 16)
            pool.wait_ge(o_mm, 2)
            for h in range(NH):
                if h >= 4:
                    pool.wait_ge(score_mm, h - 3)
                pool.dma_start(bias_h[:, h % 4, :], bass.AP(bias_dram, h * 384, [[1, P], [1, T]])
                               ).then_inc(bias_in[h % 4], 16)
            pool.wait_ge(h2_ready, 2)
            g.iota(iota_s[:, :], pattern=[[1, SLOTS]], base=0, channel_multiplier=0,
                   allow_small_or_imprecise_dtypes=True).then_inc(iota_ready, 1)
            pool.wait_ge(xn_hi_ready, 1)
            g.tensor_tensor(xn_lo[:, :, :], xn[:, :, :], xn_hi[:, :, :].bitcast(F32),
                            ALU.subtract).then_inc(xn_lo_ready, 1)
            pool.wait_ge(router_mm, 1)
            g.memset(xs[:, :, SLOTS:SPAD], 0.0).then_inc(iota_ready, 1)
            pool.wait_ge(iota_ready, 2)
            for b in range(2):
                pool.dma_start(y_rows[(NE + b) * WIN:(NE + b + 1) * WIN, 0:KD * WIN].rearrange("r (k n) -> r k n", k=KD),
                               xs[0:WIN, :, SLOTS:SPAD]).then_inc(y_stored[b], 16)

            def low_part(p, i, q):
                s = slot_of(q)
                for c in POOL_LO:
                    n = c if p is None else PER_PASS * CHUNKS * p + RING * CHUNKS * i + CHUNKS * q + c
                    pool.wait_ge(hi_ready, n + 1)
                    g.tensor_tensor(ring_lo[s][:, chunk(c)], ring[s][:, chunk(c)], hi_buf(q, c).bitcast(F32),
                                    ALU.subtract).then_inc(lo_ready_pool, 1)

            low_part(None, 0, 0)

            pool.wait_ge(route_ready, 1)
            passes = pool.value_load(npass[0:1, 0:1], min_val=1, max_val=MAXWIN)

            def offset(p, e):
                return pool.value_load(off_tab[0:1, bass.ds(p * NE + e, 1)], min_val=0, max_val=SLOTS)

            def window(p, e, b):
                n = (NE + 1) * p + e
                off = offset(p, e)
                v = xs[:, :, bass.ds(off, WIN)]
                pool.wait_ge(xs_act, KD // 2)
                pool.wait_ge(xs_dve, KD // 2)
                g.tensor_copy(xe[b][:, :, 0:WIN], v).then_inc(xe_high, 1)
                pool.wait_ge(xe_high, n)
                pool.sem_inc(xe_ready, 1)
                g.tensor_tensor(xe[b][:, :, WIN:2 * WIN], v, xe[b][:, :, 0:WIN].bitcast(F32),
                                ALU.subtract).then_inc(xe_ready, 1)

            def store(p, e, b):
                pool.wait_ge(y_ready, NE * p + e + 2)
                pool.sem_inc(storing, 1)
                pool.dma_start(y_rows[bass.ds(e * WIN, WIN), :], y_tok[:, b, :]).then_inc(y_stored[b], 16)

            pool.sem_inc(xe_ready, 2)
            with pool.Fori(0, passes) as p:
                with pool.If(p > 0):
                    pool.wait_ge(freed, after_slots(p, 0))
                    window(p, 0, 0)
                window(p, 1, 1)
                with pool.If(p > 0):
                    low_part(p, 0, 0)
                low_part(p, 0, 1)
                low_part(p, 0, 2)
                pool.wait_ge(freed, after_slots(p, 2))
                window(p, 2, 0)
                low_part(p, 0, 3)
                low_part(p, 0, 4)
                with pool.Fori(0, NE // 2 - 1) as i:
                    for s in range(2):
                        low_part(p, i, 5 + 3 * s)
                        pool.wait_ge(freed, after_slots(p, 6 * i + (4 + 3 * s)))
                        window(p, 3 + 2 * i + s, (s + 1) % 2)
                        low_part(p, i, 6 + 3 * s)
                        store(p, 2 * i + s, s)
                        low_part(p, i, 7 + 3 * s)
                low_part(p, 0, PER_PASS - 1)
                store(p, NE - 2, 0)
                store(p, NE - 1, 1)
                for b in range(2):
                    pool.wait_ge(y_stored[b], (8 * NE) * p + (8 * NE + 16))
                pool.wait_ge(picked, 2 * p + 1)
                pool.sem_inc(gathering, 1)
                for j in range(TT * TOPK):
                    g.indirect_dma_start(out=y_back[j // TOPK][:, j % TOPK, :], out_offset=None, in_=y_rows[0:NE * WIN, :],
                                         in_offset=bass.IndirectOffsetOnAxis(ap=row_now[:, j:j + 1], axis=0)
                                         ).then_inc(back_in[j], 16)
                for j in range(TT * TOPK):
                    pool.wait_ge(back_in[j], 16 * p + 16)

        @block.scalar
        def _(act):
            s_ = nc.scalar

            act.dma_start(g_mix[:, :], norm_mix[0].rearrange("(p k) -> p k", k=KD)).then_inc(gain_in, 16)
            act.dma_start(w_al[:, :], w_gla_alpha[0]).then_inc(alpha_in, 16)
            act.dma_start(b_al[:, :], b_gla_alpha[0].rearrange("(a p) -> p a", p=P)).then_inc(alpha_in, 16)
            early = [(onehot[:, :], onehot_dram),
                     (table[:, :], rel_bias_table)]
            assert len(early) == N_EARLY
            for dst, src in early:
                act.dma_start(dst, src).then_inc(early_in, 16)

            act.wait_ge(ms_ready, 2)
            s_.activation(stat[:, 2:4], stat[:, 0:2], ACT.Sqrt).then_inc(rms_ready, 1)

            def high_pre(g, cs=range(CHUNKS)):
                act.wait_ge(landed[g % PRE_RING], 16 * (g // PRE_RING + 1))
                for c in cs:
                    if g and c < CHUNKS - 1:
                        act.wait_ge(chunk_done, (CHUNKS - 1) * (g - 1) + c + 1)
                    elif g:
                        act.wait_ge(proj_done, first_bank[g])
                    s_.activation(w_hi[c][:, :], ring[g % PRE_RING][:, chunk(c)], ACT.Copy).then_inc(wpre_hi, 1)

            act.wait_ge(gain_in, 16)
            for kp in range(4):
                if kp >= 2:
                    high_pre(0, (kp - 2,))
                act.wait_ge(hT_turned, kp + 1)
                for k in range(2):
                    s_.activation(hT_hi[:, 2 * kp + k, :], bank(4 + kp, 2)[:, k, :], ACT.Copy,
                                  scale=g_mix[:, 2 * kp + k:2 * kp + k + 1]).then_inc(hT_act, 1)
            high_pre(0, (2, 3))
            act.wait_ge(wz_in, 16)
            s_.activation(w_z_hi[:, :, :], w_z[:, :, :], ACT.Copy).then_inc(wz_hi_ready, 1)

            def evac(g, m, dst, func=ACT.Copy, scale=1.0):
                b, _ = bank_of(g, m)
                act.wait_ge(proj_done, first_bank[g] + m + 1)
                s_.activation(dst, bank(b), func, scale=scale).then_inc(evacuated[b], 1)

            evac(0, 0, flat(gqk[:, 0:2, :]), scale=float(GK) ** -0.5)
            high_pre(1)
            evac(0, 1, flat(gqk[:, 2:4, :]))
            act.wait_ge(z_mm, 1)
            s_.activation(zT[:, :], ps[0:16, 4, 0:T], ACT.Copy).then_inc(z_ready, 1)
            evac(1, 0, gv[:, 0, :])
            act.wait_ge(alpha_in, 32)
            high_pre(2, (0,))
            act.wait_ge(sigmin_ready, 2)
            for a in range(2):
                s_.activation(e_pos[:, a, :], bank(5, 2)[:, a, :], ACT.Abs,
                              bias=b_al[:, a:a + 1]).then_inc(a_chain, 1)
            high_pre(2, (1,))
            act.wait_ge(a_chain, 2)
            s_.activation(e_pos, e_pos, ACT.Exp, scale=-1.0).then_inc(a_chain, 1)
            high_pre(2, (2,))
            act.wait_ge(a_chain, 3)
            s_.activation(e_pos, e_pos, ACT.Ln, bias=1.0).then_inc(softplus_ready, 1)
            high_pre(2, (3,))
            evac(1, 1, gv[:, 1, :])
            act.wait_ge(cum_ready, 3)
            s_.activation(e_rest, e_rest, ACT.Exp, scale=1.0 / TEMP).then_inc(decay_ready, 1)
            s_.activation(e_pos, la, ACT.Exp, scale=1.0 / TEMP).then_inc(decay_ready, 1)
            s_.activation(e_neg, la, ACT.Exp, scale=-1.0 / TEMP).then_inc(decay_ready, 1)
            evac(2, 0, gr[:, 0, :], func=ACT.Silu)
            high_pre(3)
            evac(2, 1, gr[:, 1, :], func=ACT.Silu)
            act.wait_ge(kd_turned, 1)
            s_.activation(flat(kdn[:, :, :]), bank(6), ACT.Copy).then_inc(kdn_ready, 1)
            high_pre(4)
            for tt in range(TT):
                act.wait_ge(o_mm, tt + 1)
                s_.activation(scr[:, tt, :], bank(4 if tt == 0 else 7), ACT.Square).then_inc(o_sq, 1)
            act.wait_ge(o_ms, 1)
            s_.activation(stat[:, 16:24], stat[:, 8:16], ACT.Sqrt).then_inc(o_rms, 1)
            act.wait_ge(small_in, 16 * N_SMALL)
            for m in range(2):
                act.wait_ge(yg_turned, 2)
                s_.activation(yg_hi[:, 2 * m:2 * m + 2, :], bank(5 + m, 2), ACT.Copy,
                              scale=on_w[:, 0:1]).then_inc(yg_hi_ready, 1)
            high_pre(5)
            act.wait_ge(qk_ms, 1)
            s_.activation(qkr[:, :, :, :], qkm[:, :, :, :], ACT.Sqrt).then_inc(qk_rms, 1)
            evac(5, 0, av[:, 0, :])
            high_pre(6)
            evac(5, 1, av[:, 1, :])
            for m in range(2):
                act.wait_ge(qk_turned, 3 + m)
                s_.activation(kT[:, 2 * m:2 * m + 2, :], bank(6 + m, 2), ACT.Copy,
                              scale=kn_w[:, 0:1]).then_inc(kT_ready, 1)

            def softmax_exp(h):
                act.wait_ge(rowmax_ready, h + 1)
                if h >= 2:
                    act.wait_ge(prob_turned, h - 1)
                for tt in range(TT):
                    s_.activation(prob[:, h % 2, P * tt:P + 2 * P * tt], ps[:, 4 + h % 2, P * tt:P + 2 * P * tt],
                                  ACT.Exp, bias=nmx[:, h, tt:tt + 1],
                                  accum_out=rsum[:, h, tt:tt + 1]).then_inc(exp_ready, 1)

            def prob_out(h):
                act.wait_ge(prob_turned, h + 1)
                if h >= 2:
                    act.wait_ge(pv_mm, h - 1)
                s_.activation(probT[:, h % 2, :], bank(6)[:, 0:384], ACT.Copy).then_inc(probT_ready, 1)

            def gate_out(n, half, m):
                if n == 2:
                    act.wait_ge(branch_done, 2 * half + m + 1)
                dt = 4 * half + 2 * m
                evac(9 + 3 * n + half, m, flat(sig[n][:, dt:dt + 2, :]), func=ACT.Sigmoid)

            evac(6, 0, flat(ycT[:, 0:2, :]))
            softmax_exp(0)
            for h in range(1, NH):
                if h % 2:
                    high_pre(7 + h // 2)
                if h == 1:
                    evac(6, 1, flat(ycT[:, 2:4, :]))
                softmax_exp(h)
                prob_out(h - 1)
                if h >= 6:
                    gate_out(0, 0, h - 6)
            prob_out(NH - 1)
            gate_out(0, 1, 0)
            high_pre(11)
            gate_out(0, 1, 1)
            for n in range(1, 3):
                high_pre(9 + 3 * n)
                for half in range(2):
                    gate_out(n, half, 0)
                    high_pre(10 + 3 * n + half)
                    gate_out(n, half, 1)

            def merged_high(m):
                act.wait_ge(branch_done, 8 + m + 1)
                s_.activation(merged_hi[:, 2 * m:2 * m + 2, :], mergedT[:, 2 * m:2 * m + 2, :],
                              ACT.Copy).then_inc(merged_hi_ready, 1)

            merged_high(0)
            merged_high(1)
            high_pre(18, (0,))
            merged_high(2)
            high_pre(18, (1, 2))
            merged_high(3)
            high_pre(18, (3,))
            high_pre(19)

            def high_part(p, i, q, cs):
                s = slot_of(q)
                for c in cs:
                    if p is None:
                        act.wait_ge(chunk_in[s][c], 16)
                        if q == 0 and c < CHUNKS - 1:
                            act.wait_ge(chunk_done, (CHUNKS - 1) * (NPRE - 1) + c + 1)
                        elif q == 0:
                            act.wait_ge(proj_done, first_bank[NPRE])
                    else:
                        act.wait_ge(chunk_in[s][c], (16 * PER_PASS // RING) * p + 16 * i + 16 * (q // RING + 1))
                        act.wait_ge(freed, PER_PASS * CHUNKS * p + RING * CHUNKS * i + CHUNKS * q + c + 1 - HI_BUFS
                                    + FREED_SEED)
                    s_.activation(hi_buf(q, c), ring[s][:, chunk(c)], ACT.Copy).then_inc(hi_ready, 1)

            high_part(None, 0, 0, (0, 1, 2, 3))
            act.wait_ge(ms2_ready, 2)
            s_.activation(stat[:, 2:4], stat[:, 0:2], ACT.Sqrt).then_inc(rms2_ready, 1)
            for kp in range(2):
                act.wait_ge(h2_turned, kp + 1)
                for k in range(2):
                    s_.activation(h2T[:, 2 * kp + k, :], bank(4 + kp, 2)[:, k, :], ACT.Copy,
                                  scale=g_ffn[:, 2 * kp + k:2 * kp + k + 1]).then_inc(hT_act, 1)
            act.wait_ge(h2_ready, 2)
            s_.activation(xn_hi[:, :, :], xn[:, :, :], ACT.Copy).then_inc(xn_hi_ready, 1)
            high_part(None, 0, 1, (0, 1))
            act.wait_ge(nmax_ready, 1)
            for tt in range(TT):
                s_.activation(rt[:, tt, 8:12], lgp[:, tt, 0:NG], ACT.Exp, bias=rt[:, tt, 0:1],
                              accum_out=rt[:, tt, 1:2]).then_inc(gexp_ready, 1)
            act.wait_ge(e2in_ready, 1)
            s_.activation(rt[:, :, 3:4], rt[:, :, 2:3], ACT.Exp).then_inc(e2_ready, 1)
            for k in range(0, KD, 2):
                act.wait_ge(gather_mm, k + 1)
                s_.activation(xs[:, k, 0:SLOTS], bank(2 + k % 4), ACT.Copy,
                              scale=g_ffn[:, k:k + 1]).then_inc(xs_act, 1)
            act.wait_ge(xs_act, KD // 2)
            act.wait_ge(xs_dve, KD // 2)
            s_.activation(xe[0][:, :, 0:WIN], xs[:, :, 0:WIN], ACT.Copy).then_inc(first_high, 1)

            act.wait_ge(route_ready, 1)
            passes = act.value_load(npass[0:1, 0:1], min_val=1, max_val=MAXWIN)

            def gu_low_rows(p, n, b):
                act.wait_ge(freed, after_slots(p, n))
                s_.activation(g_lo[:, :], ps[WIN:P, 2 * b, :], ACT.Copy).then_inc(gu_lo_out, 1)
                s_.activation(u_lo[:, :], ps[WIN:P, 2 * b + 1, :], ACT.Copy).then_inc(gu_lo_out, 1)

            def silu(p, e):
                act.wait_ge(gu_free, 2 * NE * p + 2 * e + 5)
                s_.activation(g_act[:, :], g_sum[:, :], ACT.Silu).then_inc(silu_ready, 1)

            def he_high(p, e):
                act.wait_ge(h_turned, NE * p + e + 1)
                s_.activation(he[:, :, 0:WIN], ps[:, 6, 0:KC * WIN].rearrange("p (k n) -> p k n", n=WIN),
                              ACT.Copy).then_inc(he_hi, 1)

            def y_low_rows(p, n, b=4):
                act.wait_ge(freed, after_slots(p, n))
                s_.activation(y_lo[:, :], flat(ps[WIN:P, b:b + 2, :]), ACT.Copy).then_inc(y_lo_out, 1)

            def step(p, e, i, q, b, before_gu, before_y):
                high_part(p, i, q, (0,))
                gu_low_rows(p, before_gu, 1 - b)
                high_part(p, i, q, (1,))
                silu(p, e - 1)
                high_part(p, i, q, (2,))
                high_part(p, i, q, (3,))
                high_part(p, i, q + 1, (0,))
                if before_y is not None:
                    y_low_rows(p, before_y)
                high_part(p, i, q + 1, (1, 2, 3))
                high_part(p, i, q + 2, (0,))
                he_high(p, e - 1)
                high_part(p, i, q + 2, (1, 2, 3))

            with act.Fori(0, passes) as p:
                with act.If(p > 0):
                    high_part(p, 0, 0, (0, 1, 2, 3))
                    high_part(p, 0, 1, (0, 1))
                high_part(p, 0, 1, (2, 3))
                step(p, 1, 0, 2, 1, 2, None)
                with act.Fori(0, NE // 2 - 1) as i:
                    for s in range(2):
                        step(p, 2 * i + (2 + s), i, 5 + 3 * s, s, 6 * i + (4 + 3 * s), 6 * i + (5 + 3 * s))
                gu_low_rows(p, PER_PASS - 2, 1)
                silu(p, NE - 1)
                high_part(p, 0, PER_PASS - 1, (0, 1, 2))
                he_high(p, NE - 1)
                high_part(p, 0, PER_PASS - 1, (3,))
                y_low_rows(p, PER_PASS - 1)
                act.wait_ge(y_ready, NE * p + NE)
                y_low_rows(p, PER_PASS, 0)

        @block.tensor
        def _(pe):
            t_ = nc.tensor

            def turn_x(src, ready, values, signal):
                for tt in range(TT):
                    pe.wait_ge(ready, values[tt])
                    for kp in range(4):
                        for k in range(2):
                            ins = t_.transpose(bank(4 + kp, 2)[:, k, tt * P:(tt + 1) * P],
                                               src[:, tt, 2 * kp + k::KD], ident[:, :])
                        if tt == TT - 1:
                            ins.then_inc(signal, 1)

            def begin(g, m):
                b, use = bank_of(g, m)
                if use:
                    pe.wait_ge(evacuated[b], use)
                return b

            def weights(g, at, n):
                c = at // CW
                return w_hi[c][:, at - CW * c:at - CW * c + n], ring_lo[g % PRE_RING][:, at:at + n]

            def by_token(g, tt, x_hi, x_lo):
                b = begin(g, tt)
                rows = slice(tt * P, (tt + 1) * P)
                for k in range(KD):
                    if g == NPRE - 2 and tt == 0 and k % 2 == 0:
                        pe.wait_ge(merged_lo_ready, k // 2 + 1)
                    if tt == 0 and k % CHUNK_T == 0:
                        pe.wait_ge(wpre_lo, CHUNKS * g + k // CHUNK_T + 1)
                    wh, wl = weights(g, k * C, C)
                    t_.matmul(bank(b), x_hi[:, k, rows], wh, start=(k == 0), stop=False)
                    t_.matmul(bank(b), x_hi[:, k, rows], wl, start=False, stop=False)
                    ins = t_.matmul(bank(b), x_lo[:, k, rows], wh, start=False, stop=(k == KD - 1))
                    if tt == TT - 1 and k % CHUNK_T == CHUNK_T - 1 and k < KD - 1:
                        ins.then_inc(chunk_done, 1)
                ins.then_inc(proj_done, 1)

            def by_feature(g, m, banks, n, x_hi, x_lo):
                b = begin(g, m)
                nk = SLOT // n
                for k in range(nk):
                    c = k * n // CW
                    first_of_chunk = k * n % CW == 0
                    if g == 0 and m == 0:
                        pe.wait_ge(hT_lo_ready, k + 1)
                    if m == 0 and first_of_chunk:
                        pe.wait_ge(wpre_lo, CHUNKS * g + c + 1)
                    for j in range(2):
                        wh, wl = weights(g, k * n + (2 * m + j) * P, P)
                        o = bank(b, 2)[:, j, :]
                        t_.matmul(o, wh, x_hi[:, k, :], start=(k == 0 and j == 0), stop=False, skip_group_check=True)
                        t_.matmul(o, wh, x_lo[:, k, :], start=False, stop=False, skip_group_check=True)
                        ins = t_.matmul(o, wl, x_hi[:, k, :], start=False, stop=(k == nk - 1), skip_group_check=True)
                    if m == banks - 1 and (k + 1) * n % CW == 0 and k < nk - 1:
                        ins.then_inc(chunk_done, 1)
                ins.then_inc(proj_done, 1)

            def feat(g, m):
                by_feature(g, m, 2, C, hT_hi, hT_lo)

            def tok(g, tt):
                by_token(g, tt, hT_hi, hT_lo)

            pe.wait_ge(consts, 6)
            turn_x(xn, xn_ready, (1, 2), hT_turned)
            pe.wait_ge(early_in, 16 * N_EARLY)
            t_.matmul(ps[0:NH, 3, 0:T], table[:, :], onehot[:, :], start=True, stop=True).then_inc(biasrow_mm, 1)
            feat(0, 0)
            feat(0, 1)
            pe.wait_ge(wz_lo_ready, 1)
            for k in range(KD):
                o = ps[0:16, 4, 0:T]
                t_.matmul(o, w_z_hi[:, k, :], hT_hi[:, k, :], start=(k == 0), stop=False)
                t_.matmul(o, w_z_hi[:, k, :], hT_lo[:, k, :], start=False, stop=False)
                ins = t_.matmul(o, w_z_lo[:, k, :], hT_hi[:, k, :], start=False, stop=(k == KD - 1))
            ins.then_inc(z_mm, 1)
            tok(1, 0)
            pe.wait_ge(z_ready, 1)
            pe.wait_ge(alpha_in, 32)
            for a in range(2):
                ins = t_.matmul(bank(5, 2)[:, a, :], w_al[:, a * P:(a + 1) * P], zT[:, :], start=True, stop=True)
            ins.then_inc(alpha_mm, 1)
            pe.wait_ge(biasrow_ready, 1)
            tok(1, 1)
            tok(2, 0)

            tok(2, 1)
            pe.wait_ge(gla_in_ready, 1)
            for tt in range(TT):
                for a in range(2):
                    ins = t_.transpose(bank(6, 4)[:, 2 * tt + a, :], e_rest[:, a, tt * P:(tt + 1) * P], ident[:, :])
            ins.then_inc(kd_turned, 1)
            pe.wait_ge(gla_in_ready, 3)
            for par in range(2):
                for tt in range(TT):
                    for a in range(2):
                        rows = slice(GK * par, GK * par + GK)
                        ins = t_.matmul(bank(4 + 3 * par, 4)[:, 2 * tt + a, :], gqk[rows, 2 + a, tt * P:(tt + 1) * P],
                                        gqk[rows, a, tt * P:(tt + 1) * P], start=True, stop=True)
                ins.then_inc(att_mm, 1)
            tok(3, 0)
            pe.wait_ge(kdn_ready, 1)
            pe.wait_ge(att_copied, 1)
            pe.wait_ge(evacuated[bank_of(1, 0)[0]], bank_of(1, 0)[1] + 1)
            pe.wait_ge(evacuated[bank_of(1, 1)[0]], bank_of(1, 1)[1] + 1)
            for c in range(3):
                rows = slice(CH * (c % 2), CH * (c % 2) + CH)
                for a in range(2):
                    ins = t_.matmul(bank((5, 6, 4)[c], 2)[:, a, :], kdn[rows, c // 2, a * P:(a + 1) * P],
                                    gv[rows, c // 2, a * 256:(a + 1) * 256], start=True, stop=True)
                ins.then_inc(kv_mm, 1)
            tok(3, 1)
            pe.wait_ge(att_ready, 1)
            pe.wait_ge(state_ready, 3)
            for tt in range(TT):
                b = 4 if tt == 0 else 7
                for h in range(GH):
                    t_.matmul(bank(b, 4)[:, h, :], attm[:, 4 * (h % 2) + 2 * tt + h // 2, :],
                              gv[:, tt, h * GV:(h + 1) * GV], start=(h == 0), stop=False, skip_group_check=True)
                for c in range(max(1, 2 * tt), 2 * tt + 2):
                    rows = slice(CH * (c % 2), CH * (c % 2) + CH)
                    for a in range(2):
                        ins = t_.matmul(bank(b, 2)[rows, a, :], gqk[:, a, c * CH:(c + 1) * CH], sbd[:, c - 1, a, :],
                                        start=False, stop=True, skip_group_check=True)
                ins.then_inc(o_mm, 1)
            tok(4, 0)
            pe.wait_ge(ygla_ready, 2)
            for m in range(2):
                for h in range(2):
                    for tt in range(TT):
                        ins = t_.transpose(bank(5 + m, 2)[:, h, tt * P:(tt + 1) * P],
                                           gr[:, tt, (2 * m + h) * GV:(2 * m + h + 1) * GV], ident[:, :])
                ins.then_inc(yg_turned, 1)
            tok(4, 1)
            tok(5, 0)
            tok(5, 1)
            pe.wait_ge(ygT_ready, 2)
            pe.wait_ge(qkn_ready, 2)
            for w in range(2):
                for m in range(2):
                    for j in range(2):
                        for tt in range(TT):
                            ins = t_.transpose(bank(4 + 2 * w + m, 2)[:, j, tt * P:(tt + 1) * P],
                                               aqk[:, w, tt, (2 * m + j) * P:(2 * m + j + 1) * P], ident[:, :])
                    ins.then_inc(qk_turned, 1)

            def scores(h):
                b = 4 + h % 2
                if h == 0:
                    pe.wait_ge(kT_ready, 2)
                    pe.wait_ge(qT_ready, 4)
                if h >= 2:
                    pe.wait_ge(exp_ready, 2 * (h - 1))
                pe.wait_ge(bias_in[h % 4], 16 * (h // 4 + 1))
                for tt in range(TT):
                    o = ps[:, b, P * tt:P + 2 * P * tt]
                    keys = slice(0, P * (tt + 1))
                    t_.matmul(o, antid[:, :], bias_h[:, h % 4, P * (1 - tt):T], start=True, stop=False)
                    ins = t_.matmul(o, qTz[:, h, tt * P:(tt + 1) * P], kT[:, h // 2, keys], start=False, stop=True)
                ins.then_inc(score_mm, 1)

            def turn_prob(h):
                pe.wait_ge(prob_ready, h + 1)
                if h >= 1:
                    pe.wait_ge(probT_ready, h)
                for j in range(3):
                    ins = t_.transpose(bank(6, 4)[:, j, :], prob[:, h % 2, j * P:(j + 1) * P], ident[:, :])
                ins.then_inc(prob_turned, 1)

            def prob_v(h):
                pe.wait_ge(probT_ready, h + 1)
                if h >= 2:
                    pe.wait_ge(yaT_ready, h // 2)
                rows = slice(DH * (h % 2), DH * (h % 2) + DH)
                o = bank(7, 2)[rows, (h // 2) % 2, :]
                t_.matmul(o, av[:, 0, h * DH:(h + 1) * DH], probT[:, h % 2, 0:T], start=True, stop=False)
                t_.matmul(o[:, P:T], av[:, 1, h * DH:(h + 1) * DH], probT[:, h % 2, T:T + P],
                          start=False, stop=True).then_inc(pv_mm, 1)

            dense = [lambda g=g, m=m: feat(g, m) for g in (6, 7, 8, 9, 10) for m in range(2)]
            pe.wait_ge(evacuated[bank_of(5, 0)[0]], bank_of(5, 0)[1] + 1)
            pe.wait_ge(evacuated[bank_of(5, 1)[0]], bank_of(5, 1)[1] + 1)
            for u in range(NH + 2):
                dense[u]()
                if u < NH:
                    scores(u)
                if 1 <= u <= NH:
                    turn_prob(u - 1)
                if u >= 2:
                    prob_v(u - 2)

            def branch(n, y_hi, y_lo):
                for m in range(4):
                    by_feature(11 + 3 * n, m, 4, D, y_hi, y_lo)

            pe.wait_ge(ycT_ready, 2)
            branch(0, yc_hi, yc_lo)
            for n in range(1, 3):
                for half in range(2):
                    for m in range(2):
                        feat(9 + 3 * n + half, m)
                if n == 1:
                    pe.wait_ge(yaT_ready, 4)
                    branch(1, ya_hi, ya_lo)
                else:
                    branch(2, yg_hi, yg_lo)
            for half in range(2):
                for tt in range(TT):
                    by_token(18 + half, tt, merged_hi, merged_lo)

            turn_x(x_tok, x1_ready, (3, 4), h2_turned)
            pe.wait_ge(hT_act, 8 + 4)
            pe.wait_ge(hT_dve, 4)
            pe.wait_ge(small_in, 16 * N_SMALL)
            for k in range(KD):
                ins = t_.matmul(ps[0:NG + NE, 0, 0:T], w_r[:, k, :], h2T[:, k, :], start=(k == 0), stop=(k == KD - 1))
            ins.then_inc(router_mm, 1)
            pe.wait_ge(logits_ready, 1)
            for tt in range(TT):
                ins = t_.transpose(ps[:, 1, tt * (NG + NE):(tt + 1) * (NG + NE)], lgT[:, tt * P:(tt + 1) * P],
                                   ident[0:NG + NE, 0:NG + NE])
            ins.then_inc(router_mm, 1)
            pe.wait_ge(assign_ready, 2)
            for tt in range(TT):
                o = ps[:, 1, tt * NE:(tt + 1) * NE]
                t_.matmul(o, tri_bf[:, :], eall_bf[:, tt, :], start=True, stop=False)
                if tt:
                    t_.matmul(o, ones_bf[:, :], eall_bf[:, 0, :], start=False, stop=False)
                t_.matmul(o, ones_bf[:, :], epre_bf[:, 0, :], start=False, stop=False)
                t_.matmul(o, ones_bf[:, :], epre_bf[:, 1, :], start=False, stop=True)
            for j, src in enumerate((epre_bf, eall_bf)):
                o = ps[:, 1, (2 + j) * NE:(3 + j) * NE]
                t_.matmul(o, ones_bf[:, :], src[:, 0, :], start=True, stop=False)
                ins = t_.matmul(o, ones_bf[:, :], src[:, 1, :], start=False, stop=True)
            ins.then_inc(pos_mm, 1)
            pe.wait_ge(xn_lo_ready, 1)
            for k4 in range(0, KD, 4):
                for tt in range(TT):
                    pe.wait_ge(perm_ready, tt + 1)
                    for k in range(k4, k4 + 4):
                        if k >= 4 and tt == 0:
                            pe.wait_ge((xs_act, xs_dve)[k % 2], (k - 4) // 2 + 1)
                        o = bank(2 + k % 4)
                        t_.matmul(o, xn_hi[:, tt, k::KD], perm[:, tt, :], start=(tt == 0), stop=False)
                        ins = t_.matmul(o, xn_lo[:, tt, k::KD], perm[:, tt, :], start=False, stop=(tt == 1))
                        if tt == 1:
                            ins.then_inc(gather_mm, 1)
            pe.wait_ge(route_ready, 1)
            pe.sem_inc(freed, FREED_SEED)
            passes = pe.value_load(npass[0:1, 0:1], min_val=1, max_val=MAXWIN)

            def products(p, i, q, lhs, out_of, tile_of):
                for c in range(CHUNKS):
                    n = PER_PASS * CHUNKS * p + RING * CHUNKS * i + CHUNKS * q + c
                    pe.wait_ge(hi_ready, n + 1)
                    if c in POOL_LO:
                        pe.wait_ge(lo_ready_pool, PER_PASS * len(POOL_LO) * p + RING * len(POOL_LO) * i
                                   + len(POOL_LO) * q + POOL_LO.index(c) + 1)
                    else:
                        nd = CHUNKS - len(POOL_LO)
                        pe.wait_ge(lo_ready, PER_PASS * nd * p + RING * nd * i + nd * q + c + 1)
                    for j in range(CHUNK_T):
                        k, o, first, last = tile_of(CHUNK_T * c + j)
                        at = CW * c + C * j
                        t_.matmul(out_of(o), lhs[:, k, :], hi_buf(q, c)[:, C * j:C * (j + 1)], start=first, stop=False)
                        ins = t_.matmul(out_of(o), lhs[:, k, :], ring_lo[slot_of(q)][:, at:at + C], start=False,
                                        stop=last)
                    ins.then_inc(freed, 1)

            def gate_up(p, i, q, b, up):
                products(p, i, q, xe[b], lambda o: ps[:, 2 * b + up, :], lambda k: (k, 0, k == 0, k == KD - 1))

            def down(p, i, q, b=4):
                products(p, i, q, he, lambda o: ps[:, b + o, :],
                         lambda n: (n // 2, n % 2, n // 2 == 0, n // 2 == KC - 1))

            def start_gate(p, e):
                pe.wait_ge(xe_ready, 2 * (NE + 1) * p + 2 * e + 2)
                pe.wait_ge(gu_free, 2 * NE * p + 2 * e + 2)
                if isinstance(e, int) and e == 0:
                    pe.wait_ge(first_window, 1)
                    pe.wait_ge(y_ready, NE * p + 1)

            def turn_h(p, e):
                pe.wait_ge(h_ready, NE * p + e + 1)
                for j in range(KC):
                    ins = t_.matmul(ps[:, 6, j * WIN:(j + 1) * WIN], h_tok[:, j * P:(j + 1) * P],
                                    ident[0:WIN, 0:WIN], start=True, stop=True)
                ins.then_inc(h_turned, 1)

            def start_down(p, e):
                pe.wait_ge(he_hi, NE * p + e + 1)
                pe.wait_ge(he_lo, NE * p + e + 1)
                pe.wait_ge(y_ready, NE * p + e + 1)

            def step(p, e, i, q, b):
                start_gate(p, e)
                gate_up(p, i, q, b, 0)
                turn_h(p, e - 1)
                gate_up(p, i, q + 1, b, 1)
                start_down(p, e - 1)
                down(p, i, q + 2)

            with pe.Fori(0, passes) as p:
                start_gate(p, 0)
                gate_up(p, 0, 0, 0, 0)
                gate_up(p, 0, 1, 0, 1)
                step(p, 1, 0, 2, 1)
                with pe.Fori(0, NE // 2 - 1) as i:
                    for s in range(2):
                        step(p, 2 * i + (2 + s), i, 5 + 3 * s, s)
                turn_h(p, NE - 1)
                pe.wait_ge(he_hi, NE * p + NE)
                pe.wait_ge(he_lo, NE * p + NE)
                pe.wait_ge(gu_free, 2 * NE * p + 2 * NE + 2)
                down(p, 0, PER_PASS - 1, 0)

        @block.vector
        def _(dve):
            v = nc.vector
            steps = [0]

            def link(ins):
                steps[0] += 1
                ins.then_inc(v_chain, 1)
                dve.wait_ge(v_chain, steps[0])

            def norm_stats(src, dst, signal, tts=range(TT)):
                for tt in tts:
                    if src is x_tok and signal is ms_ready:
                        dve.wait_ge(x_in[tt], 16)
                    link(v.tensor_tensor_reduce(dst[tt], src[:, tt, :], src[:, tt, :], 1.0, 0.0, ALU.mult,
                                                ALU.add, stat[:, tt:tt + 1]))
                    v.tensor_scalar(stat[:, tt:tt + 1], stat[:, tt:tt + 1], 1.0 / D, EPS, ALU.mult,
                                    ALU.add).then_inc(signal, 1)

            def norm_apply(src, dst, rms, signal):
                dve.wait_ge(rms, 1)
                link(v.reciprocal(stat[:, 4:6], stat[:, 2:4]))
                for tt in range(TT):
                    v.tensor_scalar(dst[:, tt, :], src[:, tt, :], stat[:, 4 + tt:5 + tt], None,
                                    ALU.mult).then_inc(signal, 1)

            def low_pre(g, cs=range(CHUNKS)):
                for c in cs:
                    dve.wait_ge(wpre_hi, CHUNKS * g + c + 1)
                    v.tensor_tensor(ring_lo[g % PRE_RING][:, chunk(c)], ring[g % PRE_RING][:, chunk(c)],
                                    w_hi[c][:, :].bitcast(F32), ALU.subtract).then_inc(wpre_lo, 1)

            norm_stats(x_tok, [xn[:, tt, :] for tt in range(TT)], ms_ready)
            norm_apply(x_tok, xn, rms_ready, xn_ready)
            dve.wait_ge(consts, 6)
            dve.wait_ge(gain_in, 16)
            for kp in range(4):
                if kp >= 2:
                    low_pre(0, (kp - 2,))
                dve.wait_ge(hT_act, 2 * (kp + 1))
                for k in (2 * kp, 2 * kp + 1):
                    v.scalar_tensor_tensor(out=hT_lo[:, k, :], in0=bank(4 + kp, 2)[:, k % 2, :],
                                           scalar=g_mix[:, k:k + 1], in1=hT_hi[:, k, :].bitcast(F32), op0=ALU.mult,
                                           op1=ALU.subtract).then_inc(hT_lo_ready, 1)
            low_pre(0, (2, 3))
            dve.wait_ge(biasrow_mm, 1)
            v.tensor_copy(bias_row[:, 0:T], ps[0:NH, 3, 0:T]).then_inc(biasrow_ready, 1)
            dve.wait_ge(wz_hi_ready, 1)
            v.tensor_tensor(w_z_lo[:, :, :], w_z[:, :, :], w_z_hi[:, :, :].bitcast(F32),
                            ALU.subtract).then_inc(wz_lo_ready, 1)
            low_pre(1)
            dve.wait_ge(alpha_in, 32)

            dve.wait_ge(alpha_mm, 1)
            for a in range(2):
                v.tensor_scalar(e_neg[:, a, :], bank(5, 2)[:, a, :], b_al[:, a:a + 1], 0.0, ALU.add,
                                ALU.min).then_inc(sigmin_ready, 1)
            low_pre(2)
            dve.wait_ge(sigmin_ready, 2)
            dve.wait_ge(softplus_ready, 1)
            link(v.tensor_tensor(e_rest, e_neg, e_pos, ALU.subtract))
            for a in range(2):
                v.tensor_tensor_scan(la[:, a, :], reset[:, :], e_rest[:, a, :], 0.0, ALU.mult,
                                     ALU.add).then_inc(cum_ready, 1)
            dve.wait_ge(cum_ready, 2)
            for a in range(2):
                run = la[:, a, :].rearrange("p (c n) -> p c n", n=CH)
                ins = v.tensor_tensor(e_rest[:, a, :].rearrange("p (c n) -> p c n", n=CH),
                                      run[:, :, CH - 1:CH].broadcast_to([P, T // CH, CH]), run, ALU.subtract)
                if a == 0:
                    link(ins)
            ins.then_inc(cum_ready, 1)
            dve.wait_ge(evacuated[bank_of(0, 1)[0]], 1)
            dve.wait_ge(decay_ready, 1)
            v.tensor_tensor(e_rest, gqk[:, 2:4, :], e_rest, ALU.mult).then_inc(gla_in_ready, 1)
            dve.wait_ge(decay_ready, 2)
            v.tensor_tensor(gqk[:, 0:2, :], gqk[:, 0:2, :], e_pos, ALU.mult).then_inc(gla_in_ready, 1)
            dve.wait_ge(decay_ready, 3)
            v.tensor_tensor(gqk[:, 2:4, :], gqk[:, 2:4, :], e_neg, ALU.mult).then_inc(gla_in_ready, 1)
            low_pre(3)
            for par in range(2):
                dve.wait_ge(att_mm, par + 1)
                v.tensor_copy(attm[:, 4 * par:4 * par + 4, :], bank(4 + 3 * par, 4)).then_inc(att_copied, 1)
            def take(g, m, w, tt):
                b, _ = bank_of(g, m)
                dve.wait_ge(proj_done, first_bank[g] + m + 1)
                v.tensor_copy(aqk[:, w, tt, :], bank(b)).then_inc(evacuated[b], 1)

            take(3, 0, 0, 0)
            dve.wait_ge(sbd_zero, 1)
            for c in range(3):
                dve.wait_ge(kv_mm, c + 1)
                kv = bank((5, 6, 4)[c], 2)
                if c:
                    dve.wait_ge(state_ready, c)
                for h in range(2):
                    rows = slice(GK * h, GK * h + GK)
                    blk = slice(GV * h, GV * h + GV)
                    if c == 0:
                        ins = v.tensor_copy(sbd[rows, 0, :, blk], kv[rows, :, blk])
                    else:
                        for a in range(2):
                            ins = v.scalar_tensor_tensor(out=sbd[rows, c, a, blk], in0=sbd[rows, c - 1, a, blk],
                                                         scalar=e_pos[rows, a, CH * c + CH - 1:CH * c + CH],
                                                         in1=kv[rows, a, blk], op0=ALU.mult, op1=ALU.add)
                ins.then_inc(state_ready, 1)

            low_pre(4)
            take(3, 1, 0, 1)
            dve.wait_ge(small_in, 16 * N_SMALL)
            def head_squares(w):
                for g, m in ((3 + w, 0), (3 + w, 1)):
                    b, u = bank_of(g, m)
                    dve.wait_ge(evacuated[b], u + 1)
                link(v.tensor_tensor(flat(ycT[:, :, :]), flat(aqk[:, w, :, :]), flat(aqk[:, w, :, :]), ALU.mult))
                link(v.tensor_reduce(qkm[:, w, :, :],
                                     flat(ycT[:, :, :]).rearrange("p (t h n) -> p t h n", t=TT, n=DH), AX_X, ALU.add))

            head_squares(0)
            for tt in range(TT):
                dve.wait_ge(o_sq, tt + 1)
                link(v.tensor_reduce(stat[:, 8 + 4 * tt:12 + 4 * tt], scr[:, tt, :].rearrange("p (h n) -> p h n", n=GV),
                                     AX_X, ALU.add))
            v.tensor_scalar(stat[:, 8:16], stat[:, 8:16], 1.0 / GV, EPS, ALU.mult, ALU.add).then_inc(o_ms, 1)
            dve.wait_ge(o_rms, 1)
            link(v.reciprocal(stat[:, 24:32], stat[:, 16:24]))
            for tt in range(TT):
                o3 = scr[:, tt, :].rearrange("p (h n) -> p h n", n=GV)
                link(v.tensor_tensor(o3, bank(4 if tt == 0 else 7, 4),
                                     stat[:, 24 + 4 * tt:28 + 4 * tt].unsqueeze(2).broadcast_to([P, GH, GV]), ALU.mult))
                dve.wait_ge(evacuated[bank_of(2, tt)[0]], bank_of(2, tt)[1] + 1)
                v.tensor_tensor(gr[:, tt, :], scr[:, tt, :], gr[:, tt, :], ALU.mult).then_inc(ygla_ready, 1)
            take(4, 0, 1, 0)
            low_pre(5)
            take(4, 1, 1, 1)
            for m in range(2):
                dve.wait_ge(yg_hi_ready, m + 1)
                v.scalar_tensor_tensor(out=yg_lo[:, 2 * m:2 * m + 2, :], in0=bank(5 + m, 2), scalar=on_w[:, 0:1],
                                       in1=yg_hi[:, 2 * m:2 * m + 2, :].bitcast(F32), op0=ALU.mult,
                                       op1=ALU.subtract).then_inc(ygT_ready, 1)
            head_squares(1)
            v.tensor_scalar(qkm[:, :, :, :], qkm[:, :, :, :], 1.0 / DH, EPS, ALU.mult, ALU.add).then_inc(qk_ms, 1)
            dve.wait_ge(qk_rms, 1)
            link(v.reciprocal(qkm[:, :, :, :], qkr[:, :, :, :]))
            for w in range(2):
                for tt in range(TT):
                    a3 = aqk[:, w, tt, :].rearrange("p (h n) -> p h n", n=DH)
                    ins = v.tensor_tensor(a3, a3, qkm[:, w, tt, :].unsqueeze(2).broadcast_to([P, NH, DH]), ALU.mult)
                ins.then_inc(qkn_ready, 1)
            low_pre(6)
            link(v.tensor_scalar(qn_w[:, :], qn_w[:, :], float(DH) ** -0.5, None, ALU.mult))
            dve.wait_ge(qz_zero, 2)
            qz = qTz[:, :, :].rearrange("p (b two) t -> p b two t", two=2)
            for m in range(2):
                dve.wait_ge(qk_turned, m + 1)
                for h in range(2):
                    rows = slice(DH * h, DH * h + DH)
                    v.tensor_scalar(qz[rows, 2 * m:2 * m + 2, h, :], bank(4 + m, 2)[rows, :, :], qn_w[rows, 0:1], None,
                                    ALU.mult).then_inc(qT_ready, 1)

            def row_max(h):
                dve.wait_ge(score_mm, h + 1)
                for tt in range(TT):
                    ins = v.tensor_reduce(nmx[:, h, tt:tt + 1], ps[:, 4 + h % 2, P * tt:P + 2 * P * tt], AX_X, ALU.max,
                                          negate=True)
                ins.then_inc(rowmax_ready, 1)

            def prob_scale(h):
                dve.wait_ge(exp_ready, 2 * h + 2)
                link(v.reciprocal(rsum[:, h, :], rsum[:, h, :]))
                for tt in range(TT):
                    pr = prob[:, h % 2, P * tt:P + 2 * P * tt]
                    ins = v.tensor_scalar(pr, pr, rsum[:, h, tt:tt + 1], None, ALU.mult)
                ins.then_inc(prob_ready, 1)

            def pair_out(b):
                dve.wait_ge(pv_mm, 2 * b + 2)
                o = bank(7, 2)[:, b % 2, :]
                link(v.tensor_copy(ya_hi[:, b, :], o))
                v.tensor_tensor(ya_lo[:, b, :], o, ya_hi[:, b, :].bitcast(F32), ALU.subtract).then_inc(yaT_ready, 1)

            def conv_in(m):
                b, _ = bank_of(7, m)
                dve.wait_ge(proj_done, first_bank[7] + m + 1)
                cb, cu = bank_of(6, m)
                dve.wait_ge(evacuated[cb], cu + 1)
                v.tensor_tensor(conv_u[:, 2 * m:2 * m + 2, 2:T + 2], ycT[:, 2 * m:2 * m + 2, :], bank(b, 2),
                                ALU.mult).then_inc(evacuated[b], 1)

            def conv_taps(m):
                b, u = bank_of(7, m)
                dve.wait_ge(evacuated[b], u + 1)
                for k in (2 * m, 2 * m + 1):
                    link(v.tensor_scalar(ycT[:, k, :], conv_u[:, k, 0:T], cw_sb[:, 0, k:k + 1], cb_sb[:, k:k + 1],
                                         ALU.mult, ALU.add))
                    for j in (1, 2):
                        link(v.scalar_tensor_tensor(out=ycT[:, k, :], in0=conv_u[:, k, j:j + T],
                                                    scalar=cw_sb[:, j, k:k + 1], in1=ycT[:, k, :], op0=ALU.mult,
                                                    op1=ALU.add))

            def conv_out(m):
                b, _ = bank_of(8, m)
                dve.wait_ge(proj_done, first_bank[8] + m + 1)
                y = ycT[:, 2 * m:2 * m + 2, :]
                hi = yc_hi[:, 2 * m:2 * m + 2, :]
                v.tensor_tensor(y, y, bank(b, 2), ALU.mult).then_inc(evacuated[b], 1)
                dve.wait_ge(evacuated[b], bank_of(8, m)[1] + 1)
                link(v.tensor_copy(hi, y))
                v.tensor_tensor(yc_lo[:, 2 * m:2 * m + 2, :], y, hi.bitcast(F32), ALU.subtract).then_inc(ycT_ready, 1)

            row_max(0)
            for h in range(1, NH):
                prob_scale(h - 1)
                if h % 2:
                    low_pre(7 + h // 2)
                if h in (2, 3):
                    conv_in(h - 2)
                if h in (4, 5):
                    conv_out(h - 4)
                if h >= 4 and h % 2 == 0:
                    pair_out(h // 2 - 2)
                row_max(h)
                if h in (2, 3):
                    conv_taps(h - 2)
            prob_scale(NH - 1)
            pair_out(2)
            low_pre(11)
            pair_out(3)

            def merged_low(m):
                dve.wait_ge(merged_hi_ready, m + 1)
                v.tensor_tensor(merged_lo[:, 2 * m:2 * m + 2, :], mergedT[:, 2 * m:2 * m + 2, :],
                                merged_hi[:, 2 * m:2 * m + 2, :].bitcast(F32),
                                ALU.subtract).then_inc(merged_lo_ready, 1)

            for n in range(3):
                for m in range(4):
                    if n == 2 and m == 3:
                        merged_low(0)
                        low_pre(18, (0,))
                    elif m == 3:
                        low_pre(12 + 3 * n)
                    r = first_bank[11 + 3 * n] + m
                    sb, su = bank_of(9 + 3 * n + m // 2, m % 2)
                    dve.wait_ge(evacuated[sb], su + 1)
                    dve.wait_ge(proj_done, r + 1)
                    dst = flat(mergedT[:, 2 * m:2 * m + 2, :])
                    gate = flat(sig[n][:, 2 * m:2 * m + 2, :])
                    if n == 0:
                        v.tensor_tensor(dst, gate, bank(r % 4), ALU.mult).then_inc(evacuated[r % 4], 1)
                        dve.wait_ge(evacuated[r % 4], r // 4 + 1)
                        v.engine_nop().then_inc(branch_done, 1)
                    else:
                        v.tensor_tensor(scr[:, m % 2, :], gate, bank(r % 4), ALU.mult).then_inc(evacuated[r % 4], 1)
                        dve.wait_ge(evacuated[r % 4], r // 4 + 1)
                        v.tensor_tensor(dst, dst, scr[:, m % 2, :], ALU.add).then_inc(branch_done, 1)
                if n < 2:
                    low_pre(13 + 3 * n)
                    low_pre(14 + 3 * n)
            for m in range(1, 4):
                merged_low(m)
                low_pre(18, (m,))
            for half in range(2):
                for tt in range(TT):
                    if half == 0 and tt == 1:
                        low_pre(19)
                    r = first_bank[18 + half] + tt
                    dve.wait_ge(proj_done, r + 1)
                    xv = x_tok[:, tt, half * C:(half + 1) * C]
                    v.tensor_tensor(xv, xv, bank(r % 4), ALU.add).then_inc(x1_ready, 1)
                    if half == 1:
                        dve.wait_ge(x1_ready, 3 + tt)
                        norm_stats(x_tok, (flat(kT[:, :, :]),) * TT, ms2_ready, (tt,))
            for kp in range(2, 4):
                dve.wait_ge(h2_turned, kp + 1)
                for k in (2 * kp, 2 * kp + 1):
                    v.tensor_scalar(h2T[:, k, :], bank(4 + kp, 2)[:, k % 2, :], g_ffn[:, k:k + 1], None,
                                    ALU.mult).then_inc(hT_dve, 1)

            def low_part(p, i, q, cs):
                s = slot_of(q)
                for c in cs:
                    if c in POOL_LO:
                        continue
                    if p is None:
                        dve.wait_ge(hi_ready, CHUNKS * q + c + 1)
                    else:
                        dve.wait_ge(hi_ready, PER_PASS * CHUNKS * p + RING * CHUNKS * i + CHUNKS * q + c + 1)
                    v.tensor_tensor(ring_lo[s][:, chunk(c)], ring[s][:, chunk(c)], hi_buf(q, c).bitcast(F32),
                                    ALU.subtract).then_inc(lo_ready, 1)

            norm_apply(x_tok, xn, rms2_ready, h2_ready)
            low_part(None, 0, 0, (0,))

            dve.wait_ge(router_mm, 1)
            v.tensor_copy(lgT[:, :], ps[0:NG + NE, 0, 0:T]).then_inc(logits_ready, 1)
            dve.wait_ge(router_mm, 2)
            for tt in range(TT):
                lg = ps[:, 1, tt * (NG + NE):(tt + 1) * (NG + NE)]
                v.scalar_tensor_tensor(out=le[:, tt, :], in0=lg[:, NG:NG + NE], scalar=stat[:, 4 + tt:5 + tt],
                                       in1=b_r[:, NG:NG + NE], op0=ALU.mult, op1=ALU.add)
                ins = v.scalar_tensor_tensor(out=lgp[:, tt, 0:NG], in0=lg[:, 0:NG], scalar=stat[:, 4 + tt:5 + tt],
                                             in1=b_r[:, 0:NG], op0=ALU.mult, op1=ALU.add)
            link(ins)
            for tt in range(TT):
                link(v.max(mg8[:, tt, :], lgp[:, tt, :]))
                link(v.max_index(ig8[:, tt, :], mg8[:, tt, :], lgp[:, tt, :]))
            v.tensor_scalar(rt[:, :, 0:1], mg8[:, :, 0:1], -1.0, None, ALU.mult).then_inc(nmax_ready, 1)
            link(v.tensor_copy(rt[:, :, 4:5], ig8[:, :, 0:1]))
            for tt in range(TT):
                link(v.tensor_scalar(rt[:, tt, 12:16], iota_f[:, 0:NG], rt[:, tt, 4:5], None, ALU.is_equal))
                link(v.tensor_tensor(lsel[:, tt, :].rearrange("p (g e) -> p g e", e=EPG),
                                     le[:, tt, :].rearrange("p (g e) -> p g e", e=EPG),
                                     rt[:, tt, 12:16].unsqueeze(2).broadcast_to([P, NG, EPG]), ALU.mult))
                link(v.tensor_reduce(les[:, tt, :], lsel[:, tt, :].rearrange("p (g e) -> p e g", e=EPG), AX_X, ALU.add))
                link(v.max(me8[:, tt, :], les[:, tt, :]))
                link(v.max_index(ie8[:, tt, :], me8[:, tt, :], les[:, tt, :]))
            v.tensor_tensor(rt[:, :, 2:3], me8[:, :, 1:2], me8[:, :, 0:1], ALU.subtract).then_inc(e2in_ready, 1)
            link(v.tensor_copy(rt[:, :, 5:7], ie8[:, :, 0:2]))
            link(v.scalar_tensor_tensor(out=rt[:, :, 5:7], in0=rt[:, :, 4:5].broadcast_to([P, TT, 2]), scalar=float(EPG),
                                        in1=rt[:, :, 5:7], op0=ALU.mult, op1=ALU.add))
            every = iota_f[:, :].unsqueeze(1).broadcast_to([P, TT, NE])
            v.tensor_tensor(e1h[:, :, :], every, rt[:, :, 5:6].broadcast_to([P, TT, NE]), ALU.is_equal)
            link(v.tensor_tensor(e2h[:, :, :], every, rt[:, :, 6:7].broadcast_to([P, TT, NE]), ALU.is_equal))
            link(v.tensor_tensor(eall[:, :, :], e1h[:, :, :], e2h[:, :, :], ALU.add))
            v.tensor_copy(eall_bf[:, :, :], eall[:, :, :]).then_inc(assign_ready, 1)
            for tt in range(TT):
                link(v.tensor_tensor_scan(epre[:, tt, :], reset[:, 1:1 + NE], eall[:, tt, :], 0.0, ALU.mult, ALU.add))
            v.tensor_tensor(epre_bf[:, :, :], epre[:, :, :], eall[:, :, :], ALU.subtract).then_inc(assign_ready, 1)
            dve.wait_ge(pos_mm, 1)
            for tt in range(TT):
                for k, eh in enumerate((e1h, e2h)):
                    link(v.tensor_tensor_reduce(lsel[:, tt, :], eh[:, tt, :], ps[:, 1, tt * NE:(tt + 1) * NE], 1.0, 0.0,
                                                ALU.mult, ALU.add, slotf[:, tt, k:k + 1]))
            dve.wait_ge(iota_ready, 1)
            for tt in range(TT):
                link(v.tensor_scalar(perm[:, tt, :], iota_s[:, :], slotf[:, tt, 0:1], None, ALU.is_equal))
                v.scalar_tensor_tensor(out=perm[:, tt, :], in0=iota_s[:, :], scalar=slotf[:, tt, 1:2],
                                       in1=perm[:, tt, :].bitcast(F32), op0=ALU.is_equal, op1=ALU.add).then_inc(perm_ready, 1)
            link(v.tensor_reduce(cntr[:, 0:1], ps[0:1, 1, 3 * NE:4 * NE], AX_X, ALU.max))
            link(v.tensor_scalar(cntr[:, 1:2], cntr[:, 0:1], float(WIN), 1.0, ALU.is_gt, ALU.add))
            for r in range(2, MAXWIN):
                link(v.scalar_tensor_tensor(out=cntr[:, r:r + 1], in0=cntr[:, 0:1], scalar=float(WIN * r),
                                            in1=cntr[:, r - 1:r], op0=ALU.is_gt, op1=ALU.add))
            for p in range(MAXWIN):
                v.tensor_scalar(offf[:, p * NE:(p + 1) * NE], ps[0:1, 1, 2 * NE:3 * NE], float(WIN * p), float(SLOTS),
                                ALU.add, ALU.min).then_inc(v_chain, 1)
                steps[0] += 1
            dve.wait_ge(v_chain, steps[0])
            link(v.tensor_copy(off_tab[:, :], offf[:, :]))
            v.tensor_copy(npass[:, :], cntr[:, MAXWIN - 1:MAXWIN]).then_inc(route_ready, 1)
            for tt in range(TT):
                for k, eh in enumerate((e1h, e2h)):
                    link(v.tensor_tensor_reduce(lsel[:, tt, :], eh[:, tt, :], ps[:, 1, 2 * NE:3 * NE], 1.0, 0.0,
                                                ALU.mult, ALU.add, startf[:, TOPK * tt + k:TOPK * tt + k + 1]))
            link(v.tensor_tensor(placef[:, :], flat(slotf[:, :, :]), startf[:, :], ALU.subtract))
            n = TT * TOPK

            def sort_out(k):
                dve.wait_ge(gather_mm, k + 1)
                v.tensor_scalar(xs[:, k, 0:SLOTS], bank(2 + k % 4), g_ffn[:, k:k + 1], None, ALU.mult).then_inc(xs_dve, 1)

            dve.wait_ge(route_ready, 1)
            dve.sem_inc(gu_free, 4)
            dve.sem_inc(fin_ready, TT * TOPK)
            dve.sem_inc(y_ready, 1)
            sort_out(1)
            sort_out(3)
            for p in range(MAXWIN):
                link(v.tensor_scalar(rem[:, n * p:n * (p + 1)], placef[:, :], -float(WIN * p), None, ALU.add))
            link(v.tensor_scalar(rowf[:, :], rem[:, :], 0.0, float(WIN - 1), ALU.max, ALU.min))
            link(v.tensor_scalar(inside[:, :], rem[:, :], 0.0, None, ALU.is_ge))
            link(v.scalar_tensor_tensor(out=inside[:, :], in0=rem[:, :], scalar=float(WIN), in1=inside[:, :],
                                        op0=ALU.is_lt, op1=ALU.mult))
            sort_out(5)
            sort_out(7)
            dve.wait_ge(first_high, 1)
            v.tensor_tensor(xe[0][:, :, WIN:2 * WIN], xs[:, :, 0:WIN], xe[0][:, :, 0:WIN].bitcast(F32),
                            ALU.subtract).then_inc(first_window, 1)
            low_part(None, 0, 0, (1, 2))
            low_part(None, 0, 1, (0, 1))
            for p in range(MAXWIN):
                now = rowf[:, n * p:n * (p + 1)].rearrange("p (t k) -> p t k", k=TOPK)
                link(v.scalar_tensor_tensor(out=now, in0=rt[:, :, 5:7], scalar=float(WIN), in1=now, op0=ALU.mult,
                                            op1=ALU.add))
            v.tensor_copy(row_u[:, :], rowf[:, :]).then_inc(picks, 1)
            dve.wait_ge(gexp_ready, 2)
            dve.wait_ge(e2_ready, 1)
            link(v.tensor_scalar(rt[:, :, 7:8], rt[:, :, 3:4], 1.0, None, ALU.add))
            link(v.tensor_tensor(rt[:, :, 7:8], rt[:, :, 7:8], rt[:, :, 1:2], ALU.mult))
            link(v.reciprocal(wts[:, :, 0:1], rt[:, :, 7:8]))
            link(v.tensor_tensor(wts[:, :, 1:2], wts[:, :, 0:1], rt[:, :, 3:4], ALU.mult))
            for p in range(MAXWIN):
                v.tensor_tensor(w_pass[:, n * p:n * (p + 1)], inside[:, n * p:n * (p + 1)], flat(wts[:, :, :]),
                                ALU.mult).then_inc(picks, 1)
            dve.wait_ge(picks, 1 + MAXWIN)

            passes = dve.value_load(npass[0:1, 0:1], min_val=1, max_val=MAXWIN)
            def gu_fold(p, e, b):
                dve.wait_ge(gu_lo_out, 2 * NE * p + 2 * e + 1)
                v.tensor_tensor(g_sum[:, :], g_lo[:, :], ps[0:WIN, 2 * b, :], ALU.add).then_inc(gu_free, 1)
                dve.wait_ge(gu_lo_out, 2 * NE * p + 2 * e + 2)
                v.tensor_tensor(u_sum[:, :], u_lo[:, :], ps[0:WIN, 2 * b + 1, :], ALU.add).then_inc(gu_free, 1)

            def gated(p, e):
                dve.wait_ge(silu_ready, NE * p + e + 1)
                dve.wait_ge(gu_free, 2 * NE * p + 2 * e + 6)
                v.tensor_tensor(h_tok[:, :], g_act[:, :], u_sum[:, :], ALU.mult).then_inc(h_ready, 1)

            def he_low(p, e):
                dve.wait_ge(he_hi, NE * p + e + 1)
                v.tensor_tensor(he[:, :, WIN:2 * WIN], ps[:, 6, 0:KC * WIN].rearrange("p (k n) -> p k n", n=WIN),
                                he[:, :, 0:WIN].bitcast(F32), ALU.subtract).then_inc(he_lo, 1)

            def y_fold(p, e, half, b, at=4):
                dve.wait_ge(y_lo_out, NE * p + e + 1)
                dve.wait_ge(y_stored[b], (8 * NE) * p + 16 * half + 16)
                v.tensor_tensor(y_tok[:, b, :], y_lo[:, :], flat(ps[0:WIN, at:at + 2, :]), ALU.add).then_inc(y_ready, 1)

            def step(p, e, i, q, b, y_too):
                low_part(p, i, q, (0,))
                gu_fold(p, e - 1, 1 - b)
                low_part(p, i, q, (1,))
                gated(p, e - 1)
                low_part(p, i, q, (2,))
                low_part(p, i, q, (3,))
                low_part(p, i, q + 1, (0,))
                if y_too:
                    y_fold(p, e - 2, i, b)
                low_part(p, i, q + 1, (1, 2, 3))
                low_part(p, i, q + 2, (0,))
                he_low(p, e - 1)
                low_part(p, i, q + 2, (1, 2, 3))

            with dve.Fori(0, passes) as p:
                with dve.If(p > 0):
                    low_part(p, 0, 0, (0, 1, 2))
                    low_part(p, 0, 1, (0, 1))
                low_part(p, 0, 1, (2,))
                v.tensor_copy(row_now[:, :], row_u[:, bass.ds(p * n, n)]).then_inc(picked, 1)
                v.tensor_copy(w_now[:, :], w_pass[:, bass.ds(p * n, n)]).then_inc(picked, 1)
                step(p, 1, 0, 2, 1, False)
                with dve.Fori(0, NE // 2 - 1) as i:
                    for s in range(2):
                        step(p, 2 * i + (2 + s), i, 5 + 3 * s, s, True)
                gu_fold(p, NE - 1, 1)
                gated(p, NE - 1)
                low_part(p, 0, PER_PASS - 1, (0, 1, 2))
                he_low(p, NE - 1)
                y_fold(p, NE - 2, NE // 2 - 1, 0)
                y_fold(p, NE - 1, NE // 2 - 1, 1, 0)
                dve.wait_ge(picked, 2 * p + 2)
                for j in range(TT * TOPK):
                    tt, k = j // TOPK, j % TOPK
                    dve.wait_ge(back_in[j], 16 * p + 16)
                    if k:
                        dve.wait_ge(fin_ready, (TT * TOPK) * p + (TT * TOPK + j))
                    v.scalar_tensor_tensor(out=x_tok[:, tt, :], in0=y_back[tt][:, k, :], scalar=w_now[:, j:j + 1],
                                           in1=x_tok[:, tt, :], op0=ALU.mult, op1=ALU.add).then_inc(fin_ready, 1)


_INS = ['x', 'rel_bias_table', 'norm_mix', 'w_in', 'conv_w', 'conv_b', 'q_norm', 'k_norm', 'w_gla_alpha',
        'b_gla_alpha', 'gla_out_norm', 'w_merge_gate', 'w_branch', 'w_out', 'norm_ffn', 'w_router_group',
        'b_router_group', 'w_router_expert', 'b_router_expert', 'w_expert_gate', 'w_expert_up', 'w_expert_down']


def kernel(**inputs):
    import concourse.bacc as _bacc
    from concourse.bass_utils import run_bass_kernel_spmd as _run

    nc = _bacc.Bacc("TRN2", target_bir_lowering=False, num_devices=1)
    arrays, args = {}, []
    for name in _INS:
        a = np.ascontiguousarray(inputs[name])
        arrays[f"in_{name}"] = a
        args.append(nc.dram_tensor(f"in_{name}", a.shape, mybir.dt.from_np(a.dtype), kind="ExternalInput").ap())
    out = nc.dram_tensor("out_x", (1, T, D), F32, kind="ExternalOutput").ap()
    hybrid_block(nc, *args, out)
    r = _run(nc, [arrays], core_ids=[0])
    return r.results[0]["out_x"]
```
